# Optimizing a Trainium2 kernel written in Bass

```python
import math
import jax, jax.numpy as jnp
from jax import lax
import numpy as np

D_MODEL = 1024
BATCH = 1
SEQ = 512
DEPTH = 1

GDN_HEADS = 4
GDN_HEAD_DIM = 128
GDN_WIDTH = GDN_HEADS * GDN_HEAD_DIM
GDN_CONV = 4
GDN_CHUNK = 64
DIL_HEADS = 8
DIL_HEAD_DIM = 64
DIL_WIDTH = DIL_HEADS * DIL_HEAD_DIM
DIL_PATTERNS = ((128, 1), (512, 4), (2048, 16))
BAND_BLOCK = 128
MIX_WIDTH = GDN_WIDTH + DIL_WIDTH
IN_COLS = 3 * GDN_WIDTH + GDN_WIDTH + 2 * GDN_HEADS + 3 * DIL_WIDTH
D_FF = 2816
FFN_CONV = 3
EPS = 1e-6


def rmsnorm(x, w):
    xf = x.astype(jnp.float32)
    y = xf * lax.rsqrt(jnp.mean(xf * xf, axis=-1, keepdims=True) + EPS)
    return (y * w.astype(jnp.float32)).astype(x.dtype)

def l2norm(x):
    return x * lax.rsqrt(jnp.sum(x * x, axis=-1, keepdims=True) + EPS)

def causal_dwconv(x, w):
    K = w.shape[0]
    S = x.shape[1]
    xp = jnp.pad(x, ((0, 0), (K - 1, 0), (0, 0)))
    out = xp[:, 0:S, :] * w[0]
    for i in range(1, K):
        out = out + xp[:, i:i + S, :] * w[i]
    return out

def gated_delta_rule(q, k, v, g, beta):
    B, S, H, Dk = q.shape
    Dv = v.shape[-1]
    C = GDN_CHUNK
    nc = S // C

    def chunk_vec(t):
        return t.reshape(B, nc, C, H, t.shape[-1]).transpose(1, 0, 3, 2, 4)

    def chunk_sc(t):
        return t.reshape(B, nc, C, H).transpose(1, 0, 3, 2)

    qc, kc, vc = chunk_vec(q), chunk_vec(k), chunk_vec(v)
    bc = chunk_sc(beta)
    gc = jnp.cumsum(chunk_sc(g), axis=-1)
    idx = jnp.arange(C)
    incl = idx[:, None] >= idx[None, :]
    strict = idx[:, None] > idx[None, :]
    diff = gc[..., :, None] - gc[..., None, :]
    dec_incl = jnp.where(incl, jnp.exp(jnp.where(incl, diff, 0.0)), 0.0)
    dec_strict = jnp.where(strict, dec_incl, 0.0)
    kk = jnp.einsum('nbhtd,nbhjd->nbhtj', kc, kc)
    lmat = dec_strict * kk * bc[..., None, :]
    gam = jnp.exp(gc)[..., None]
    rhs = jnp.concatenate([vc, gam * kc], axis=-1)
    sol = lax.linalg.triangular_solve(lmat, rhs, left_side=True, lower=True, unit_diagonal=True)
    u_v, w_k = sol[..., :Dv], sol[..., Dv:]
    attn = dec_incl * jnp.einsum('nbhtd,nbhjd->nbhtj', qc, kc) * bc[..., None, :]
    q_dec = gam * qc
    k_end = kc * (jnp.exp(gc[..., -1:] - gc) * bc)[..., None]
    g_end = jnp.exp(gc[..., -1])

    def step(state, xs):
        uv, wk, qd, at, ke, ge = xs
        u = uv - jnp.einsum('bhck,bhkv->bhcv', wk, state)
        o = jnp.einsum('bhck,bhkv->bhcv', qd, state) + jnp.einsum('bhcj,bhjv->bhcv', at, u)
        state = ge[..., None, None] * state + jnp.einsum('bhck,bhcv->bhkv', ke, u)
        return state, o

    s0 = jnp.zeros((B, H, Dk, Dv), jnp.float32)
    _, o = lax.scan(step, s0, (u_v, w_k, q_dec, attn, k_end, g_end))
    return o.transpose(1, 0, 3, 2, 4).reshape(B, S, H, Dv)

def band_attention(q, k, v, n_back):
    L, Dh = q.shape[-2], q.shape[-1]
    nb = -(-L // BAND_BLOCK)
    pad = nb * BAND_BLOCK - L
    padcfg = [(0, 0)] * (q.ndim - 2) + [(0, pad), (0, 0)]
    lead = q.shape[:-2]

    def blocks(t):
        return jnp.pad(t, padcfg).reshape(*lead, nb, BAND_BLOCK, Dh)

    qb, kb, vb = blocks(q), blocks(k), blocks(v)

    def with_prev(t):
        prev = jnp.concatenate([jnp.zeros_like(t[..., :1, :, :]), t[..., :-1, :, :]], axis=-3)
        return jnp.concatenate([prev, t], axis=-2)

    kk, vv = with_prev(kb), with_prev(vb)
    s = jnp.einsum('...nqd,...nkd->...nqk', qb, kk)
    blk = jnp.arange(nb)[:, None, None] * BAND_BLOCK
    qpos = blk + jnp.arange(BAND_BLOCK)[None, :, None]
    kpos = blk - BAND_BLOCK + jnp.arange(2 * BAND_BLOCK)[None, None, :]
    dist = qpos - kpos
    valid = (dist >= 0) & (dist <= n_back) & (kpos >= 0)
    s = jnp.where(valid, s, -jnp.inf)
    m = jnp.max(s, axis=-1)
    p = jnp.exp(s - m[..., None])
    den = jnp.sum(p, axis=-1)
    num = jnp.einsum('...nqk,...nkd->...nqd', p, vv)
    num = num.reshape(*lead, nb * BAND_BLOCK, Dh)[..., :L, :]
    den = den.reshape(*lead, nb * BAND_BLOCK)[..., :L]
    m = m.reshape(*lead, nb * BAND_BLOCK)[..., :L]
    return num, den, m

def dilated_attention(q, k, v):
    B, S, H, Dh = q.shape
    qf = q.astype(jnp.float32).transpose(0, 2, 1, 3) * (Dh ** -0.5)
    kf = k.astype(jnp.float32).transpose(0, 2, 1, 3)
    vf = v.astype(jnp.float32).transpose(0, 2, 1, 3)
    nums, dens, ms = [], [], []
    for window, dil in DIL_PATTERNS:
        L = S // dil

        def stride(t):
            return t.reshape(B, H, L, dil, Dh).transpose(0, 1, 3, 2, 4)

        num, den, m = band_attention(stride(qf), stride(kf), stride(vf), window // dil)
        nums.append(num.transpose(0, 1, 3, 2, 4).reshape(B, H, S, Dh))
        dens.append(den.transpose(0, 1, 3, 2).reshape(B, H, S))
        ms.append(m.transpose(0, 1, 3, 2).reshape(B, H, S))
    m_all = jnp.maximum(jnp.maximum(ms[0], ms[1]), ms[2])
    wts = [jnp.exp(mi - m_all) for mi in ms]
    num_tot = wts[0][..., None] * nums[0] + wts[1][..., None] * nums[1] + wts[2][..., None] * nums[2]
    den_tot = wts[0] * dens[0] + wts[1] * dens[1] + wts[2] * dens[2]
    out = num_tot / den_tot[..., None]
    return out.transpose(0, 2, 1, 3).reshape(B, S, H * Dh)

def hybrid_layer(x, norm1_w, w_in, conv_qkv_w, a_log, dt_bias, gdn_norm_w, w_out,
                 norm2_w, w_up, ffn_conv_w, w_down):
    B, S, _ = x.shape
    h = rmsnorm(x, norm1_w)
    proj = h @ w_in
    o1 = 3 * GDN_WIDTH
    o2 = o1 + GDN_WIDTH
    o3 = o2 + GDN_HEADS
    o4 = o3 + GDN_HEADS
    qkv_a, z_a, b_a, a_a, qkv_b = (proj[..., :o1], proj[..., o1:o2], proj[..., o2:o3],
                                   proj[..., o3:o4], proj[..., o4:])
    qkv_a = jax.nn.silu(causal_dwconv(qkv_a, conv_qkv_w)).astype(jnp.float32)
    qa = qkv_a[..., :GDN_WIDTH].reshape(B, S, GDN_HEADS, GDN_HEAD_DIM)
    ka = qkv_a[..., GDN_WIDTH:2 * GDN_WIDTH].reshape(B, S, GDN_HEADS, GDN_HEAD_DIM)
    va = qkv_a[..., 2 * GDN_WIDTH:].reshape(B, S, GDN_HEADS, GDN_HEAD_DIM)
    qa = l2norm(qa) * (GDN_HEAD_DIM ** -0.5)
    ka = l2norm(ka)
    beta = jax.nn.sigmoid(b_a.astype(jnp.float32))
    g = -jnp.exp(a_log.astype(jnp.float32)) * jax.nn.softplus(
        a_a.astype(jnp.float32) + dt_bias.astype(jnp.float32))
    o_a = gated_delta_rule(qa, ka, va, g, beta)
    z = z_a.astype(jnp.float32).reshape(B, S, GDN_HEADS, GDN_HEAD_DIM)
    o_a = (rmsnorm(o_a, gdn_norm_w) * jax.nn.silu(z)).reshape(B, S, GDN_WIDTH).astype(x.dtype)
    qb = qkv_b[..., :DIL_WIDTH].reshape(B, S, DIL_HEADS, DIL_HEAD_DIM)
    kb = qkv_b[..., DIL_WIDTH:2 * DIL_WIDTH].reshape(B, S, DIL_HEADS, DIL_HEAD_DIM)
    vb = qkv_b[..., 2 * DIL_WIDTH:].reshape(B, S, DIL_HEADS, DIL_HEAD_DIM)
    o_b = dilated_attention(qb, kb, vb).astype(x.dtype)
    x = x + jnp.concatenate([o_a, o_b], axis=-1) @ w_out
    h = rmsnorm(x, norm2_w)
    u = causal_dwconv(h @ w_up, ffn_conv_w)
    gate, up = u[..., :D_FF], u[..., D_FF:]
    x = x + (jax.nn.silu(gate) * up) @ w_down
    return x

def first_inputs(seed: int = 0) -> dict:
    key = jax.random.key(seed)
    ks = jax.random.split(key, 14)
    f32 = jnp.float32
    x = jax.random.normal(ks[0], (BATCH, SEQ, D_MODEL), f32)
    norm1_w = 1.0 + 0.02 * jax.random.normal(ks[1], (DEPTH, D_MODEL), f32)
    w_in = jax.random.normal(ks[2], (DEPTH, D_MODEL, IN_COLS), f32) * D_MODEL ** -0.5
    conv_qkv_w = jax.random.normal(ks[3], (DEPTH, GDN_CONV, 3 * GDN_WIDTH), f32) * GDN_CONV ** -0.5
    a_log = jnp.log(jax.random.uniform(ks[4], (DEPTH, GDN_HEADS), f32, 1.0, 16.0))
    dt = jnp.exp(jax.random.uniform(ks[5], (DEPTH, GDN_HEADS), f32, math.log(1e-3), math.log(1e-1)))
    dt_bias = dt + jnp.log(-jnp.expm1(-dt))
    gdn_norm_w = 1.0 + 0.02 * jax.random.normal(ks[6], (DEPTH, GDN_HEAD_DIM), f32)
    w_out = jax.random.normal(ks[7], (DEPTH, MIX_WIDTH, D_MODEL), f32) * MIX_WIDTH ** -0.5
    norm2_w = 1.0 + 0.02 * jax.random.normal(ks[8], (DEPTH, D_MODEL), f32)
    w_up = jax.random.normal(ks[9], (DEPTH, D_MODEL, 2 * D_FF), f32) * D_MODEL ** -0.5
    ffn_conv_w = jax.random.normal(ks[10], (DEPTH, FFN_CONV, 2 * D_FF), f32) * FFN_CONV ** -0.5
    w_down = jax.random.normal(ks[11], (DEPTH, D_FF, D_MODEL), f32) * D_FF ** -0.5
    final_norm_w = 1.0 + 0.02 * jax.random.normal(ks[12], (D_MODEL,), f32)
    return {"x": x, "norm1_w": norm1_w, "w_in": w_in, "conv_qkv_w": conv_qkv_w,
            "a_log": a_log, "dt_bias": dt_bias, "gdn_norm_w": gdn_norm_w, "w_out": w_out,
            "norm2_w": norm2_w, "w_up": w_up, "ffn_conv_w": ffn_conv_w, "w_down": w_down,
            "final_norm_w": final_norm_w}

def first_block(x, norm1_w, w_in, conv_qkv_w, a_log, dt_bias, gdn_norm_w, w_out,
              norm2_w, w_up, ffn_conv_w, w_down, final_norm_w):
    for l in range(DEPTH):
        x = hybrid_layer(x, norm1_w[l], w_in[l], conv_qkv_w[l], a_log[l], dt_bias[l],
                         gdn_norm_w[l], w_out[l], norm2_w[l], w_up[l], ffn_conv_w[l], w_down[l])
    return rmsnorm(x, final_norm_w)


DEPTH_2 = 2

GRID_W = 64
CTX_LEN = 256
EXPAND = 2
D_INNER = EXPAND * D_MODEL
HG_HEAD_DIM = 128
HG_HEADS = D_INNER // HG_HEAD_DIM
HG_STREAMS = 5
FT_GROUPS = 8
FT_GROUP_DIM = D_INNER // FT_GROUPS
CHUNK = 64
N_MIXERS = 2
N_HGRN = (DEPTH_2 + 1) // 2
N_FOURIER = DEPTH_2 // 2


def rms_norm(x, g):
    xf = x.astype(jnp.float32)
    var = jnp.mean(xf * xf, axis=-1, keepdims=True)
    return (xf * lax.rsqrt(var + EPS)).astype(x.dtype) * g

def adaln(cvec, w, b):
    m = jax.nn.silu(cvec) @ w + b
    return jnp.split(m, 3, axis=-1)

def chunk_scan(q, k, v, g, s0):
    B, H, N, Dk = q.shape
    Dv = v.shape[-1]
    nc = N // CHUNK

    def to_chunks(a):
        a = a.astype(jnp.float32).reshape(B, H, nc, CHUNK, a.shape[-1])
        return jnp.moveaxis(a, 2, 0)

    causal = jnp.tril(jnp.ones((CHUNK, CHUNK), dtype=bool))[:, :, None]

    def step(S, inp):
        qc, kc, vc, gc = inp
        b = jnp.cumsum(gc, axis=-2)
        diff = b[..., :, None, :] - b[..., None, :, :]
        decay = jnp.exp(jnp.where(causal, diff, -jnp.inf))
        scores = jnp.einsum('bhtc,bhtsc,bhsc->bhts', qc, decay, kc)
        o = (jnp.einsum('bhts,bhsv->bhtv', scores, vc)
             + jnp.einsum('bhtc,bhcv->bhtv', qc * jnp.exp(b), S))
        b_last = b[..., -1:, :]
        S_new = (jnp.exp(b_last)[..., 0, :, None] * S
                 + jnp.einsum('bhsc,bhsv->bhcv', kc * jnp.exp(b_last - b), vc))
        return S_new, o

    S_fin, o = lax.scan(step, s0, (to_chunks(q), to_chunks(k), to_chunks(v), to_chunks(g)))
    o = jnp.moveaxis(o, 0, 2).reshape(B, H, N, Dv)
    return o, S_fin

def hgrn_lower_bound(logits, j):
    p = jax.nn.softmax(logits.astype(jnp.float32), axis=0)
    return jnp.cumsum(p, axis=0)[j]

def hgrn_project(h, w_in, lb):
    B, N, _ = h.shape
    p = (h @ w_in).reshape(B, N, HG_STREAMS, HG_HEADS, HG_HEAD_DIM)
    p = jnp.transpose(p, (2, 0, 3, 1, 4))
    q = jax.nn.silu(p[0])
    lbh = lb.reshape(2, 1, HG_HEADS, 1, HG_HEAD_DIM)
    f = lbh + (1.0 - lbh) * jax.nn.sigmoid(p[1:3].astype(jnp.float32))
    return q, 1.0 - f, jnp.log(f), p[3], p[4]

def hgrn_readout(o, z, norm_g, w_out):
    y = rms_norm(o, norm_g).astype(z.dtype) * jax.nn.silu(z)
    B, H, N, d = y.shape
    return jnp.transpose(y, (0, 2, 1, 3)).reshape(B, N, H * d) @ w_out

def hgrn_mixer(h_ctx, h_lat, w_in, lb, norm_g, w_out, ctx_out):
    qc, kc, gc, vc, zc = hgrn_project(h_ctx, w_in, lb)
    ql, kl, gl, vl, zl = hgrn_project(h_lat, w_in, lb)
    B = h_lat.shape[0]
    s0 = jnp.zeros((B, HG_HEADS, HG_HEAD_DIM, HG_HEAD_DIM), jnp.float32)
    flip = lambda a: jnp.flip(a, axis=2)
    o_cf, s_cf = chunk_scan(qc, kc[0], vc, gc[0], s0)
    o_cb, s_cb = chunk_scan(flip(qc), flip(kc[1]), flip(vc), flip(gc[1]), s0)
    o_lf, _ = chunk_scan(ql, kl[0], vl, gl[0], s_cf)
    o_lb, _ = chunk_scan(flip(ql), flip(kl[1]), flip(vl), flip(gl[1]), s_cb)
    y_lat = hgrn_readout(o_lf + flip(o_lb), zl, norm_g, w_out)
    y_ctx = hgrn_readout(o_cf + flip(o_cb), zc, norm_g, w_out) if ctx_out else None
    return y_lat, y_ctx

def fourier_mixer(h, w_in, w_out):
    B, N, _ = h.shape
    u, z = jnp.split(h @ w_in, 2, axis=-1)
    ug = u.astype(jnp.float32).reshape(B, N, FT_GROUPS, FT_GROUP_DIM)
    y = jnp.fft.fft2(ug, axes=(1, 3), norm='ortho').real.reshape(B, N, D_INNER)
    return (y.astype(h.dtype) * jax.nn.silu(z)) @ w_out

def second_inputs(seed: int = 0) -> dict:
    key = jax.random.key(seed)
    ks = jax.random.split(key, 14)
    D, E = D_MODEL, D_INNER
    nrm = jax.random.normal
    return {
        'x': nrm(ks[0], (BATCH, SEQ, D), jnp.float32),
        'c': nrm(ks[1], (BATCH, D), jnp.float32),
        'ctx': nrm(ks[2], (BATCH, CTX_LEN, D), jnp.float32),
        'c_ctx': nrm(ks[3], (D,), jnp.float32),
        'ada_w': nrm(ks[4], (DEPTH_2, D, 3 * D), jnp.float32) * (0.5 * D ** -0.5),
        'ada_b': nrm(ks[5], (DEPTH_2, 3 * D), jnp.float32) * 0.01,
        'norm_g': 1.0 + 0.05 * nrm(ks[6], (DEPTH_2, D), jnp.float32),
        'hg_w_in': nrm(ks[7], (N_HGRN, D, HG_STREAMS * E), jnp.float32) * D ** -0.5,
        'hg_lb_logits': 0.5 * nrm(ks[8], (N_HGRN + 1, 2, E), jnp.float32),
        'hg_norm_g': 1.0 + 0.05 * nrm(ks[9], (N_HGRN, HG_HEAD_DIM), jnp.float32),
        'hg_w_out': nrm(ks[10], (N_HGRN, E, D), jnp.float32) * E ** -0.5,
        'ft_w_in': nrm(ks[11], (N_FOURIER, D, 2 * E), jnp.float32) * D ** -0.5,
        'ft_w_out': nrm(ks[12], (N_FOURIER, E, D), jnp.float32) * E ** -0.5,
        'final_g': 1.0 + 0.05 * nrm(ks[13], (D,), jnp.float32),
    }

def second_block(x, c, ctx, c_ctx, ada_w, ada_b, norm_g, hg_w_in, hg_lb_logits, hg_norm_g,
              hg_w_out, ft_w_in, ft_w_out, final_g):
    x_lat, x_ctx = x, ctx
    for i in range(DEPTH_2):
        ctx_out = i < DEPTH_2 - 1
        j = i // N_MIXERS
        sh_l, sc_l, gt_l = adaln(c, ada_w[i], ada_b[i])
        h_lat = rms_norm(x_lat, norm_g[i]) * (1.0 + sc_l[:, None]) + sh_l[:, None]
        if i % N_MIXERS == 0:
            sh_c, sc_c, gt_c = adaln(c_ctx, ada_w[i], ada_b[i])
            h_ctx = rms_norm(x_ctx, norm_g[i]) * (1.0 + sc_c) + sh_c
            lb = hgrn_lower_bound(hg_lb_logits, j)
            y_lat, y_ctx = hgrn_mixer(h_ctx, h_lat, hg_w_in[j], lb, hg_norm_g[j], hg_w_out[j], ctx_out)
        else:
            y_lat = fourier_mixer(h_lat, ft_w_in[j], ft_w_out[j])
            if ctx_out:
                sh_c, sc_c, gt_c = adaln(c_ctx, ada_w[i], ada_b[i])
                h_ctx = rms_norm(x_ctx, norm_g[i]) * (1.0 + sc_c) + sh_c
                y_ctx = fourier_mixer(h_ctx, ft_w_in[j], ft_w_out[j])
        x_lat = x_lat + gt_l[:, None] * y_lat
        if ctx_out:
            x_ctx = x_ctx + gt_c * y_ctx
    return rms_norm(x_lat, final_g)


def setup_inputs(seed=0):
    out = dict(first_inputs(seed))
    for name, value in second_inputs(seed + 1).items():
        if name != "x":
            out[name + "_2"] = value
    return out


def reference(
    x, norm1_w, w_in, conv_qkv_w, a_log, dt_bias, gdn_norm_w, w_out, norm2_w, w_up, ffn_conv_w,
    w_down, final_norm_w, c_2, ctx_2, c_ctx_2, ada_w_2, ada_b_2, norm_g_2, hg_w_in_2,
    hg_lb_logits_2, hg_norm_g_2, hg_w_out_2, ft_w_in_2, ft_w_out_2, final_g_2,
):
    x = first_block(
        x, norm1_w, w_in, conv_qkv_w, a_log, dt_bias, gdn_norm_w, w_out, norm2_w, w_up,
        ffn_conv_w, w_down, final_norm_w,
    )
    return second_block(
        x, c_2, ctx_2, c_ctx_2, ada_w_2, ada_b_2, norm_g_2, hg_w_in_2, hg_lb_logits_2,
        hg_norm_g_2, hg_w_out_2, ft_w_in_2, ft_w_out_2, final_g_2,
    )


_drawn_inputs = setup_inputs


def setup_inputs(seed=0):
    import zlib

    import numpy as np

    out = dict(_drawn_inputs(seed))
    spreads = {}
    factors = {'norm1_w': 3.5,
     'gdn_norm_w': 6.387,
     'norm2_w': 4.152,
     'final_norm_w': 2.822,
     'ctx_2': 8.0,
     'c_ctx_2': 8.0,
     'ada_b_2': 5.586,
     'norm_g_2': 3.419,
     'hg_lb_logits_2': 6.839,
     'hg_norm_g_2': 6.336}
    for name, (base, spread) in spreads.items():
        noise = np.random.default_rng([zlib.crc32(name.encode()), seed]).standard_normal(out[name].shape)
        drawn = base * np.exp(spread * noise) if base else spread * noise
        out[name] = __import__('jax').numpy.asarray(drawn.astype(out[name].dtype))
    for name, factor in factors.items():
        out[name] = (out[name] * factor).astype(out[name].dtype)
    return out
```

```python
from contextlib import ExitStack

import numpy as np

import concourse.bass as bass
from concourse import mybir

F32 = mybir.dt.float32
F32R = mybir.dt.float32r
U32 = mybir.dt.uint32
ALU = mybir.AluOpType
ACT = mybir.ActivationFunctionType
AX = mybir.AxisListType

P = 128
T = 512
TT = T // P
D = 1024
KT = D // P
GH_N, DH_N = 4, 8
GW, DW = 512, 512
O_Z, O_BA, O_B = 3 * GW, 4 * GW, 4 * GW + 2 * GH_N
FF = 2816
FT = FF // P
ROUND = [range(0, 8), range(8, 16), range(16, 22)]
HG = 16
E_IN = 2048
CT = 256
EPS = 1e-6
GROUPS, GDIM = 8, 256
NST, NSPLIT, NLIN = 4, 3, 3
LEVELS = [1, 2, 4, 8, 16, 32, 64, 128, 256]

ROWS = {}
_at = 0
for _name, _n in [("norm1", 8), ("norm2", 8), ("final1", 8), ("conv", 48), ("gdn_norm", 1),
                  ("hg_norm", 1), ("norm_g", 16), ("final_g", 8), ("lb0", 32), ("lb1", 32),
                  ("ada_b", 48), ("c", 8), ("c_ctx", 8), ("ffn_conv", 132)]:
    ROWS[_name] = (_at, _n)
    _at += _n
NROWS = _at
NV = 3 * P
assert NROWS <= NV


def host_constants():
    i = np.arange(P)
    ident = np.eye(P)
    upper = (i[:, None] <= i[None, :]) * 1.0
    lev = []
    for h in [1, 2, 4, 8, 16, 32, 64]:
        same = (i[:, None] // (2 * h)) == (i[None, :] // (2 * h))
        first, second = (i // h) % 2 == 0, (i // h) % 2 == 1
        lev.append((same & first[:, None] & second[None, :]) * 1.0)
    cnt = []
    for dist in [3, 2, 1, 0]:
        d = i[:, None] - i[None, :] + dist * P
        cnt.append(((d >= 0) & (d <= 128)) * 1.0 + ((d >= 0) & (d % 4 == 0)) + ((d >= 0) & (d % 16 == 0)))
    cnt = np.concatenate(cnt, 1)
    neg = np.where(cnt > 0, 0.0, -1e30)
    cf = np.concatenate([ident, upper] + lev + [cnt, neg], 1).astype(np.float32)
    m = [np.eye(P)]
    for h in [1, 2, 4, 8, 16, 32, 64]:
        same = (i[:, None] // (2 * h)) == (i[None, :] // (2 * h))
        m.append(same & ((i[:, None] // h) % 2 != (i[None, :] // h) % 2))
    hm = np.stack(m, 1).astype(np.uint32)
    c = np.arange(GDIM)
    g = np.arange(GDIM // 2 + 1)
    dch = np.concatenate([np.cos(2 * np.pi * np.outer(c, g) / GDIM),
                          np.sin(2 * np.pi * np.outer(c, g[1:-1]) / GDIM)], 1).astype(np.float32)
    t = np.arange(T)
    u = np.arange(T // 2 + 1)
    s = 1.0 / np.sqrt(T * GDIM)
    dtok = (s * np.concatenate([np.cos(2 * np.pi * (np.outer(t, u) % T) / T),
                                np.sin(2 * np.pi * (np.outer(t, u[1:-1]) % T) / T)], 1)).astype(np.float32)
    onecol = np.zeros((P, 31), np.float32)
    onecol[:, 15] = 1.0
    return {"cf": cf, "hm": hm, "dch": dch, "dtok": dtok, "onecol": onecol}


def make_units():
    units, tiles = [], []

    def add(w, rows, col, x, start=True, stop=True, ctx=False):
        if start:
            tiles.append([])
        tiles[-1].append(sum(u["lin"] for u in units))
        units.append(dict(w=w, rows=rows, col=col, x=x, start=start, stop=stop, lin=True,
                          tile=len(tiles) - 1, ctx=ctx))

    raws = [dict(w="ada_w", layer=l, rows=(0, 8), col=j * P, lin=False, raw=l * 24 + j)
            for l in range(2) for j in range(24)]

    for t in range(28):
        add("w_in", (0, 8), t * P if t < 16 else O_B + (t - 16) * P, "h")
    for n in range(KT):
        add("w_out", (0, 8), n * P, "g")
    for r in ROUND:
        for j in r:
            for half in range(2):
                lone = 2 * j + half < 3
                for _ in range(0 if lone else 2 if half and j in (2, 4, 6, 9, 11, 13, 18) else 1):
                    units.append(raws.pop(0))
                add("w_up", (0, 8), half * FF + j * P, "h")
        for n in range(KT):
            add("w_down", (r[0], len(r)), n * P, "g")
    assert not raws
    for hd in range(HG):
        for s in range(5):
            add("hg_w_in", (0, 8), s * E_IN + hd * P, "h", ctx=s in (1, 2, 3))
    for n in range(KT):
        add("hg_w_out", (0, 8), n * P, "h", stop=False)
        add("hg_w_out", (8, 8), n * P, "g", start=False)
    for half in range(2):
        for gi in range(4 * half, 4 * half + 4):
            for part in range(2):
                for c in range(2):
                    add("ft_w_in", (0, 8), part * E_IN + (2 * gi + c) * P, "h")
        for n in range(KT):
            add("ft_w_out", (8 * half, 8), n * P, "g")
    lin = 0
    seen = [0] * NST
    for n, u in enumerate(units):
        u["slot"], u["load"] = n % NST, n // NST
        if u["lin"]:
            u["lin_no"] = lin
            lin += 1
    return units, tiles


def view(ap, dims, off=0):
    return bass.AP(tensor=ap.tensor, offset=ap.offset + off, ap=[list(ap.ap[0])] + [list(x) for x in dims])


def build(nc, d, out, upto=99, debug=None):
    units, tiles = make_units()
    lin_units = [u for u in units if u["lin"]]
    n_lin = len(lin_units)
    ctx = ExitStack()
    with ctx:
        sems = {}

        def S(name):
            if name not in sems:
                sems[name] = ctx.enter_context(nc.semaphore("s_" + name))
            return sems[name]

        base = 16640
        assert nc.sbuf_base <= base

        def at(name, kib, shape, dt=F32):
            size = int(np.prod(shape[1:])) * 4
            assert base + kib * 1024 + size <= 229360, name
            return nc.alloc_sbuf_tensor_at(name, shape, dt, offset=int(base + kib * 1024))

        xT = at("xT", 0, [P, KT, T])
        stage = at("stage", 16, [P, NST, KT, P])
        wh = at("wh", 32, [P, NSPLIT, KT, P], F32R)
        wl = at("wl", 44, [P, NSPLIT, KT, P], F32R)
        hh = at("hh", 56, [P, KT, T], F32R)
        hl = at("hl", 72, [P, KT, T], F32R)
        gh = at("gh", 88, [P, KT, T], F32R)
        gl = at("gl", 104, [P, KT, T], F32R)
        V = at("V", 120, [P, NV])
        ident = at("ident", 121.5, [P, P])
        ones = at("ones", 122, [P, P])
        sq = at("sq", 122.5, [P, 2, T])
        hf = at("hf", 126.5, [P, 2, T])
        rs = at("rs", 130.5, [P, T])
        small = at("small", 132.5, [P, 256])
        A0 = 133.5
        zT = at("zT", A0, [P, 4, T])
        qkv = at("qkv", A0 + 8, [P, 12, T])
        xtok = at("xtok", A0 + 8, [P, TT, D])
        rowsT = at("rowsT", A0 + 24, [P, 3, P])
        bqkv = at("bqkv", A0 + 32, [P, 12, T])
        raw = at("raw", A0 + 56, [P, 2, T + 8])
        cacc = at("cacc", A0 + 60.25, [P, T])
        cst = at("cst", A0 + 62.25, [P, 2 * P])
        gmask = at("gmask", A0 + 63.25, [P, 7, P])
        dcnt = at("dcnt", A0 + 66.75, [P, T])
        dneg = at("dneg", A0 + 68.75, [P, T])
        w8 = at("w8", A0 + 70.75, [P, KT, 8])
        gs = at("gs", A0 + 71, [P, 320])
        vb = at("vb", 56, [P, TT, T])
        pT = at("pT", 64, [P, 2, TT, T])
        sm = at("sm", 80, [P, 2, T])
        pr = at("pr", 84, [P, 2, T])
        names = ["ug", "ee", "eg", "dt_", "at_", "lt", "m0", "m1", "xx", "xt", "tt", "vtok", "gk", "kend",
                 "uv", "wkT"]
        G = {n: at("g_" + n, 56 + 2 * i, [P, 4, P]) for i, n in enumerate(names)}
        for i, n in enumerate(["qdec", "u", "st", "x2"]):
            G[n] = at("g_" + n, A0 + 32 + 2 * i, [P, 4, P])
        oT = at("oT", A0 + 40, [P, 4, T])

        fraw = at("fraw", A0, [P, 4, T + 8])
        facc = at("facc", A0 + 9, [P, 4, T])
        fg = at("fg", A0 + 17, [P, 2, T])
        yA = at("yA", 88, [P, 8, T])
        yB = at("yB", A0, [P, 8, T])
        hmask = at("hmask", A0 + 16, [P, 8, P], U32)
        ch = at("ch", A0 + 20, [P, KT, CT], F32R)
        cl = at("cl", A0 + 28, [P, KT, CT], F32R)
        W0 = A0 + 36
        PP = at("PP", W0, [P, 2, T])
        QQ = at("QQ", W0 + 4, [P, 2, T])
        KK = at("KK", W0 + 8, [P, 2, T])
        KC = at("KC", W0 + 12, [P, 2, T])
        QC = at("QC", W0 + 16, [P, 2, T])
        qs = at("qs", W0 + 20, [P, 2, T])
        sz = at("sz", W0 + 24, [P, 2, T])
        sgt = at("sgt", W0 + 28, [P, 2, T])
        sgf = at("sgf", W0 + 32, [P, 2, T])
        MT = at("MT", 104, [P, TT, T])
        vT = at("vT", 112, [P, T])
        vt = at("vt", 114, [P, T])
        sgc = at("sgc", 116, [P, 2, CT])
        kcx = at("kcx", 118, [P, 2, CT])
        qcx = at("qcx", W0 + 36, [P, 2, CT])
        vcT = sq
        ctok = hf
        st2 = rs
        craw = at("craw", W0, [P, KT, CT])
        ctxtok = at("ctxtok", W0 + 8, [P, 2, D])
        dtok = at("dtok", A0, [P, TT, T])
        dch = at("dch", A0 + 8, [P, 2, GDIM])
        uT = at("uT", A0 + 10, [P, 2, T])
        zs = at("zs", A0 + 14, [P, 2, T])
        zsg = at("zsg", A0 + 18, [P, 2, T])
        AB = at("AB", A0 + 22, [P, TT, T])
        qsn = at("qsn", A0 + 30, [P, 2, T])
        yf = at("yf", A0 + 34, [P, 2, T])
        yg = at("yg", A0 + 38, [P, 2, T])
        otok = at("otok", A0 + 44, [P, TT, D])

        bank = [ctx.enter_context(nc.psum_tensor(f"bank{i}", [P, 512], F32)) for i in range(8)]

        def vcol(name, i=0):
            c = ROWS[name][0] + i
            return V[:, c:c + 1]

        halfeps = small[:, 0:1]
        onecol = small[:, 1:32]
        ada = small[:, 32:128]
        lb, oml = small[:, 128:160], small[:, 160:192]
        acoef = small[:, 192:240]
        beta, ggc, gcc, egc, kec = (gs[:, 16 * i:16 * i + 16] for i in range(5))
        ab = gs[:, 80:96]
        t1, t2 = gs[:, 96:128], gs[:, 128:160]
        mx, nmx, den, rden = gs[:, 160:192], gs[:, 192:224], gs[:, 224:256], gs[:, 256:288]
        silc = gs[:, 288:304]

        block = ctx.enter_context(nc.Block())

        def tile_last(t):
            return tiles[t][-1]

        FIRST = {}
        for t_no in range(len(tiles)):
            u = lin_units[tiles[t_no][0]]
            FIRST.setdefault(u["w"], t_no)
        T_OUT, T_UP, T_HG, T_HO, T_FT = FIRST["w_out"], FIRST["w_up"], FIRST["hg_w_in"], FIRST["hg_w_out"], FIRST["ft_w_in"]
        ffn_tiles = []
        t_no = T_UP
        for r in ROUND:
            ffn_tiles.append((t_no, t_no + 2 * len(r)))
            t_no += 2 * len(r) + KT
        ft_tiles = [T_FT, T_FT + 16 + KT]

        @block.sync
        def _(sp):
            sp.dma_start(xtok[:], d["x"][0].rearrange("(a p) c -> p a c", p=P)).then_inc(S("x_in"), 16)
            sp.dma_start(ident[:], d["cf"][:, 0:P]).then_inc(S("ident_in"), 16)

            def rows_in(name, src):
                r0, n = ROWS[name]
                done = 0
                while done < n:
                    a = r0 + done
                    k = min(n - done, P - a % P)
                    sp.dma_start(rowsT[a % P:a % P + k, a // P, :], src[done:done + k, :]).then_inc(S("rows_in"), 16)
                    rows_in.count += 16
                    done += k
            rows_in.count = 0
            rows_in("norm1", d["norm1_w"].rearrange("a (k p) -> (a k) p", p=P))
            rows_in("norm2", d["norm2_w"].rearrange("a (k p) -> (a k) p", p=P))
            rows_in("final1", d["final_norm_w"].rearrange("(k p) -> k p", p=P))
            rows_in("conv", d["conv_qkv_w"].rearrange("a i (k p) -> (a i k) p", p=P))
            rows_in("gdn_norm", d["gdn_norm_w"])
            rows_in("hg_norm", d["hg_norm_g_2"])
            rows_in("norm_g", d["norm_g_2"].rearrange("a (k p) -> (a k) p", p=P))
            rows_in("final_g", d["final_g_2"].rearrange("(k p) -> k p", p=P))
            lbl = d["hg_lb_logits_2"].rearrange("l s (k p) -> l (s k) p", p=P)
            rows_in("lb0", lbl[0])
            rows_in("lb1", lbl[1])
            rows_in("ada_b", d["ada_b_2"].rearrange("a (k p) -> (a k) p", p=P))
            rows_in("c", d["c_2"].rearrange("a (k p) -> (a k) p", p=P))
            rows_in("c_ctx", d["c_ctx_2"].rearrange("(k p) -> k p", p=P))
            rows_in("ffn_conv", d["ffn_conv_w"].rearrange("a i (k p) -> (a i k) p", p=P))
            assert rows_in.count == ROWS_LOADED
            sp.dma_start(cst[:, 0:P], d["cf"][:, P:2 * P]).then_inc(S("cst_in"), 16)
            sp.dma_start(gmask[:], d["cf"][:, 2 * P:9 * P].rearrange("p (l c) -> p l c", c=P)).then_inc(S("cst_in"), 16)
            sp.dma_start(dcnt[:], d["cf"][:, 9 * P:13 * P]).then_inc(S("cst_in"), 16)
            sp.dma_start(dneg[:], d["cf"][:, 13 * P:17 * P]).then_inc(S("cst_in"), 16)
            sp.dma_start(onecol, d["onecol"]).then_inc(S("cst_in"), 16)
            sp.dma_start(t1[0:1, 0:4], d["a_log"]).then_inc(S("cst_in"), 16)
            sp.dma_start(t1[0:1, 4:8], d["dt_bias"]).then_inc(S("cst_in"), 16)
            sp.dma_start(w8[:], d["w_in"][0, :, O_BA:O_BA + 8].rearrange("(k p) c -> p k c", p=P)).then_inc(S("cst_in"), 16)
            weights = {"w_in": d["w_in"][0], "w_out": d["w_out"][0], "w_up": d["w_up"][0], "w_down": d["w_down"][0],
                       "hg_w_in": d["hg_w_in_2"][0], "hg_w_out": d["hg_w_out_2"][0],
                       "ft_w_in": d["ft_w_in_2"][0], "ft_w_out": d["ft_w_out_2"][0]}
            for n, u in enumerate(units):
                w = d["ada_w_2"][u["layer"]] if u["w"] == "ada_w" else weights[u["w"]]
                k0, nk = u["rows"]
                if u["load"]:
                    sp.wait_ge(S(f"stage_free{u['slot']}"), u["load"])
                if u["lin"] and u["tile"] == T_HG and u["start"]:
                    sp.wait_ge(S("flo"), FT)
                    sp.dma_start(hmask[:], d["hm"]).then_inc(S("hmask_in"), 16)
                    sp.dma_start(ctxtok[:], d["ctx_2"][0].rearrange("(a p) c -> p a c", p=P)).then_inc(S("ctx_in"), 16)
                if u["lin"] and u["tile"] == T_FT and u["start"]:
                    sp.wait_ge(S("y_lo"), HG)
                    sp.dma_start(dtok[:], d["dtok"].rearrange("(a p) c -> p a c", p=P)).then_inc(S("dft_in"), 16)
                    sp.dma_start(dch[:], d["dch"].rearrange("(a p) c -> p a c", p=P)).then_inc(S("dft_in"), 16)
                sp.dma_start(stage[:, u["slot"], 0:nk, :],
                             w[k0 * P:(k0 + nk) * P, u["col"]:u["col"] + P].rearrange("(k p) c -> p k c", p=P)
                             ).then_inc(S(f"stage_in{u['slot']}"), 16)
            sp.wait_ge(S("out_ready"), 2 * TT)
            sp.dma_start(out[0].rearrange("(a p) c -> p a c", p=P), otok[:]).then_inc(S("stored"), 16)
            sp.wait_ge(S("stored"), 16)

        @block.gpsimd
        def _(pool):
            for l, u in enumerate(lin_units):
                nk = u["rows"][1]
                pool.wait_ge(S("hi_ready"), l + 1)
                pool.tensor_tensor(wl[:, l % NSPLIT, 0:nk, :], stage[:, u["slot"], 0:nk, :],
                                   wh[:, l % NSPLIT, 0:nk, :].bitcast(F32), ALU.subtract
                                   ).then_inc(S(f"stage_free{u['slot']}"), 1)

        class Own:

            def __init__(self, eng, chain):
                self.eng, self.chain, self.n, self.past = eng, chain, {}, []

            def __call__(self, ins, name=None, value=None):
                name = name or self.chain
                self.n[name] = value or self.n.get(name, 0) + 1
                ins.then_inc(S(name), 1)
                self.past = self.past[-3:] + [(name, self.n[name])]

            def settle(self, back=0):
                name, value = self.past[-1 - back]
                self.eng.wait_ge(S(name), value)

        def evac_name(t):
            return f"evac{t % NLIN}"

        @block.tensor
        def _(pe):
            pos = [0]

            def unit(u, first_x=None):
                slot, nk = u["slot"], u["rows"][1]
                if not u["lin"]:
                    pe.wait_ge(S(f"stage_in{slot}"), 16 * (u["load"] + 1))
                    pe.wait_ge(S("silc_ready"), 2)
                    for k in range(KT):
                        mm = pe.matmul(bank[7][:, 2 * u["raw"]:2 * u["raw"] + 2], stage[:, slot, k, :],
                                       silc[:, 2 * k:2 * k + 2], start=(k == 0), stop=(k == KT - 1))
                    mm.then_inc(S(f"stage_free{slot}"), 1)
                    return
                l, t = u["lin_no"], u["tile"]
                xh, xl = (hh, hl) if u["x"] == "h" else (gh, gl)
                pe.wait_ge(S(f"stage_free{slot}"), u["load"] + 1)
                if u["start"] and t >= NLIN:
                    pe.wait_ge(S(evac_name(t)), t // NLIN)
                s = l % NSPLIT
                for k in range(nk):
                    if first_x:
                        pe.wait_ge(S(first_x[0]), first_x[1] + k + 1)
                    a, b = u["start"] and k == 0, u["stop"] and k == nk - 1
                    pe.matmul(bank[t % NLIN][:], wh[:, s, k, :], xh[:, k, :], start=a, stop=False)
                    pe.matmul(bank[t % NLIN][:], wh[:, s, k, :], xl[:, k, :], start=False, stop=False)
                    mm = pe.matmul(bank[t % NLIN][:], wl[:, s, k, :], xh[:, k, :], start=False, stop=b)
                if u["ctx"]:
                    ci = 3 * ((t - T_HG) // 5) + (t - T_HG) % 5 - 1
                    half = [0, CT, 0][ci % 3]
                    if ci:
                        pe.wait_ge(S("cevac"), ci)
                    for k in range(nk):
                        a, b = k == 0, k == nk - 1
                        o = bank[7][:, half:half + CT]
                        pe.matmul(o, wh[:, s, k, :], ch[:, k, :], start=a, stop=False)
                        pe.matmul(o, wh[:, s, k, :], cl[:, k, :], start=False, stop=False)
                        mm = pe.matmul(o, wl[:, s, k, :], ch[:, k, :], start=False, stop=b)
                mm.then_inc(S("unit_done"), 1)

            def units_to(tile, first_x=None):
                while True:
                    u = units[pos[0]]
                    unit(u, first_x)
                    first_x = None if u["lin"] else first_x
                    pos[0] += 1
                    if u["lin"] and u["tile"] == tile and u["stop"]:
                        break

            def norm_sum(n, width):
                for k in range(KT):
                    pe.wait_ge(S("sq_ready"), KT * n + k + 1)
                    pe.matmul(bank[3][:, 0:width], ones[:], sq[:, k % 2, 0:width], start=(k == 0), stop=(k == KT - 1)
                              ).then_inc(S("sq_used"), 1)

            def col_sum(i):
                pe.wait_ge(S("l2_sq"), i + 1)
                if i >= 2:
                    pe.wait_ge(S("l2_rs"), i - 1)
                pe.matmul(bank[4 + i % 2][:], ones[:], sq[:, i % 2, :], start=True, stop=True
                          ).then_inc(S("l2_sum"), 1)

            pe.wait_ge(S("ident_in"), 16)
            pe.wait_ge(S("rows_in"), ROWS_LOADED)
            for a in range(3):
                n = min(P, NROWS - a * P)
                mm = pe.transpose(bank[4][:, a * P:a * P + n], rowsT[0:n, a, :], ident[0:n, 0:n])
            mm.then_inc(S("rows_T"), 1)
            pe.wait_ge(S("x_in"), 16)
            for k in range(KT):
                if k >= 2:
                    pe.wait_ge(S("xT_ev"), k - 1)
                for a in range(TT):
                    mm = pe.transpose(bank[k % 2][:, a * P:(a + 1) * P], xtok[:, a, k * P:(k + 1) * P], ident[:])
                mm.then_inc(S("xT_ps"), 1)
            pe.wait_ge(S("const_set"), 2)
            norm_sum(0, T)
            units_to(27, ("h_ready", 0))
            pe.wait_ge(S("cst_in"), 8 * 16)
            for a in range(TT):
                for k in range(KT):
                    for part, xx_ in enumerate((hh, hl)):
                        pe.matmul(bank[3][:, a * 8:a * 8 + 8], xx_[:, k, a * P:(a + 1) * P].bitcast(F32), w8[:, k, :],
                                  start=(k == 0 and part == 0), stop=(k == KT - 1 and part == 1))
            pe.matmul(bank[3][:, 64:72], ones[0:1, :], t1[0:1, 0:8], start=True, stop=True).then_inc(S("ba_ready"), 1)
            for i in range(8):
                col_sum(i)

            for a in range(TT):
                if a >= 2:
                    pe.wait_ge(S("vb_ev"), a - 1)
                if a == 0:
                    pe.wait_ge(S("evac0"), 28 // 3 + 1)
                    pe.wait_ge(S("evac1"), 9)
                    pe.wait_ge(S("evac2"), 9)
                for j in range(4):
                    mm = pe.transpose(bank[6 + a % 2][:, j * P:(j + 1) * P], bqkv[:, 8 + j, a * P:(a + 1) * P], ident[:])
                mm.then_inc(S("vb_T"), 1)

            def turn(n):
                h, i = n // 4, n % 4
                pe.wait_ge(S("p_ready"), n + 1)
                if n >= 2:
                    pe.wait_ge(S("pT_ev"), n - 1)
                else:
                    pe.wait_ge(S("vb_ev"), TT)
                for j in range(i + 1):
                    mm = pe.transpose(bank[6 + n % 2][:, j * P:(j + 1) * P], pr[:, n % 2, j * P:(j + 1) * P], ident[:])
                mm.then_inc(S("pT_done"), 1)

            def weigh(h):
                pe.wait_ge(S("pT_ev"), 4 * h + 4)
                if h % 2 == 0 and h >= 4:
                    pe.wait_ge(S("ob_lo"), h // 2 - 1)
                o = 64 * (h % 2)
                for j in range(TT):
                    mm = pe.matmul(bank[(h // 2) % 2][o:o + 64, j * P:T], vb[:, j, h * 64:h * 64 + 64],
                                   pT[:, h % 2, j, j * P:T], start=(j == 0), stop=(j == TT - 1))
                mm.then_inc(S("pv_done"), 1)

            for n in range(4 * DH_N + 1):
                if n < 4 * DH_N:
                    h, i = n // 4, n % 4
                    o = 64 * (h % 2)
                    if n >= 2:
                        pe.wait_ge(S("sm_ready"), n - 1)
                    else:
                        pe.wait_ge(S("l2_rs"), 8)
                    pe.matmul(bank[4 + n % 2][:, 0:(i + 1) * P], bqkv[o:o + 64, h // 2, i * P:(i + 1) * P],
                              bqkv[o:o + 64, 4 + h // 2, 0:(i + 1) * P], start=True, stop=True).then_inc(S("s_done"), 1)
                if n >= 1:
                    turn(n - 1)
                    if n % 4 == 0:
                        weigh(n // 4 - 1)

            pe.wait_ge(S("g_ready"), 1)
            pe.matmul(bank[3][:, 80:96], cst[:, 0:P], ggc, start=True, stop=True).then_inc(S("gc_ps"), 1)
            for c in range(TT):
                tok = slice(c * P, (c + 1) * P)
                pe.wait_ge(S("ug"), c + 1)
                for h in range(4):
                    mm = pe.matmul(bank[3][:, h * P:(h + 1) * P], ones[:], G["ug"][:, h, :], start=True, stop=True)
                mm.then_inc(S("gr"), 1)
                if c:
                    pe.wait_ge(S("o_ev"), c)
                    pe.wait_ge(S("st_upd"), c)
                else:
                    pe.wait_ge(S("pT_ev"), 32)
                for h in range(4):
                    pe.matmul(bank[4][:, h * P:(h + 1) * P], qkv[:, 4 + h, tok], qkv[:, 4 + h, tok], start=True, stop=True)
                for h in range(4):
                    mm = pe.matmul(bank[5][:, h * P:(h + 1) * P], qkv[:, 4 + h, tok], qkv[:, h, tok], start=True, stop=True)
                mm.then_inc(S("kk"), 1)
                for h in range(4):
                    pe.transpose(bank[6][:, h * P:(h + 1) * P], qkv[:, 8 + h, tok], ident[:])
                for h in range(4):
                    mm = pe.transpose(bank[7][:, h * P:(h + 1) * P], qkv[:, 4 + h, tok], ident[:])
                mm.then_inc(S("vk"), 1)
                pe.wait_ge(S("x1"), c + 1)
                for h in range(4):
                    mm = pe.transpose(bank[4][:, h * P:(h + 1) * P], G["xt"][:, h, :], ident[:])
                mm.then_inc(S("x1T"), 1)
                for l in range(1, 7):
                    q = 6 * c + l
                    pe.wait_ge(S("m_rdy"), q)
                    if l == 1:
                        pe.wait_ge(S("x1e"), c + 1)
                    else:
                        pe.wait_ge(S("x_upd"), q - 1)
                    for h in range(4):
                        mm = pe.matmul(bank[3][:, h * P:(h + 1) * P], G["m%d" % (l % 2)][:, h, :], G["xx"][:, h, :],
                                       start=True, stop=True)
                    mm.then_inc(S("T"), 1)
                    pe.wait_ge(S("Te"), q)
                    if l < 6:
                        for h in range(4):
                            pe.matmul(bank[4][:, h * P:(h + 1) * P], G["xt"][:, h, :], G["tt"][:, h, :], start=True, stop=True)
                    for h in range(4):
                        mm = pe.matmul(bank[5][:, h * P:(h + 1) * P], G["tt"][:, h, :], G["xt"][:, h, :], start=True, stop=True)
                    mm.then_inc(S("XX"), 1)
                pe.wait_ge(S("x_upd"), 6 * c + 6)
                pe.wait_ge(S("gkv"), c + 1)
                for h in range(4):
                    pe.matmul(bank[6][:, h * P:(h + 1) * P], G["xt"][:, h, :], G["vtok"][:, h, :], start=True, stop=True)
                for h in range(4):
                    mm = pe.matmul(bank[7][:, h * P:(h + 1) * P], G["gk"][:, h, :], G["xt"][:, h, :], start=True, stop=True)
                mm.then_inc(S("uw"), 1)
                if c:
                    pe.wait_ge(S("uwe"), c + 1)
                    for h in range(4):
                        mm = pe.matmul(bank[3][:, h * P:(h + 1) * P], G["wkT"][:, h, :], G["st"][:, h, :], start=True, stop=True)
                    mm.then_inc(S("PS"), 1)
                pe.wait_ge(S("u"), c + 1)
                for h in range(4):
                    o = bank[4][:, h * P:(h + 1) * P]
                    if c:
                        pe.matmul(o, G["st"][:, h, :], G["qdec"][:, h, :], start=True, stop=False)
                    mm = pe.matmul(o, G["u"][:, h, :], G["at_"][:, h, :], start=(c == 0), stop=True)
                mm.then_inc(S("o"), 1)
                if c < TT - 1:
                    for h in range(4):
                        mm = pe.matmul(bank[5][:, h * P:(h + 1) * P], G["kend"][:, h, :], G["u"][:, h, :], start=True, stop=True)
                    mm.then_inc(S("ds"), 1)
            pe.wait_ge(S("o_ev"), TT)
            for i in range(8, 12):
                col_sum(i)

            pe.wait_ge(S("oa_lo"), 4)
            pe.wait_ge(S("ob_lo"), 4)
            units_to(T_OUT + KT - 1)
            norm_sum(1, T)
            pairs = 0
            for r, (t0, t1_) in enumerate(ffn_tiles):
                units_to(t1_ - 1, ("h_ready", KT) if r == 0 else None)
                pairs += len(ROUND[r])
                pe.wait_ge(S("flo"), pairs)
                units_to(t1_ + KT - 1)
            norm_sum(2, T)
            norm_sum(3, T)
            pe.wait_ge(S("ctx_in"), 16)
            for k in range(KT):
                if k >= 2:
                    pe.wait_ge(S("cx_ev"), k - 1)
                for a in range(2):
                    mm = pe.transpose(bank[4 + k % 2][:, a * P:(a + 1) * P], ctxtok[:, a, k * P:(k + 1) * P], ident[:])
                mm.then_inc(S("cx_T"), 1)
            norm_sum(4, CT)

            def turn_values(h):
                tv = T_HG + 5 * h + 3
                pe.wait_ge(S(evac_name(tv)), tv // NLIN + 1)
                if h:
                    pe.wait_ge(S("osq"), h)
                    pe.wait_ge(S("y_pre"), h)
                for a in range(TT):
                    mm = pe.transpose(bank[6][:, a * P:(a + 1) * P], vT[:, a * P:(a + 1) * P], ident[:])
                mm.then_inc(S("b6"), 1)
                pe.wait_ge(S("kq_rdy"), h + 1)
                pe.wait_ge(S("b6e"), 4 * h + 1)
                for a in range(4):
                    mm = pe.transpose(bank[6][:, a * P:(a + 1) * P], kcx[:, a // 2, (a % 2) * P:(a % 2 + 1) * P], ident[:])
                mm.then_inc(S("b6"), 1)
                pe.wait_ge(S("b6e"), 4 * h + 2)
                for a in range(2):
                    mm = pe.transpose(bank[6][:, a * P:(a + 1) * P], vcT[:, 0, a * P:(a + 1) * P], ident[:])
                mm.then_inc(S("b6"), 1)
                pe.wait_ge(S("b6e"), 4 * h + 3)
                for dr in range(2):
                    for a in range(2):
                        mm = pe.matmul(bank[6][:, dr * P:(dr + 1) * P], ctok[:, 0, (2 * dr + a) * P:(2 * dr + a + 1) * P],
                                       st2[:, CT + a * P:CT + (a + 1) * P], start=(a == 0), stop=(a == 1))
                mm.then_inc(S("b6"), 1)

            def level(h, li):
                prod = min(li, 9)
                pe.wait_ge(S("lv_rdy"), 10 * h + prod + 1)
                if 11 * h + li >= 2:
                    pe.wait_ge(S("lv_ev%d" % (li % 2)), (6 if li % 2 == 0 else 5) * h + li // 2)
                b = bank[4 + li % 2]
                kc, qc = KC[:, prod % 2, :], QC[:, prod % 2, :]
                if li <= 7:
                    for a in range(TT):
                        mm = pe.matmul(b[:, a * P:(a + 1) * P], kc[:, a * P:(a + 1) * P], qc[:, a * P:(a + 1) * P],
                                       start=True, stop=True)
                elif li == 8:
                    for a in range(TT):
                        o = a ^ 1
                        mm = pe.matmul(b[:, a * P:(a + 1) * P], kc[:, a * P:(a + 1) * P], qc[:, o * P:(o + 1) * P],
                                       start=True, stop=True)
                else:
                    for i in range(2):
                        a = 2 * (li - 9) + i
                        o = 256 * (1 - a // 2)
                        mm = pe.matmul(b[:, i * 256:(i + 1) * 256], kc[:, a * P:(a + 1) * P], qc[:, o:o + 256],
                                       start=True, stop=True)
                mm.then_inc(S("lv_mm"), 1)

            def output(h):
                pe.wait_ge(S("b6e"), 4 * h + 4)
                pe.wait_ge(S("lv_ev0"), 6 * h + 6)
                pe.wait_ge(S("lv_ev1"), 5 * h + 5)
                pe.wait_ge(S("qp_rdy"), h + 1)
                for a in range(TT):
                    pe.matmul(bank[6][:], vt[:, a * P:(a + 1) * P], MT[:, a, :], start=(a == 0), stop=False)
                for dr in range(2):
                    mm = pe.matmul(bank[6][:], st2[:, dr * P:(dr + 1) * P], QQ[:, dr, :], start=False, stop=(dr == 1))
                mm.then_inc(S("o_mm"), 1)

            def meansq(h):
                pe.wait_ge(S("osq"), h + 1)
                pe.matmul(bank[3][0:HG, :], onecol[:, 15 - h:31 - h], vcT[:, 1, :], start=(h == 0), stop=(h == HG - 1)
                          ).then_inc(S("ms_mm"), 1)

            for h in range(HG + 1):
                t = T_HG + 5 * h
                if h < HG:
                    units_to(t, ("h_ready", 2 * KT) if h == 0 else None)
                    if h == 0:
                        pe.wait_ge(S("h_ready"), 4 * KT)
                if h:
                    if h >= 2:
                        meansq(h - 2)
                    turn_values(h - 1)
                if h < HG:
                    units_to(t + 1)
                if h:
                    for li in range(0, 3):
                        level(h - 1, li)
                if h < HG:
                    units_to(t + 2)
                if h:
                    for li in range(3, 6):
                        level(h - 1, li)
                if h < HG:
                    units_to(t + 3)
                if h:
                    for li in range(6, 9):
                        level(h - 1, li)
                if h < HG:
                    units_to(t + 4)
                if h:
                    for li in range(9, 11):
                        level(h - 1, li)
                    output(h - 1)
            meansq(HG - 1)
            pe.wait_ge(S("rs16"), 1)
            for h in range(HG):
                if h >= 2:
                    pe.wait_ge(S("y_norm"), h - 1)
                pe.matmul(bank[4 + h % 2][:], bass.AP(tensor=ident[:].tensor, offset=h, ap=[[P, HG], [0, P]]),
                          rs[0:HG, :], start=True, stop=True).then_inc(S("rs_row"), 1)
            pe.wait_ge(S("y_lo"), HG)
            units_to(T_HO + KT - 1)
            norm_sum(5, T)

            for gi in range(GROUPS):
                t = ft_tiles[gi // 4] + 4 * (gi % 4)
                units_to(t + 1, ("h_ready", 4 * KT) if gi == 0 else None)
                units_to(t + 3)
                pe.wait_ge(S(evac_name(t + 1)), (t + 1) // NLIN + 1)
                pe.wait_ge(S("dft_in"), 32)
                if gi:
                    pe.wait_ge(S("ab_ev"), 2 * gi)
                for a in range(TT):
                    for c in range(2):
                        mm = pe.matmul(bank[4 + a // 2][:, (a % 2) * GDIM:(a % 2 + 1) * GDIM], uT[:, c, a * P:(a + 1) * P],
                                       dch[:, c, :], start=(c == 0), stop=(c == 1))
                mm.then_inc(S("ab_mm"), 1)
                pe.wait_ge(S("ab_ev"), 2 * gi + 2)
                for g in range(2):
                    if gi:
                        pe.wait_ge(S("y_ev"), 2 * (gi - 1) + g + 1)
                    b = bank[6 + g]
                    for a in range(TT):
                        pe.matmul(b[:, 0:257], AB[:, a, g * P:(g + 1) * P], dtok[:, a, 0:257], start=(a == 0), stop=(a == TT - 1))
                    for a in range(TT):
                        mm = pe.matmul(b[:, 257:512], AB[:, a, GDIM + g * P:GDIM + (g + 1) * P], dtok[:, a, 257:512],
                                       start=(a == 0), stop=(a == TT - 1))
                    mm.then_inc(S("y_mm"), 1)
                if gi % 4 == 3:
                    pe.wait_ge(S("yg_lo"), 2 * gi + 2)
                    units_to(t + 4 + KT - 1)
            assert pos[0] == len(units)
            norm_sum(6, T)
            pe.wait_ge(S("x_final"), KT)
            for a in range(TT):
                for half in range(2):
                    i = 2 * a + half
                    if i >= 2:
                        pe.wait_ge(S("out_ready"), i - 1)
                    for k in range(4):
                        mm = pe.transpose(bank[4 + i % 2][:, k * P:(k + 1) * P],
                                          xT[:, 4 * half + k, a * P:(a + 1) * P], ident[:])
                    mm.then_inc(S("out_ps"), 1)

        @block.scalar
        def _(act):
            do = Own(act, "act_chain")
            A = nc.scalar

            def high(l):
                if l >= n_lin:
                    return
                u = lin_units[l]
                act.wait_ge(S(f"stage_in{u['slot']}"), 16 * (u["load"] + 1))
                if l >= NSPLIT:
                    act.wait_ge(S("unit_done"), l - NSPLIT + 1)
                nk = u["rows"][1]
                do(A.activation(wh[:, l % NSPLIT, 0:nk, :], stage[:, u["slot"], 0:nk, :], ACT.Copy), "hi_ready")

            def finish_tile(t):
                for l in tiles[t]:
                    high(l + NSPLIT)
                act.wait_ge(S("unit_done"), tile_last(t) + 1)

            def evac(t, ins):
                do(ins, evac_name(t), t // NLIN + 1)

            def norm(n, width, src, ready):
                for k in range(KT):
                    if k >= 2 or n:
                        act.wait_ge(S("sq_used"), KT * n + k - 1)
                    act.wait_ge(S(ready[0]), ready[1] + (k + 1 if ready[2] else 0))
                    do(A.activation(sq[:, k % 2, 0:width], src[:, k, :], ACT.Square), "sq_ready")
                act.wait_ge(S("sq_used"), KT * n + KT)
                do(A.activation(rs[:, 0:width], bank[3][:, 0:width], ACT.Ln, scale=1.0 / D, bias=halfeps))
                do.settle()
                do(A.activation(rs[:, 0:width], rs[:, 0:width], ACT.Exp, scale=-0.5), "rs_ready")

            def split_high(m, dst, width):
                for k in range(KT):
                    act.wait_ge(S("hf_ready"), KT * m + k + 1)
                    do(A.activation(dst[:, k, :], hf[:, k % 2, 0:width], ACT.Copy), "hh_ready")

            def col_root(i, eps_scale):
                act.wait_ge(S("l2_sum"), i + 1)
                if i >= 2:
                    act.wait_ge(S("l2_done"), i - 1)
                do(A.activation(hf[:, i % 2, :], bank[4 + i % 2][:], ACT.Ln, scale=eps_scale, bias=halfeps))
                do.settle()
                do(A.activation(hf[:, i % 2, :], hf[:, i % 2, :], ACT.Exp, scale=-0.5), "l2_rs")

            def col_square(i, src):
                if i >= 2:
                    act.wait_ge(S("l2_sum"), i - 1)
                do(A.activation(sq[:, i % 2, :], src, ACT.Square), "l2_sq")

            act.wait_ge(S("rows_T"), 1)
            do(A.activation(V[:, 0:NROWS], bank[4][:, 0:NROWS], ACT.Copy), "V_ready")
            do.settle()
            act.wait_ge(S("const_set"), 2)
            norm(0, T, xT, ("xT_ev", 0, True))
            split_high(0, hh, T)
            for l in range(NSPLIT):
                high(l)
            act.wait_ge(S("lb_diff"), 2)
            do(A.activation(lb, lb, ACT.Exp))
            do(A.activation(oml, oml, ACT.Exp), "lb_exp")

            def silu_conv(t):
                act.wait_ge(S("conv_done"), t + 1)
                do(A.activation(qkv[:, t, :], hf[:, t % 2, :], ACT.Silu), "silu_done")
            for t in range(28):
                finish_tile(t)
                if t < 12:
                    if t == 0:
                        act.wait_ge(S("raw_zero"), 1)
                    if t >= 2:
                        act.wait_ge(S("conv_done"), t - 1)
                    evac(t, A.activation(raw[:, t % 2, 3:3 + T], bank[t % NLIN][:], ACT.Copy))
                elif t < 16:
                    evac(t, A.activation(zT[:, t - 12, :], bank[t % NLIN][:], ACT.Silu))
                else:
                    evac(t, A.activation(bqkv[:, t - 16, :], bank[t % NLIN][:], ACT.Copy))
                if 1 <= t <= 12:
                    silu_conv(t - 1)
            do(A.activation(silc[:, 0:16:2], V[:, ROWS["c"][0]:ROWS["c"][0] + 8], ACT.Silu), "silc_ready")
            do(A.activation(silc[:, 1:16:2], V[:, ROWS["c_ctx"][0]:ROWS["c_ctx"][0] + 8], ACT.Silu), "silc_ready")
            act.wait_ge(S("ba_ready"), 1)
            b3 = bank[3][:, 0:32].rearrange("p (a c) -> p a c", c=8)
            do(A.activation(beta.rearrange("p (a c) -> p a c", c=4), b3[:, :, 0:4], ACT.Sigmoid))
            do(A.activation(ab[:, 4:8], bank[3][:, 68:72], ACT.Copy))
            do(A.activation(ab[:, 0:4], bank[3][:, 64:68], ACT.Exp), "ba_act")
            act.wait_ge(S("sp_abs"), 1)
            do(A.activation(t2[:, 16:32], t2[:, 16:32], ACT.Exp, scale=-1.0))
            do.settle()
            do(A.activation(t2[:, 16:32], t2[:, 16:32], ACT.Ln, bias=1.0), "sp_ln")
            for i in range(9):
                if i < 8:
                    col_square(i, qkv[:, i, :])
                if i >= 1:
                    col_root(i - 1, 1.0)

            for a in range(TT):
                act.wait_ge(S("vb_T"), a + 1)
                do(A.activation(vb[:, a, :], bank[6 + a % 2][:], ACT.Copy), "vb_ev")

            def place(n):
                h, i = n // 4, n % 4
                act.wait_ge(S("pT_done"), n + 1)
                if h >= 2:
                    act.wait_ge(S("pv_done"), h - 1)
                do(A.activation(pT[:, h % 2, 0:i + 1, i * P:(i + 1) * P],
                                bank[6 + n % 2][:, 0:(i + 1) * P].rearrange("p (j c) -> p j c", c=P), ACT.Copy), "pT_ev")
            for n in range(4 * DH_N + 1):
                if n < 4 * DH_N:
                    w = (n % 4 + 1) * P
                    act.wait_ge(S("nmx_ready"), n + 1)
                    do(A.activation(sm[:, n % 2, 0:w], sm[:, n % 2, 0:w], ACT.Exp, bias=nmx[:, n:n + 1]), "pexp")
                if n:
                    place(n - 1)
                if n % 8 == 0 and n:
                    hp = n // 8 - 1
                    act.wait_ge(S("pv_done"), 2 * hp + 2)
                    do(A.activation(gh[:, 4 + hp, :], bank[hp % 2][:], ACT.Copy), "ob_hi")

            act.wait_ge(S("gc_ps"), 1)
            do(A.activation(gcc, bank[3][:, 80:96], ACT.Copy))
            do(A.activation(egc, bank[3][:, 80:96], ACT.Exp), "gcc_ready")
            for c in range(TT):
                tok = slice(c * P, (c + 1) * P)
                act.wait_ge(S("dif"), c + 1)
                do(A.activation(G["ee"][:], G["ee"][:], ACT.Exp))
                do(A.activation(G["eg"][:], bank[3][:].rearrange("p (h c) -> p h c", c=P), ACT.Exp))
                do(A.activation(kec[:, 4 * c:4 * c + 4], kec[:, 4 * c:4 * c + 4], ACT.Exp), "eex")
                act.wait_ge(S("x1T"), c + 1)
                do(A.activation(G["xx"][:], bank[4][:].rearrange("p (h c) -> p h c", c=P), ACT.Copy), "x1e")
                for l in range(1, 7):
                    act.wait_ge(S("T"), 6 * c + l)
                    do(A.activation(G["tt"][:], bank[3][:].rearrange("p (h c) -> p h c", c=P), ACT.Copy), "Te")
                act.wait_ge(S("uw"), c + 1)
                do(A.activation(G["uv"][:], bank[6][:].rearrange("p (h c) -> p h c", c=P), ACT.Copy))
                do(A.activation(G["wkT"][:], bank[7][:].rearrange("p (h c) -> p h c", c=P), ACT.Copy), "uwe")
                act.wait_ge(S("o"), c + 1)
                do(A.activation(oT[:, :, tok], bank[4][:].rearrange("p (h c) -> p h c", c=P), ACT.Copy), "o_ev")
            for i in range(8, 13):
                if i < 12:
                    col_square(i, oT[:, i - 8, :]) if i > 8 else (do.settle(), col_square(i, oT[:, 0, :]))
                if i >= 9:
                    col_root(i - 1, 1.0 / P)
            for h in range(4):
                act.wait_ge(S("oa"), h + 1)
                do(A.activation(gh[:, h, :], oT[:, h, :], ACT.Copy), "oa_hi")

            for n in range(KT):
                finish_tile(T_OUT + n)
            norm(1, T, xT, (evac_name(T_OUT + KT - 1), (T_OUT + KT - 1) // NLIN + 1, False))
            split_high(1, hh, T)
            p = 0
            for r, (t0, t1_) in enumerate(ffn_tiles):
                for j in range(len(ROUND[r])):
                    for half in range(2):
                        t = t0 + 2 * j + half
                        finish_tile(t)
                        if p == 0:
                            act.wait_ge(S("fraw_zero"), 1)
                        if p >= 2:
                            act.wait_ge(S("fconv"), 2 * p - 2)
                        evac(t, A.activation(fraw[:, 2 * (p % 2) + half, 2:2 + T], bank[t % NLIN][:], ACT.Copy))
                    act.wait_ge(S("fconv"), 2 * p + 1)
                    do(A.activation(fg[:, p % 2, :], facc[:, 2 * (p % 2), :], ACT.Silu), "fsilu")
                    act.wait_ge(S("fprod"), p + 1)
                    do(A.activation(gh[:, j, :], facc[:, 2 * (p % 2) + 1, :], ACT.Copy), "fhi")
                    p += 1
                for n in range(KT):
                    finish_tile(t1_ + n)
            last = T_HG - 1
            norm(2, T, xT, (evac_name(last), last // NLIN + 1, False))
            norm(3, T, xT, ("x1_norm", 0, True))
            split_high(2, hh, T)
            for k in range(KT):
                act.wait_ge(S("cx_T"), k + 1)
                do(A.activation(craw[:, k, :], bank[4 + k % 2][:, 0:CT], ACT.Copy), "cx_ev")
            norm(4, CT, craw, ("cx_ev", 0, True))
            split_high(3, ch, CT)

            def aux_early(g):
                act.wait_ge(S("b6"), 4 * g + 1)
                do(A.activation(vt[:], bank[6][:], ACT.Copy), "b6e")
                act.wait_ge(S("b6"), 4 * g + 2)
                do(A.activation(ctok[:, 0, :], bank[6][:], ACT.Copy), "b6e")
                act.wait_ge(S("b6"), 4 * g + 3)
                do(A.activation(st2[:, CT:2 * CT], bank[6][:, 0:CT], ACT.Copy), "b6e")
                act.wait_ge(S("b6"), 4 * g + 4)
                do(A.activation(st2[:, 0:CT], bank[6][:, 0:CT], ACT.Copy), "b6e")

            def place_level(g, li):
                act.wait_ge(S("lv_mm"), 11 * g + li + 1)
                b = bank[4 + li % 2]
                if li == 8:
                    src = view(b[:], [[2 * P, 2], [P, 2], [1, P]])
                    dst = view(MT[:, 0, 0:1], [[2 * T + 2 * P, 2], [T - P, 2], [1, P]], P)
                else:
                    a = 2 * (li - 9)
                    src = b[:].rearrange("p (i c) -> p i c", i=2)
                    dst = MT[:, a:a + 2, 256 * (10 - li):256 * (10 - li) + 256]
                do(A.activation(dst, src, ACT.Copy), "lv_ev%d" % (li % 2), (6 if li % 2 == 0 else 5) * g + li // 2 + 1)

            for h in range(HG + 1):
                t = T_HG + 5 * h
                if h < HG:
                    finish_tile(t)
                    if h:
                        act.wait_ge(S("sgt_q"), h)
                    do(A.activation(sgt[:, 0, :], bank[t % NLIN][:], ACT.Sigmoid), "sg_q")
                if h:
                    aux_early(h - 1)
                if h < HG:
                    for dr in range(2):
                        finish_tile(t + 1 + dr)
                        if h:
                            act.wait_ge(S("sgf_used"), h)
                            act.wait_ge(S("kq_rdy"), h)
                        do(A.activation(sgc[:, dr, :], bank[7][:, dr * CT:(dr + 1) * CT], ACT.Sigmoid), "cevac")
                        evac(t + 1 + dr, A.activation(sgf[:, dr, :], bank[(t + 1 + dr) % NLIN][:], ACT.Sigmoid))
                    finish_tile(t + 3)
                    if h:
                        act.wait_ge(S("b6"), 4 * h)
                    do(A.activation(vcT[:, 0, 0:CT], bank[7][:, 0:CT], ACT.Copy), "cevac")
                    do(A.activation(vT[:], bank[(t + 3) % NLIN][:], ACT.Copy), evac_name(t + 3), (t + 3) // NLIN + 1)
                if h:
                    place_level(h - 1, 8)
                if h < HG:
                    finish_tile(t + 4)
                    if h:
                        act.wait_ge(S("sz_rdy"), h)
                    do(A.activation(sgt[:, 1, :], bank[(t + 4) % NLIN][:], ACT.Sigmoid), "sg_z")
                if h:
                    place_level(h - 1, 9)
                    place_level(h - 1, 10)
                    act.wait_ge(S("o_mm"), h)
                    if h >= 2:
                        act.wait_ge(S("ms_mm"), h - 1)
                    do(A.activation(vcT[:, 1, :], bank[6][:], ACT.Square), "osq")
            act.wait_ge(S("ms_mm"), HG)
            do(A.activation(rs[0:HG, :], bank[3][0:HG, :], ACT.Ln, scale=1.0 / P, bias=halfeps[0:HG, :]))
            do.settle()
            do(A.activation(rs[0:HG, :], rs[0:HG, :], ACT.Exp, scale=-0.5), "rs16")
            for h in range(HG):
                act.wait_ge(S("y_norm"), h + 1)
                src = yA[:, h, :] if h < 8 else yB[:, h - 8, :]
                dst = hh[:, h, :] if h < 8 else gh[:, h - 8, :]
                do(A.activation(dst, src, ACT.Copy), "y_hi")
            for n in range(KT):
                finish_tile(T_HO + n)
            norm(5, T, xT, (evac_name(T_HO + KT - 1), (T_HO + KT - 1) // NLIN + 1, False))
            split_high(4, hh, T)

            for gi in range(GROUPS):
                t = ft_tiles[gi // 4] + 4 * (gi % 4)
                for c in range(2):
                    finish_tile(t + c)
                    if gi:
                        act.wait_ge(S("ab_mm"), gi)
                    do(A.activation(uT[:, c, :], bank[(t + c) % NLIN][:], ACT.Copy), evac_name(t + c), (t + c) // NLIN + 1)
                for c in range(2):
                    finish_tile(t + 2 + c)
                    if gi:
                        act.wait_ge(S("zs_rdy"), 2 * gi)
                    do(A.activation(zsg[:, c, :], bank[(t + 2 + c) % NLIN][:], ACT.Sigmoid), "zsg")
                act.wait_ge(S("ab_mm"), gi + 1)
                if gi:
                    act.wait_ge(S("y_mm"), 2 * gi)
                else:
                    act.wait_ge(S("ab_zero"), 2)
                for i in range(2):
                    src, dst = bank[4 + i], AB[:, 2 * i, 0:1]
                    do(A.activation(view(dst, [[T, 2], [1, 129]]), view(src[:, 0:1], [[GDIM, 2], [1, 129]]), ACT.Copy))
                    do(A.activation(view(dst, [[T, 2], [1, 127]], 129), view(src[:, 0:1], [[GDIM, 2], [-1, 127]], 127), ACT.Copy))
                    do(A.activation(view(dst, [[T, 2], [1, 127]], GDIM + 1), view(src[:, 0:1], [[GDIM, 2], [1, 127]], 129), ACT.Copy),
                       "ab_act")
                for g in range(2):
                    act.wait_ge(S("y_mm"), 2 * gi + g + 1)
                    if gi:
                        act.wait_ge(S("yf_rdy"), 2 * gi + g - 1)
                    do(A.activation(qsn[:, g, 0:255], bank[6 + g][:, 257:512], ACT.Copy), "qsn")
                for g in range(2):
                    act.wait_ge(S("yg_rdy"), 2 * gi + g + 1)
                    if gi == 4:
                        pass
                    do(A.activation(gh[:, 2 * (gi % 4) + g, :], yg[:, g, :], ACT.Copy), "yg_hi")
                if gi % 4 == 3:
                    for n in range(KT):
                        finish_tile(t + 4 + n)
            last = len(tiles) - 1
            norm(6, T, xT, (evac_name(last), last // NLIN + 1, False))
            for i in range(2 * TT):
                act.wait_ge(S("out_ps"), i + 1)
                do(A.activation(otok[:, i // 2, (i % 2) * 512:(i % 2 + 1) * 512], bank[4 + i % 2][:], ACT.Copy), "out_ready")

        @block.vector
        def _(dve):
            do = Own(dve, "dve_chain")
            X = nc.vector

            def evac(t, ins):
                do(ins, evac_name(t), t // NLIN + 1)

            def finish_tile(t):
                dve.wait_ge(S("unit_done"), tile_last(t) + 1)

            def norm(n, m, width, src, coef, shift, dst_hi, dst_lo):
                dve.wait_ge(S("rs_ready"), n + 1)
                do.settle()

                def low(k):
                    dve.wait_ge(S("hh_ready"), KT * m + k + 1)
                    do(X.tensor_tensor(dst_lo[:, k, :], hf[:, k % 2, 0:width], dst_hi[:, k, :].bitcast(F32), ALU.subtract),
                       "h_ready")
                for k in range(KT):
                    if k >= 2:
                        do.settle()
                    if shift:
                        do(X.scalar_tensor_tensor(hf[:, k % 2, 0:width], src[:, k, :], coef(k), rs[:, 0:width], ALU.mult, ALU.mult))
                        do.settle()
                        do(X.tensor_scalar(hf[:, k % 2, 0:width], hf[:, k % 2, 0:width], shift(k), None, ALU.add), "hf_ready")
                    else:
                        do(X.scalar_tensor_tensor(hf[:, k % 2, 0:width], src[:, k, :], coef(k), rs[:, 0:width], ALU.mult, ALU.mult),
                           "hf_ready")
                    if k:
                        low(k - 1)
                low(KT - 1)

            def residual(t, n, gate=None):
                finish_tile(t)
                if gate is None:
                    evac(t, X.tensor_tensor(xT[:, n, :], xT[:, n, :], bank[t % NLIN][:], ALU.add))
                else:
                    evac(t, X.scalar_tensor_tensor(xT[:, n, :], bank[t % NLIN][:], gate(n), xT[:, n, :], ALU.mult, ALU.add))

            do(X.memset(ones[:], 1.0), "const_set")
            do(X.memset(halfeps, EPS), "const_set")
            for k in range(KT):
                dve.wait_ge(S("xT_ps"), k + 1)
                do(X.tensor_copy(xT[:, k, :], bank[k % 2][:]), "xT_ev")
            dve.wait_ge(S("V_ready"), 1)
            L0 = V[:, ROWS["lb0"][0]:ROWS["lb0"][0] + 32]
            L1 = V[:, ROWS["lb1"][0]:ROWS["lb1"][0] + 32]
            mxl = small[:, 192:224]
            do(X.tensor_tensor(mxl, L0, L1, ALU.max))
            do.settle()
            do(X.tensor_tensor(lb, L0, mxl, ALU.subtract), "lb_diff")
            do(X.tensor_tensor(oml, L1, mxl, ALU.subtract), "lb_diff")
            norm(0, 0, T, xT, lambda k: vcol("norm1", k), None, hh, hl)
            dve.wait_ge(S("lb_exp"), 1)
            do.settle()
            do(X.tensor_tensor(mxl, lb, oml, ALU.add))
            do.settle()
            do(X.reciprocal(mxl, mxl))
            do.settle()
            do(X.tensor_tensor(lb, lb, mxl, ALU.mult))
            do.settle()
            do(X.tensor_scalar(oml, lb, -1.0, 1.0, ALU.mult, ALU.add))

            do(X.memset(raw[:, :, 0:3], 0.0), "raw_zero")
            for t in range(12):
                dve.wait_ge(S(evac_name(t)), t // NLIN + 1)
                if t >= 2:
                    dve.wait_ge(S("silu_done"), t - 1)
                a, r = hf[:, t % 2, :], raw[:, t % 2, :]
                do(X.tensor_scalar(a, r[:, 0:T], vcol("conv", t), None, ALU.mult))
                for i in range(1, 4):
                    do.settle()
                    do(X.scalar_tensor_tensor(a, r[:, i:i + T], vcol("conv", 12 * i + t), a, ALU.mult, ALU.add),
                       "conv_done" if i == 3 else None)
            dve.wait_ge(S("ba_act"), 1)
            b3 = bank[3][:, 0:32].rearrange("p (a c) -> p a c", c=8)
            do(X.tensor_tensor(t2[:, 0:16].rearrange("p (a c) -> p a c", c=4), b3[:, :, 4:8],
                               view(ab, [[0, 4], [1, 4]], 4), ALU.add))
            do.settle()
            do(X.scalar_tensor_tensor(t2[:, 16:32], t2[:, 0:16], -1.0, t2[:, 0:16], ALU.mult, ALU.max), "sp_abs")
            dve.wait_ge(S("sp_ln"), 1)
            do.settle()
            do(X.scalar_tensor_tensor(t2[:, 16:32], t2[:, 0:16], 0.0, t2[:, 16:32], ALU.max, ALU.add))
            do.settle()
            do(X.scalar_tensor_tensor(ggc.rearrange("p (a c) -> p a c", c=4), t2[:, 16:32].rearrange("p (a c) -> p a c", c=4),
                                      -1.0, view(ab, [[0, 4], [1, 4]]), ALU.mult, ALU.mult), "g_ready")
            for i in range(8):
                dve.wait_ge(S("l2_rs"), i + 1)
                do(X.scalar_tensor_tensor(qkv[:, i, :], qkv[:, i, :], 128.0 ** -0.5 if i < 4 else 1.0, hf[:, i % 2, :],
                                          ALU.mult, ALU.mult), "l2_done")

            def back(n):
                w = (n % 4 + 1) * P
                dve.wait_ge(S("pexp"), n + 1)
                if n >= 2:
                    dve.wait_ge(S("pT_done"), n - 1)
                do.settle()
                do(X.tensor_tensor_reduce(pr[:, n % 2, 0:w], sm[:, n % 2, 0:w], dcnt[:, T - w:T], 1.0, 0.0, ALU.mult, ALU.add,
                                          den[:, n:n + 1]))
                do.settle()
                do(X.reciprocal(rden[:, n:n + 1], den[:, n:n + 1]))
                do.settle()
                do(X.tensor_scalar(pr[:, n % 2, 0:w], pr[:, n % 2, 0:w], rden[:, n:n + 1], None, ALU.mult), "p_ready")
            for n in range(4 * DH_N + 1):
                if n < 4 * DH_N:
                    w = (n % 4 + 1) * P
                    dve.wait_ge(S("s_done"), n + 1)
                    do.settle()
                    do(X.scalar_tensor_tensor(sm[:, n % 2, 0:w], bank[4 + n % 2][:, 0:w], 0.125, dneg[:, T - w:T],
                                              ALU.mult, ALU.add), "sm_ready")
                    do.settle()
                    do(X.tensor_reduce(mx[:, n:n + 1], sm[:, n % 2, 0:w], AX.X, ALU.max))
                    do.settle()
                    do(X.tensor_scalar(nmx[:, n:n + 1], mx[:, n:n + 1], -1.0, None, ALU.mult), "nmx_ready")
                if n:
                    back(n - 1)
                if n % 8 == 0 and n:
                    hp = n // 8 - 1
                    dve.wait_ge(S("ob_hi"), hp + 1)
                    do(X.tensor_tensor(gl[:, 4 + hp, :], bank[hp % 2][:], gh[:, 4 + hp, :].bitcast(F32), ALU.subtract), "ob_lo")

            dve.wait_ge(S("gcc_ready"), 1)
            dve.wait_ge(S("pT_ev"), 32)
            up = cst[:, 0:P]
            upb = view(up, [[0, 4], [1, P]])
            for c in range(TT):
                tok = slice(c * P, (c + 1) * P)
                if c:
                    dve.wait_ge(S("o_ev"), c)
                for h in range(4):
                    do(X.tensor_scalar(G["ug"][:, h, :], up, ggc[:, 4 * c + h:4 * c + h + 1], None, ALU.mult),
                       "ug" if h == 3 else None)
                dve.wait_ge(S("gr"), c + 1)
                for h in range(4):
                    do(X.tensor_scalar(G["ee"][:, h, :], bank[3][:, h * P:(h + 1) * P], gcc[:, 4 * c + h:4 * c + h + 1], 0.0,
                                       ALU.subtract, ALU.min))
                do(X.tensor_tensor(kec[:, 4 * c:4 * c + 4], view(bank[3][:, 0:1], [[P, 4]], P - 1), gcc[:, 4 * c:4 * c + 4],
                                   ALU.subtract), "dif")
                dve.wait_ge(S("eex"), c + 1)
                for h in range(4):
                    do(X.scalar_tensor_tensor(G["dt_"][:, h, :], G["ee"][:, h, :], beta[:, 4 * c + h:4 * c + h + 1], up,
                                              ALU.mult, ALU.mult))
                do(X.tensor_tensor(kec[:, 4 * c:4 * c + 4], kec[:, 4 * c:4 * c + 4], beta[:, 4 * c:4 * c + 4], ALU.mult))
                do.settle()
                dve.wait_ge(S("kk"), c + 1)
                b4, b5 = (bank[i][:].rearrange("p (h c) -> p h c", c=P) for i in (4, 5))
                do(X.tensor_tensor(G["lt"][:], G["dt_"][:], b4, ALU.mult))
                do(X.tensor_tensor(G["at_"][:], G["dt_"][:], b5, ALU.mult))
                do.settle()
                do(X.tensor_tensor(G["m0"][:], G["lt"][:], view(gmask[:, 0, :], [[0, 4], [1, P]]), ALU.mult))
                do.settle()
                do(X.tensor_tensor(G["xt"][:], view(ident[:], [[0, 4], [1, P]]), G["m0"][:], ALU.subtract), "x1")
                dve.wait_ge(S("vk"), c + 1)
                for h in range(4):
                    i = 4 * c + h
                    do(X.tensor_scalar(G["gk"][:, h, :], bank[7][:, h * P:(h + 1) * P], egc[:, i:i + 1], None, ALU.mult))
                    do(X.tensor_scalar(G["kend"][:, h, :], bank[7][:, h * P:(h + 1) * P], kec[:, i:i + 1], None, ALU.mult))
                do(X.tensor_copy(G["vtok"][:], bank[6][:].rearrange("p (h c) -> p h c", c=P)), "gkv")
                do(X.tensor_tensor(G["qdec"][:], qkv[:, 0:4, tok], G["eg"][:], ALU.mult))
                for l in range(1, 7):
                    do(X.tensor_tensor(G["m%d" % (l % 2)][:], G["lt"][:], view(gmask[:, l, :], [[0, 4], [1, P]]), ALU.mult), "m_rdy")
                    dve.wait_ge(S("XX"), 6 * c + l)
                    if l < 6:
                        if l == 1:
                            dve.wait_ge(S("x1e"), c + 1)
                        do(X.tensor_tensor(G["xx"][:], G["xx"][:], b4, ALU.subtract))
                    do(X.tensor_tensor(G["xt"][:], G["xt"][:], b5, ALU.subtract), "x_upd")
                if c == 0:
                    dve.wait_ge(S("uwe"), 1)
                    do(X.tensor_copy(G["u"][:], G["uv"][:]), "u")
                else:
                    dve.wait_ge(S("PS"), c)
                    do(X.tensor_tensor(G["u"][:], G["uv"][:], bank[3][:].rearrange("p (h c) -> p h c", c=P), ALU.subtract), "u")
                if c < TT - 1:
                    dve.wait_ge(S("ds"), c + 1)
                    if c == 0:
                        do(X.tensor_copy(G["st"][:], b5), "st_upd")
                    else:
                        for h in range(4):
                            do(X.scalar_tensor_tensor(G["st"][:, h, :], G["st"][:, h, :], G["eg"][:, h, P - 1:P],
                                                      bank[5][:, h * P:(h + 1) * P], ALU.mult, ALU.add),
                               "st_upd" if h == 3 else None)
            for i in range(8, 12):
                h = i - 8
                dve.wait_ge(S("l2_rs"), i + 1)
                do(X.scalar_tensor_tensor(oT[:, h, :], oT[:, h, :], vcol("gdn_norm"), hf[:, i % 2, :], ALU.mult, ALU.mult), "l2_done")
                do.settle()
                do(X.tensor_tensor(oT[:, h, :], oT[:, h, :], zT[:, h, :], ALU.mult), "oa")
            for h in range(4):
                dve.wait_ge(S("oa_hi"), h + 1)
                do(X.tensor_tensor(gl[:, h, :], oT[:, h, :], gh[:, h, :].bitcast(F32), ALU.subtract), "oa_lo")

            do(X.memset(fraw[:, :, 0:2], 0.0), "fraw_zero")
            for n in range(KT):
                residual(T_OUT + n, n)
            norm(1, 1, T, xT, lambda k: vcol("norm2", k), None, hh, hl)
            p = 0
            for r, (t0, t1_) in enumerate(ffn_tiles):
                for j in range(len(ROUND[r])):
                    for half in range(2):
                        t = t0 + 2 * j + half
                        jj = ROUND[r][j] + half * FT
                        dve.wait_ge(S(evac_name(t)), t // NLIN + 1)
                        i = 2 * (p % 2) + half
                        a, w = facc[:, i, :], fraw[:, i, :]
                        do(X.tensor_scalar(a, w[:, 0:T], vcol("ffn_conv", jj), None, ALU.mult))
                        for k in range(1, 3):
                            do.settle()
                            do(X.scalar_tensor_tensor(a, w[:, k:k + T], vcol("ffn_conv", 2 * FT * k + jj), a, ALU.mult, ALU.add),
                               "fconv" if k == 2 else None)
                    dve.wait_ge(S("fsilu"), p + 1)
                    do.settle()
                    do(X.tensor_tensor(a, a, fg[:, p % 2, :], ALU.mult), "fprod")
                    dve.wait_ge(S("fhi"), p + 1)
                    do(X.tensor_tensor(gl[:, j, :], a, gh[:, j, :].bitcast(F32), ALU.subtract), "flo")
                    p += 1
                for n in range(KT):
                    residual(t1_ + n, n)
            for s in range(2):
                do(X.tensor_tensor(ada[:, s::2], bank[7][:, s:96:2], V[:, ROWS["ada_b"][0]:ROWS["ada_b"][0] + 48], ALU.add))
            do.settle()
            for i, (l, s) in enumerate([(0, 0), (0, 1), (1, 0)]):
                g0 = ROWS["norm_g"][0] + 8 * l
                do(X.scalar_tensor_tensor(acoef[:, 8 * i:8 * i + 8], view(ada, [[2, 8]], (24 * l + 8) * 2 + s), 1.0, V[:, g0:g0 + 8],
                                          ALU.add, ALU.mult))

            def shift(l, s):
                return lambda k: ada[:, (24 * l + k) * 2 + s:(24 * l + k) * 2 + s + 1]

            def gate(l):
                return lambda k: ada[:, (24 * l + 16 + k) * 2:(24 * l + 16 + k) * 2 + 1]

            def coef(i):
                return lambda k: acoef[:, 8 * i + k:8 * i + k + 1]
            dve.wait_ge(S("rs_ready"), 3)
            for k in range(KT):
                do(X.scalar_tensor_tensor(xT[:, k, :], xT[:, k, :], vcol("final1", k), rs[:], ALU.mult, ALU.mult), "x1_norm")
            norm(3, 2, T, xT, coef(0), shift(0, 0), hh, hl)
            norm(4, 3, CT, craw, coef(1), shift(0, 1), ch, cl)

            do.settle()
            do(X.memset(qcx[:, 0, CT - 1:CT], 1.0))
            do(X.memset(qcx[:, 1, 0:1], 1.0))
            dve.wait_ge(S("hmask_in"), 16)

            def col(vec, dr, g):
                return vec[:, 16 * dr + g:16 * dr + g + 1]

            def context(g):
                dve.wait_ge(S("cevac"), 3 * g + 2)
                for dr in range(2):
                    do(X.tensor_scalar(sgc[:, dr, :], sgc[:, dr, :], col(oml, dr, g), col(lb, dr, g), ALU.mult, ALU.add))
                do.settle()
                if g:
                    dve.wait_ge(S("b6"), 4 * g - 2)
                do(X.tensor_scalar(kcx[:], sgc[:], -1.0, 1.0, ALU.mult, ALU.add))
                f0, f1, q0, q1 = sgc[:, 0, :], sgc[:, 1, :], qcx[:, 0, :], qcx[:, 1, :]
                r0 = view(f0[:, 0:1], [[-1, CT - 1]], CT - 1)
                do(X.tensor_tensor_scan(view(q0[:, 0:1], [[-1, CT - 1]], CT - 2), r0, r0, 1.0, ALU.mult, ALU.bypass))
                do(X.tensor_tensor_scan(q1[:, 1:CT], f1[:, 0:CT - 1], f1[:, 0:CT - 1], 1.0, ALU.mult, ALU.bypass))
                do.settle()
                do(X.tensor_tensor(kcx[:], kcx[:], qcx[:], ALU.mult), "kq_rdy")

            def start(g):
                dve.wait_ge(S(evac_name(T_HG + 5 * g + 2)), (T_HG + 5 * g + 2) // NLIN + 1)
                for dr in range(2):
                    do(X.tensor_scalar(PP[:, dr, :], sgf[:, dr, :], col(oml, dr, g), col(lb, dr, g), ALU.mult, ALU.add),
                       "sgf_used" if dr else None)
                if g:
                    dve.wait_ge(S("o_mm"), g)
                do(X.memset(QQ[:], 1.0))
                do.settle()
                do(X.tensor_scalar(KK[:], PP[:], -1.0, 1.0, ALU.mult, ALU.add))
                do.settle()

            def produce(g, pi, between=None):
                used = 11 * g + pi - 1 if pi >= 2 else (11 * g + (-1 if pi == 0 else 0) if g else 0)
                if used > 0:
                    dve.wait_ge(S("lv_mm"), used)
                kc, qc = KC[:, pi % 2, :], QC[:, pi % 2, :]
                q = qs[:, g % 2, :]
                if pi == 0:
                    do.settle()
                    do(X.tensor_tensor(kc, KK[:, 0, :], KK[:, 1, :], ALU.add))
                    do(X.tensor_copy(qc, q), "lv_rdy")
                    return
                n = LEVELS[pi - 1]
                nb = T // (2 * n)
                sel = [[2 * n, nb], [T + n, 2], [1, n]]
                flat = [[2 * n, nb], [n, 2], [1, n]]
                do.settle(1)
                do(X.tensor_tensor(view(kc[:, 0:1], flat), view(KK[:, 0, 0:1], sel), view(QQ[:, 0, 0:1], sel), ALU.mult))
                do.settle(1)
                do(X.tensor_tensor(view(qc[:, 0:1], flat), view(q[:, 0:1], flat),
                                   view(PP[:, 0, 0:1], [[2 * n, nb], [n - T, 2], [1, n]], T), ALU.mult), "lv_rdy")
                if pi < 9:
                    do.settle(1)
                    do(X.tensor_tensor(view(QQ[:, 0, 0:1], [[T + n, 2], [2 * n, nb], [1, n]]),
                                       view(QQ[:, 0, 0:1], [[T + n, 2], [2 * n, nb], [1, n]]),
                                       view(PP[:, 0, 0:1], [[T - 2 * n + 1, 2], [2 * n, nb], [0, n]], 2 * n - 1), ALU.mult))
                if between:
                    between()
                    do.settle(1)
                else:
                    do.settle()
                do(X.tensor_tensor(view(PP[:, 0, 0:1], [[T - n, 2], [2 * n, nb], [1, n]], n),
                                   view(PP[:, 0, 0:1], [[T - n, 2], [2 * n, nb], [1, n]], n),
                                   view(PP[:, 0, 0:1], [[T + 1, 2], [2 * n, nb], [0, n]], n - 1), ALU.mult))

            def take(g, li):
                dve.wait_ge(S("lv_mm"), 11 * g + li + 1)
                do(X.copy_predicated(view(MT[:, 0, 0:1], [[T + P, 4], [1, P]]), view(hmask[:, li, :], [[0, 4], [1, P]]),
                                     bank[4 + li % 2][:].rearrange("p (a c) -> p a c", c=P)),
                   "lv_ev%d" % (li % 2), (6 if li % 2 == 0 else 5) * g + li // 2 + 1)

            def silu(h, which, t, dst):
                i = t % NLIN
                dve.wait_ge(S("sg_q" if which == 0 else "sg_z"), h + 1)
                evac(t, X.tensor_tensor(dst, bank[i][:], sgt[:, which, :], ALU.mult))

            for h in range(HG + 1):
                t = T_HG + 5 * h
                g = h - 1
                if h:
                    context(g)
                    start(g)
                    produce(g, 0)
                    produce(g, 1)
                if h < HG:
                    silu(h, 0, t, qs[:, h % 2, :])
                    do(X.tensor_copy(small[:, 250:251], small[:, 0:1]), "sgt_q")
                if h:
                    for pi in range(2, 10):
                        produce(g, pi, (lambda li=pi - 2: take(g, li)))
                    do.settle()
                    for dr in range(2):
                        do(X.tensor_tensor(QQ[:, dr, :], qs[:, g % 2, :], PP[:, dr, :], ALU.mult), "qp_rdy" if dr else None)
                if h < HG:
                    silu(h, 1, t + 4, sz[:, h % 2, :])
                    do(X.tensor_copy(small[:, 251:252], small[:, 0:1]), "sz_rdy")
                if h:
                    dve.wait_ge(S("osq"), h)
                    y = yA[:, g, :] if g < 8 else yB[:, g - 8, :]
                    do(X.scalar_tensor_tensor(y, bank[6][:], vcol("hg_norm"), sz[:, g % 2, :], ALU.mult, ALU.mult), "y_pre")
            do.settle()
            for h in range(HG + 1):
                if h < HG:
                    y = yA[:, h, :] if h < 8 else yB[:, h - 8, :]
                    dve.wait_ge(S("rs_row"), h + 1)
                    do(X.tensor_tensor(y, y, bank[4 + h % 2][:], ALU.mult), "y_norm")
                if h:
                    g = h - 1
                    dve.wait_ge(S("y_hi"), h)
                    y = yA[:, g, :] if g < 8 else yB[:, g - 8, :]
                    hi_, lo_ = (hh[:, g, :], hl[:, g, :]) if g < 8 else (gh[:, g - 8, :], gl[:, g - 8, :])
                    do(X.tensor_tensor(lo_, y, hi_.bitcast(F32), ALU.subtract), "y_lo")
            for n in range(KT):
                residual(T_HO + n, n, gate(0))
            norm(5, 4, T, xT, coef(2), shift(1, 0), hh, hl)

            do(X.memset(AB[:, :, GDIM:GDIM + 1], 0.0), "ab_zero")
            do(X.memset(AB[:, :, GDIM + 128:GDIM + 129], 0.0), "ab_zero")
            for gi in range(GROUPS):
                t = ft_tiles[gi // 4] + 4 * (gi % 4)
                for c in range(2):
                    dve.wait_ge(S("zsg"), 2 * gi + c + 1)
                    evac(t + 2 + c, X.tensor_tensor(zs[:, c, :], bank[(t + 2 + c) % NLIN][:], zsg[:, c, :], ALU.mult))
                    do(X.tensor_copy(small[:, 250 + c:251 + c], small[:, 0:1]), "zs_rdy")
                for i in range(2):
                    dve.wait_ge(S("ab_mm"), gi + 1)
                    dve.wait_ge(S("ab_act"), 2 * gi + i + 1)
                    src, dst = bank[4 + i], AB[:, 2 * i, 0:1]
                    do(X.tensor_scalar(view(dst, [[T, 2], [1, 127]], GDIM + 129), view(src[:, 0:1], [[GDIM, 2], [-1, 127]], 255),
                                       -1.0, None, ALU.mult), "ab_ev")
                for g in range(2):
                    b, q, y = bank[6 + g], qsn[:, g, :], yf[:, g, :]
                    dve.wait_ge(S("qsn"), 2 * gi + g + 1)
                    do(X.tensor_tensor(y[:, 1:256], b[:, 1:256], q[:, 0:255], ALU.subtract))
                    do(X.tensor_tensor(y[:, 257:512], view(b[:, 0:1], [[-1, 255]], 255), view(q[:, 0:1], [[-1, 255]], 254), ALU.add),
                       "yf_rdy")
                    do(X.tensor_copy(y[:, 0:512:256], b[:, 0:512:256]), "y_ev")
                    do.settle()
                    if gi:
                        dve.wait_ge(S("yg_hi"), 2 * (gi - 1) + g + 1)
                    do(X.tensor_tensor(yg[:, g, :], y, zs[:, g, :], ALU.mult), "yg_rdy")
                for g in range(2):
                    k = 2 * (gi % 4) + g
                    dve.wait_ge(S("yg_hi"), 2 * gi + g + 1)
                    do(X.tensor_tensor(gl[:, k, :], yg[:, g, :], gh[:, k, :].bitcast(F32), ALU.subtract), "yg_lo")
                if gi % 4 == 3:
                    for n in range(KT):
                        residual(t + 4 + n, n, gate(1))
            dve.wait_ge(S("rs_ready"), 7)
            for k in range(KT):
                do(X.scalar_tensor_tensor(xT[:, k, :], xT[:, k, :], vcol("final_g", k), rs[:], ALU.mult, ALU.mult), "x_final")


ROWS_LOADED = 0
for _name, (_r, _n) in ROWS.items():
    ROWS_LOADED += 16 * ((_r + _n - 1) // P - _r // P + 1)

INPUTS = ["x", "norm1_w", "w_in", "conv_qkv_w", "a_log", "dt_bias", "gdn_norm_w", "w_out", "norm2_w", "w_up", "ffn_conv_w",
          "w_down", "final_norm_w", "c_2", "ctx_2", "c_ctx_2", "ada_w_2", "ada_b_2", "norm_g_2", "hg_w_in_2",
          "hg_lb_logits_2", "hg_norm_g_2", "hg_w_out_2", "ft_w_in_2", "ft_w_out_2", "final_g_2"]


def kernel(**inputs):
    import concourse.bacc as bacc
    from concourse.bass_utils import run_bass_kernel_spmd

    nc = bacc.Bacc("TRN2", target_bir_lowering=False, num_devices=1)
    arrays, aps = {}, {}
    for name in INPUTS:
        arrays[f"in_{name}"] = np.ascontiguousarray(inputs[name])
    for name, a in host_constants().items():
        arrays[f"const_{name}"] = a
    for name, a in arrays.items():
        aps[name.split("_", 1)[1]] = nc.dram_tensor(name, a.shape, mybir.dt.from_np(a.dtype), kind="ExternalInput").ap()
    out = nc.dram_tensor("out", (1, T, D), F32, kind="ExternalOutput").ap()
    build(nc, aps, out)
    r = run_bass_kernel_spmd(nc, [arrays], core_ids=[0])
    return r.results[0]["out"]
```

```python
from contextlib import ExitStack

import numpy as np

import concourse.bass as bass
from concourse import mybir

F32 = mybir.dt.float32
F32R = mybir.dt.float32r
U32 = mybir.dt.uint32
ALU = mybir.AluOpType
ACT = mybir.ActivationFunctionType
AX = mybir.AxisListType

P = 128
T = 512
TT = T // P
D = 1024
KT = D // P
GH_N, DH_N = 4, 8
GW, DW = 512, 512
O_Z, O_BA, O_B = 3 * GW, 4 * GW, 4 * GW + 2 * GH_N
FF = 2816
FT = FF // P
ROUND = [range(0, 8), range(8, 16), range(16, 22)]
HG = 16
E_IN = 2048
CT = 256
EPS = 1e-6
GROUPS, GDIM = 8, 256
NST, NSPLIT, NLIN = 4, 3, 3
LEVELS = [1, 2, 4, 8, 16, 32, 64, 128, 256]

ROWS = {}
_at = 0
for _name, _n in [("norm1", 8), ("norm2", 8), ("final1", 8), ("conv", 48), ("gdn_norm", 1),
                  ("hg_norm", 1), ("norm_g", 16), ("final_g", 8), ("lb0", 32), ("lb1", 32),
                  ("ada_b", 48), ("c", 8), ("c_ctx", 8), ("ffn_conv", 132)]:
    ROWS[_name] = (_at, _n)
    _at += _n
NROWS = _at
NV = 3 * P
assert NROWS <= NV


def modulated(i):
    return (0, 1) if i < 2 * KT else (0,)


def modulation_sums(i):
    return 2 * i if i < 2 * KT else i + 2 * KT


def host_constants():
    i = np.arange(P)
    ident = np.eye(P)
    upper = (i[:, None] <= i[None, :]) * 1.0
    lev = []
    for h in [1, 2, 4, 8, 16, 32, 64]:
        same = (i[:, None] // (2 * h)) == (i[None, :] // (2 * h))
        first, second = (i // h) % 2 == 0, (i // h) % 2 == 1
        lev.append((same & first[:, None] & second[None, :]) * 1.0)
    cnt = []
    for dist in [3, 2, 1, 0]:
        d = i[:, None] - i[None, :] + dist * P
        cnt.append(((d >= 0) & (d <= 128)) * 1.0 + ((d >= 0) & (d % 4 == 0)) + ((d >= 0) & (d % 16 == 0)))
    cnt = np.concatenate(cnt, 1)
    neg = np.where(cnt > 0, 0.0, -1e30)
    cf = np.concatenate([ident, upper] + lev + [cnt, neg], 1).astype(np.float32)
    m = [np.eye(P)]
    for h in [1, 2, 4, 8, 16, 32, 64]:
        same = (i[:, None] // (2 * h)) == (i[None, :] // (2 * h))
        m.append(same & ((i[:, None] // h) % 2 != (i[None, :] // h) % 2))
    hm = np.stack(m, 1).astype(np.uint32)
    c = np.arange(GDIM)
    g = np.arange(GDIM // 2 + 1)
    dch = np.concatenate([np.cos(2 * np.pi * np.outer(c, g) / GDIM),
                          np.sin(2 * np.pi * np.outer(c, g[1:-1]) / GDIM)], 1).astype(np.float32)
    t = np.arange(T)
    u = np.arange(T // 2 + 1)
    s = 1.0 / np.sqrt(T * GDIM)
    dtok = (s * np.concatenate([np.cos(2 * np.pi * (np.outer(t, u) % T) / T),
                                np.sin(2 * np.pi * (np.outer(t, u[1:-1]) % T) / T)], 1)).astype(np.float32)
    onecol = np.zeros((P, 31), np.float32)
    onecol[:, 15] = 1.0
    return {"cf": cf, "hm": hm, "dch": dch, "dtok": dtok, "onecol": onecol}


def make_units():
    units, tiles = [], []

    def add(w, rows, col, x, start=True, stop=True, ctx=False):
        if start:
            tiles.append([])
        tiles[-1].append(sum(u["lin"] for u in units))
        units.append(dict(w=w, rows=rows, col=col, x=x, start=start, stop=stop, lin=True,
                          tile=len(tiles) - 1, ctx=ctx))

    raws = [dict(w="ada_w", layer=l, rows=(0, 8), col=j * P, lin=False, raw=l * 24 + j)
            for l in range(2) for j in range(24)]

    for t in range(28):
        add("w_in", (0, 8), t * P if t < 16 else O_B + (t - 16) * P, "h")
    units.extend(raws)
    for n in range(KT):
        add("w_out", (0, 8), n * P, "g")
    for r in ROUND:
        for j in r:
            for half in range(2):
                add("w_up", (0, 8), half * FF + j * P, "h")
        for n in range(KT):
            add("w_down", (r[0], len(r)), n * P, "g")
    for hd in range(HG):
        for s in range(5):
            add("hg_w_in", (0, 8), s * E_IN + hd * P, "h", ctx=s in (1, 2, 3))
    for n in range(KT):
        add("hg_w_out", (0, 8), n * P, "h", stop=False)
        add("hg_w_out", (8, 8), n * P, "g", start=False)
    for half in range(2):
        for gi in range(4 * half, 4 * half + 4):
            for part in range(2):
                for c in range(2):
                    add("ft_w_in", (0, 8), part * E_IN + (2 * gi + c) * P, "h")
        for n in range(KT):
            add("ft_w_out", (8 * half, 8), n * P, "g")
    lin = 0
    seen = [0] * NST
    for n, u in enumerate(units):
        u["slot"], u["load"] = n % NST, n // NST
        if u["lin"]:
            u["lin_no"] = lin
            lin += 1
    return units, tiles


def view(ap, dims, off=0):
    return bass.AP(tensor=ap.tensor, offset=ap.offset + off, ap=[list(ap.ap[0])] + [list(x) for x in dims])


def build(nc, d, out, upto=99, debug=None):
    units, tiles = make_units()
    lin_units = [u for u in units if u["lin"]]
    n_lin = len(lin_units)
    ctx = ExitStack()
    with ctx:
        sems = {}

        def S(name):
            if name not in sems:
                sems[name] = ctx.enter_context(nc.semaphore("s_" + name))
            return sems[name]

        base = 16640
        assert nc.sbuf_base <= base

        def at(name, kib, shape, dt=F32):
            size = int(np.prod(shape[1:])) * 4
            assert base + kib * 1024 + size <= 229360, name
            return nc.alloc_sbuf_tensor_at(name, shape, dt, offset=int(base + kib * 1024))

        xT = at("xT", 0, [P, KT, T])
        stage = at("stage", 16, [P, NST, KT, P])
        wh = at("wh", 32, [P, NSPLIT, KT, P], F32R)
        wl = at("wl", 44, [P, NSPLIT, KT, P], F32R)
        hh = at("hh", 56, [P, KT, T], F32R)
        hl = at("hl", 72, [P, KT, T], F32R)
        gh = at("gh", 88, [P, KT, T], F32R)
        gl = at("gl", 104, [P, KT, T], F32R)
        V = at("V", 120, [P, NV])
        ident = at("ident", 121.5, [P, P])
        ones = at("ones", 122, [P, P])
        sq = at("sq", 122.5, [P, 2, T])
        hf = at("hf", 126.5, [P, 2, T])
        rs = at("rs", 130.5, [P, T])
        small = at("small", 132.5, [P, 256])
        A0 = 133.5
        zT = at("zT", A0, [P, 4, T])
        qkv = at("qkv", A0 + 8, [P, 12, T])
        xtok = at("xtok", A0 + 8, [P, TT, D])
        rowsT = at("rowsT", A0 + 24, [P, 3, P])
        bqkv = at("bqkv", A0 + 32, [P, 12, T])
        raw = at("raw", A0 + 56, [P, 2, T + 8])
        mprod = at("mprod", A0 + 56, [P, KT, P])
        mod = at("mod", A0 + 60.25, [P, 2, 2, P])
        cst = at("cst", A0 + 62.25, [P, 2 * P])
        gmask = at("gmask", A0 + 63.25, [P, 7, P])
        dcnt = at("dcnt", A0 + 66.75, [P, T])
        dneg = at("dneg", A0 + 68.75, [P, T])
        w8 = at("w8", A0 + 70.75, [P, KT, 8])
        gs = at("gs", A0 + 71, [P, 320])
        pT = at("pT", 32, [P, 2, TT, T])
        sm = at("sm", 48, [P, 2, T])
        pr = at("pr", 52, [P, 2, T])
        names = ["ee", "eg", "at_", "lt", "m0", "m1", "xx", "xt", "tt", "vtok", "gk", "kend", "u", "wkT", "qdec", "st"]
        G = {n: at("g_" + n, 56 + 2 * i, [P, 4, P]) for i, n in enumerate(names)}
        G["ug"] = G["tt"]
        oT = at("oT", 104, [P, 4, T])

        fraw = at("fraw", A0, [P, 4, T + 8])
        facc = at("facc", A0 + 9, [P, 4, T])
        fg = at("fg", A0 + 17, [P, 2, T])
        yA = at("yA", 88, [P, 8, T])
        yB = at("yB", A0, [P, 8, T])
        hmask = at("hmask", A0 + 16, [P, 8, P], U32)
        ch = at("ch", A0 + 20, [P, KT, CT], F32R)
        cl = at("cl", A0 + 28, [P, KT, CT], F32R)
        W0 = A0 + 36
        PP = at("PP", W0, [P, 2, T])
        QQ = at("QQ", W0 + 4, [P, 2, T])
        KK = at("KK", W0 + 8, [P, 2, T])
        KC = at("KC", W0 + 12, [P, 2, T])
        QC = at("QC", W0 + 16, [P, 2, T])
        qs = at("qs", W0 + 20, [P, 2, T])
        sz = at("sz", W0 + 24, [P, 2, T])
        sgt = at("sgt", W0 + 28, [P, 2, T])
        sgf = at("sgf", W0 + 32, [P, 2, T])
        MT = at("MT", 104, [P, TT, T])
        vT = at("vT", 112, [P, T])
        vt = at("vt", 114, [P, T])
        sgc = at("sgc", 116, [P, 2, CT])
        kcx = at("kcx", 118, [P, 2, CT])
        qcx = at("qcx", W0 + 36, [P, 2, CT])
        vcT = sq
        ctok = hf
        st2 = rs
        craw = at("craw", W0, [P, KT, CT])
        ctxtok = at("ctxtok", W0 + 8, [P, 2, D])
        dtok = at("dtok", A0, [P, TT, T])
        dch = at("dch", A0 + 8, [P, 2, GDIM])
        uT = at("uT", A0 + 10, [P, 2, T])
        zs = at("zs", A0 + 14, [P, 2, T])
        zsg = at("zsg", A0 + 18, [P, 2, T])
        AB = at("AB", A0 + 22, [P, TT, T])
        qsn = at("qsn", A0 + 30, [P, 2, T])
        yf = at("yf", A0 + 34, [P, 2, T])
        yg = at("yg", A0 + 38, [P, 2, T])
        otok = at("otok", A0 + 44, [P, TT, D])

        bank = [ctx.enter_context(nc.psum_tensor(f"bank{i}", [P, 512], F32)) for i in range(8)]

        def vcol(name, i=0):
            c = ROWS[name][0] + i
            return V[:, c:c + 1]

        halfeps = small[:, 0:1]
        onecol = small[:, 1:32]
        ada = small[:, 32:128]
        lb, oml = small[:, 128:160], small[:, 160:192]
        acoef = small[:, 192:240]
        beta, ggc, gcc, egc, kec = (gs[:, 16 * i:16 * i + 16] for i in range(5))
        ab = gs[:, 80:96]
        t1, t2 = gs[:, 96:128], gs[:, 128:160]
        mx, nmx, den, rden = gs[:, 160:192], gs[:, 192:224], gs[:, 224:256], gs[:, 256:288]
        silc = gs[:, 288:304]

        block = ctx.enter_context(nc.Block())

        def tile_last(t):
            return tiles[t][-1]

        FIRST = {}
        for t_no in range(len(tiles)):
            u = lin_units[tiles[t_no][0]]
            FIRST.setdefault(u["w"], t_no)
        T_OUT, T_UP, T_HG, T_HO, T_FT = FIRST["w_out"], FIRST["w_up"], FIRST["hg_w_in"], FIRST["hg_w_out"], FIRST["ft_w_in"]
        ffn_tiles = []
        t_no = T_UP
        for r in ROUND:
            ffn_tiles.append((t_no, t_no + 2 * len(r)))
            t_no += 2 * len(r) + KT
        ft_tiles = [T_FT, T_FT + 16 + KT]

        @block.sync
        def _(sp):
            sp.dma_start(xtok[:], d["x"][0].rearrange("(a p) c -> p a c", p=P)).then_inc(S("x_in"), 16)
            sp.dma_start(ident[:], d["cf"][:, 0:P]).then_inc(S("ident_in"), 16)

            def rows_in(name, src):
                r0, n = ROWS[name]
                done = 0
                while done < n:
                    a = r0 + done
                    k = min(n - done, P - a % P)
                    sp.dma_start(rowsT[a % P:a % P + k, a // P, :], src[done:done + k, :]).then_inc(S("rows_in"), 16)
                    rows_in.count += 16
                    done += k
            rows_in.count = 0
            rows_in("norm1", d["norm1_w"].rearrange("a (k p) -> (a k) p", p=P))
            rows_in("norm2", d["norm2_w"].rearrange("a (k p) -> (a k) p", p=P))
            rows_in("final1", d["final_norm_w"].rearrange("(k p) -> k p", p=P))
            rows_in("conv", d["conv_qkv_w"].rearrange("a i (k p) -> (a i k) p", p=P))
            rows_in("gdn_norm", d["gdn_norm_w"])
            rows_in("hg_norm", d["hg_norm_g_2"])
            rows_in("norm_g", d["norm_g_2"].rearrange("a (k p) -> (a k) p", p=P))
            rows_in("final_g", d["final_g_2"].rearrange("(k p) -> k p", p=P))
            lbl = d["hg_lb_logits_2"].rearrange("l s (k p) -> l (s k) p", p=P)
            rows_in("lb0", lbl[0])
            rows_in("lb1", lbl[1])
            rows_in("ada_b", d["ada_b_2"].rearrange("a (k p) -> (a k) p", p=P))
            rows_in("c", d["c_2"].rearrange("a (k p) -> (a k) p", p=P))
            rows_in("c_ctx", d["c_ctx_2"].rearrange("(k p) -> k p", p=P))
            rows_in("ffn_conv", d["ffn_conv_w"].rearrange("a i (k p) -> (a i k) p", p=P))
            assert rows_in.count == ROWS_LOADED
            sp.dma_start(cst[:, 0:P], d["cf"][:, P:2 * P]).then_inc(S("cst_in"), 16)
            sp.dma_start(gmask[:], d["cf"][:, 2 * P:9 * P].rearrange("p (l c) -> p l c", c=P)).then_inc(S("cst_in"), 16)
            sp.dma_start(dcnt[:], d["cf"][:, 9 * P:13 * P]).then_inc(S("cst_in"), 16)
            sp.dma_start(dneg[:], d["cf"][:, 13 * P:17 * P]).then_inc(S("cst_in"), 16)
            sp.dma_start(onecol, d["onecol"]).then_inc(S("cst_in"), 16)
            sp.dma_start(t1[0:1, 0:4], d["a_log"]).then_inc(S("cst_in"), 16)
            sp.dma_start(t1[0:1, 4:8], d["dt_bias"]).then_inc(S("cst_in"), 16)
            sp.dma_start(w8[:], d["w_in"][0, :, O_BA:O_BA + 8].rearrange("(k p) c -> p k c", p=P)).then_inc(S("cst_in"), 16)
            weights = {"w_in": d["w_in"][0], "w_out": d["w_out"][0], "w_up": d["w_up"][0], "w_down": d["w_down"][0],
                       "hg_w_in": d["hg_w_in_2"][0], "hg_w_out": d["hg_w_out_2"][0],
                       "ft_w_in": d["ft_w_in_2"][0], "ft_w_out": d["ft_w_out_2"][0]}
            for n, u in enumerate(units):
                w = d["ada_w_2"][u["layer"]] if u["w"] == "ada_w" else weights[u["w"]]
                k0, nk = u["rows"]
                if u["load"]:
                    sp.wait_ge(S(f"stage_free{u['slot']}"), u["load"])
                if u["lin"] and u["tile"] == T_HG and u["start"]:
                    sp.wait_ge(S("flo"), FT)
                    sp.dma_start(hmask[:], d["hm"]).then_inc(S("hmask_in"), 16)
                    sp.dma_start(ctxtok[:], d["ctx_2"][0].rearrange("(a p) c -> p a c", p=P)).then_inc(S("ctx_in"), 16)
                if u["lin"] and u["tile"] == T_FT and u["start"]:
                    sp.wait_ge(S("y_lo"), HG)
                    sp.dma_start(dtok[:], d["dtok"].rearrange("(a p) c -> p a c", p=P)).then_inc(S("dft_in"), 16)
                    sp.dma_start(dch[:], d["dch"].rearrange("(a p) c -> p a c", p=P)).then_inc(S("dft_in"), 16)
                sp.dma_start(stage[:, u["slot"], 0:nk, :],
                             w[k0 * P:(k0 + nk) * P, u["col"]:u["col"] + P].rearrange("(k p) c -> p k c", p=P)
                             ).then_inc(S(f"stage_in{u['slot']}"), 16)
            sp.wait_ge(S("out_ready"), 2 * TT)
            sp.dma_start(out[0].rearrange("(a p) c -> p a c", p=P), otok[:]).then_inc(S("stored"), 16)
            sp.wait_ge(S("stored"), 16)

        class Own:

            def __init__(self, eng, chain):
                self.eng, self.chain, self.n, self.past = eng, chain, {}, []

            def __call__(self, ins, name=None, value=None):
                name = name or self.chain
                self.n[name] = value or self.n.get(name, 0) + 1
                ins.then_inc(S(name), 1)
                self.past = self.past[-3:] + [(name, self.n[name])]

            def settle(self, back=0):
                name, value = self.past[-1 - back]
                self.eng.wait_ge(S(name), value)

        @block.gpsimd
        def _(pool):
            do = Own(pool, "pool_chain")
            for u in units:
                nk = u["rows"][1]
                if not u["lin"]:
                    i, vecs = u["raw"], modulated(u["raw"])
                    if i == 0:
                        pool.wait_ge(S("silc_ready"), 2)
                        pool.wait_ge(S("conv_done"), 12)
                    pool.wait_ge(S(f"stage_in{u['slot']}"), 16 * (u["load"] + 1))
                    for v in vecs:
                        n = modulation_sums(i) + v
                        if n:
                            do.settle()
                        end = v == vecs[-1]
                        do(nc.gpsimd.tensor_tensor(mprod[:], stage[:, u["slot"], :, :], view(silc[:, v:v + 1], [[2, KT], [0, P]]),
                                                   ALU.mult),
                           f"stage_free{u['slot']}" if end else None, u["load"] + 1 if end else None)
                        do.settle()
                        do(nc.gpsimd.tensor_tensor(mprod[:, 0:4, :], mprod[:, 0:4, :], mprod[:, 4:8, :], ALU.add))
                        if n >= 2:
                            pool.wait_ge(S("mod_mm"), n - 1)
                        do.settle()
                        do(nc.gpsimd.tensor_tensor(mod[:, n % 2, :, :], mprod[:, 0:2, :], mprod[:, 2:4, :], ALU.add), "mod_ready")
                    continue
                l = u["lin_no"]
                pool.wait_ge(S("hi_ready"), l + 1)
                pool.tensor_tensor(wl[:, l % NSPLIT, 0:nk, :], stage[:, u["slot"], 0:nk, :],
                                   wh[:, l % NSPLIT, 0:nk, :].bitcast(F32), ALU.subtract
                                   ).then_inc(S(f"stage_free{u['slot']}"), 1)

        def evac_name(t):
            return f"evac{t % NLIN}"

        @block.tensor
        def _(pe):
            pos = [0]

            def unit(u, first_x=None, between=iter(())):
                slot, nk = u["slot"], u["rows"][1]
                if not u["lin"]:
                    for v in modulated(u["raw"]):
                        n = modulation_sums(u["raw"]) + v
                        pe.wait_ge(S("mod_ready"), n + 1)
                        for k in range(2):
                            mm = pe.matmul(bank[7][:, 2 * u["raw"] + v:2 * u["raw"] + v + 1], mod[:, n % 2, k, :],
                                           ones[:, 0:1], start=(k == 0), stop=(k == 1))
                        mm.then_inc(S("mod_mm"), 1)
                    return
                l, t = u["lin_no"], u["tile"]
                xh, xl = (hh, hl) if u["x"] == "h" else (gh, gl)
                pe.wait_ge(S(f"stage_free{slot}"), u["load"] + 1)
                if u["start"] and t >= NLIN:
                    pe.wait_ge(S(evac_name(t)), t // NLIN)
                s = l % NSPLIT
                for k in range(nk):
                    if first_x:
                        pe.wait_ge(S(first_x[0]), first_x[1] + k + 1)
                    a, b = u["start"] and k == 0, u["stop"] and k == nk - 1
                    pe.matmul(bank[t % NLIN][:], wh[:, s, k, :], xh[:, k, :], start=a, stop=False)
                    pe.matmul(bank[t % NLIN][:], wh[:, s, k, :], xl[:, k, :], start=False, stop=False)
                    mm = pe.matmul(bank[t % NLIN][:], wl[:, s, k, :], xh[:, k, :], start=False, stop=b)
                    if k % 4 == 1:
                        next(between, None)
                if u["ctx"]:
                    next(between, None)
                    ci = 3 * ((t - T_HG) // 5) + (t - T_HG) % 5 - 1
                    half = [0, CT, 0][ci % 3]
                    if ci:
                        pe.wait_ge(S("cevac"), ci)
                    for k in range(nk):
                        a, b = k == 0, k == nk - 1
                        o = bank[7][:, half:half + CT]
                        pe.matmul(o, wh[:, s, k, :], ch[:, k, :], start=a, stop=False)
                        pe.matmul(o, wh[:, s, k, :], cl[:, k, :], start=False, stop=False)
                        mm = pe.matmul(o, wl[:, s, k, :], ch[:, k, :], start=False, stop=b)
                mm.then_inc(S("unit_done"), 1)

            def units_to(tile, first_x=None, between=iter(())):
                while True:
                    u = units[pos[0]]
                    unit(u, first_x, between)
                    first_x = None if u["lin"] else first_x
                    pos[0] += 1
                    if u["lin"] and u["tile"] == tile and u["stop"]:
                        break

            def norm_sum(n, width):
                for k in range(KT):
                    pe.wait_ge(S("sq_ready"), KT * n + k + 1)
                    pe.matmul(bank[3][:, 0:width], ones[:], sq[:, k % 2, 0:width], start=(k == 0), stop=(k == KT - 1)
                              ).then_inc(S("sq_used"), 1)

            def col_sum(i):
                pe.wait_ge(S("l2_sq"), i + 1)
                if i >= 2:
                    pe.wait_ge(S("l2_ln"), i - 1)
                pe.matmul(bank[4 + i % 2][:], ones[:], sq[:, i % 2, :], start=True, stop=True
                          ).then_inc(S("l2_sum"), 1)

            pe.wait_ge(S("ident_in"), 16)
            pe.wait_ge(S("rows_in"), ROWS_LOADED)
            for a in range(3):
                n = min(P, NROWS - a * P)
                mm = pe.transpose(bank[4][:, a * P:a * P + n], rowsT[0:n, a, :], ident[0:n, 0:n])
            mm.then_inc(S("rows_T"), 1)
            pe.wait_ge(S("x_in"), 16)
            for k in range(KT):
                if k >= 2:
                    pe.wait_ge(S("xT_ev"), k - 1)
                for a in range(TT):
                    mm = pe.transpose(bank[k % 2][:, a * P:(a + 1) * P], xtok[:, a, k * P:(k + 1) * P], ident[:])
                mm.then_inc(S("xT_ps"), 1)
            pe.wait_ge(S("const_set"), 2)
            norm_sum(0, T)
            units_to(27, ("h_ready", 0))
            pe.wait_ge(S("cst_in"), 8 * 16)
            for a in range(TT):
                for k in range(KT):
                    for part, xx_ in enumerate((hh, hl)):
                        pe.matmul(bank[3][:, a * 8:a * 8 + 8], xx_[:, k, a * P:(a + 1) * P].bitcast(F32), w8[:, k, :],
                                  start=(k == 0 and part == 0), stop=(k == KT - 1 and part == 1))
            pe.matmul(bank[3][:, 64:72], ones[0:1, :], t1[0:1, 0:8], start=True, stop=True).then_inc(S("ba_ready"), 1)
            for i in range(8):
                col_sum(i)

            for a in range(TT):
                if a == 0:
                    for t in (25, 26, 27):
                        pe.wait_ge(S(evac_name(t)), t // NLIN + 1)
                else:
                    pe.wait_ge(S("vb_ev"), a)
                for j in range(4):
                    mm = pe.transpose(bank[1][:, j * P:(j + 1) * P], bqkv[:, 8 + j, a * P:(a + 1) * P], ident[:])
                mm.then_inc(S("vb_T"), 1)

            def scores(n):
                h, i = n // 4, n % 4
                o = 64 * (h % 2)
                if n:
                    pe.wait_ge(S("sm_ready"), n)
                pe.matmul(bank[0][:, 0:(i + 1) * P], bqkv[o:o + 64, h // 2, i * P:(i + 1) * P],
                          bqkv[o:o + 64, 4 + h // 2, 0:(i + 1) * P], start=True, stop=True).then_inc(S("s_done"), 1)

            def turn(n):
                h, i = n // 4, n % 4
                pe.wait_ge(S("p_ready"), n + 1)
                if n:
                    pe.wait_ge(S("pT_ev"), n)
                else:
                    pe.wait_ge(S("vb_ev"), TT)
                for j in range(i + 1):
                    mm = pe.transpose(bank[1][:, j * P:(j + 1) * P], pr[:, n % 2, j * P:(j + 1) * P], ident[:])
                mm.then_inc(S("pT_done"), 1)

            def weigh(h):
                pe.wait_ge(S("pT_ev"), 4 * h + 4)
                if h % 2 == 0 and h >= 2:
                    pe.wait_ge(S("ob_lo"), h // 2)
                o = 64 * (h % 2)
                for j in range(TT):
                    mm = pe.matmul(bank[2][o:o + 64, j * P:T],
                                   bqkv[:, 8 + h // 2, j * P + 64 * (h % 2):j * P + 64 * (h % 2) + 64],
                                   pT[:, h % 2, j, j * P:T], start=(j == 0), stop=(j == TT - 1))
                mm.then_inc(S("pv_done"), 1)

            def modulation(n):
                for _ in range(n):
                    if not units[pos[0]]["lin"]:
                        unit(units[pos[0]])
                        pos[0] += 1

            def attention_tail(n):
                if n >= 1:
                    if n % 4 == 1 and n > 1:
                        weigh(n // 4 - 1)
                    turn(n - 1)

            scores(0)
            pe.wait_ge(S("g_ready"), 1)
            pe.matmul(bank[3][:, 80:96], cst[:, 0:P], ggc, start=True, stop=True).then_inc(S("gc_ps"), 1)
            for c in range(TT):
                tok = slice(c * P, (c + 1) * P)
                n = 8 * c
                pe.wait_ge(S("ug"), c + 1)
                for h in range(4):
                    mm = pe.matmul(bank[3][:, h * P:(h + 1) * P], ones[:], G["ug"][:, h, :], start=True, stop=True)
                mm.then_inc(S("gr"), 1)
                if c:
                    pe.wait_ge(S("o_ev"), c)
                    pe.wait_ge(S("st_upd"), c)
                else:
                    pe.wait_ge(S("l2_rs"), 8)
                    pe.wait_ge(S("l2_done"), 8)
                for h in range(4):
                    pe.matmul(bank[4][:, h * P:(h + 1) * P], qkv[:, 4 + h, tok], qkv[:, 4 + h, tok], start=True, stop=True)
                for h in range(4):
                    pe.matmul(bank[5][:, h * P:(h + 1) * P], qkv[:, 4 + h, tok], qkv[:, h, tok], start=True, stop=True)
                for h in range(4):
                    mm = pe.transpose(bank[6][:, h * P:(h + 1) * P], qkv[:, 8 + h, tok], ident[:])
                mm.then_inc(S("kk"), 1)
                attention_tail(n)
                pe.wait_ge(S("eex"), c + 1)
                for h in range(4):
                    mm = pe.transpose(bank[3][:, h * P:(h + 1) * P], qkv[:, 4 + h, tok], ident[:])
                mm.then_inc(S("vk"), 1)
                pe.wait_ge(S("x1"), c + 1)
                for h in range(4):
                    mm = pe.transpose(bank[4][:, h * P:(h + 1) * P], G["xt"][:, h, :], ident[:])
                mm.then_inc(S("x1T"), 1)
                scores(n + 1)
                modulation(1 if c < 2 else 2)
                for l in range(1, 7):
                    q = 6 * c + l
                    n = 8 * c + l
                    pe.wait_ge(S("m_rdy"), q)
                    if l == 1:
                        pe.wait_ge(S("x1e"), c + 1)
                        pe.wait_ge(S("gkv"), c + 1)
                    else:
                        pe.wait_ge(S("x_upd"), q - 1)
                    for h in range(4):
                        mm = pe.matmul(bank[3][:, h * P:(h + 1) * P], G["m%d" % (l % 2)][:, h, :], G["xx"][:, h, :],
                                       start=True, stop=True)
                    mm.then_inc(S("T"), 1)
                    attention_tail(n)
                    pe.wait_ge(S("Te"), q)
                    if l < 6:
                        for h in range(4):
                            pe.matmul(bank[4][:, h * P:(h + 1) * P], G["xt"][:, h, :], G["tt"][:, h, :], start=True, stop=True)
                    for h in range(4):
                        mm = pe.matmul(bank[5][:, h * P:(h + 1) * P], G["tt"][:, h, :], G["xt"][:, h, :], start=True, stop=True)
                    mm.then_inc(S("XX"), 1)
                    scores(n + 1)
                    modulation(1 if c < 2 else 2)
                n = 8 * c + 7
                pe.wait_ge(S("x_upd"), 6 * c + 6)
                for h in range(4):
                    pe.matmul(bank[6][:, h * P:(h + 1) * P], G["xt"][:, h, :], G["vtok"][:, h, :], start=True, stop=True)
                for h in range(4):
                    mm = pe.matmul(bank[5][:, h * P:(h + 1) * P], G["gk"][:, h, :], G["xt"][:, h, :], start=True, stop=True)
                mm.then_inc(S("uw"), 1)
                attention_tail(n)
                pe.wait_ge(S("uwe"), c + 1)
                if c:
                    for h in range(4):
                        mm = pe.matmul(bank[3][:, h * P:(h + 1) * P], G["wkT"][:, h, :], G["st"][:, h, :], start=True, stop=True)
                    mm.then_inc(S("PS"), 1)
                pe.wait_ge(S("u"), c + 1)
                for h in range(4):
                    o = bank[4][:, h * P:(h + 1) * P]
                    if c:
                        pe.matmul(o, G["st"][:, h, :], G["qdec"][:, h, :], start=True, stop=False)
                    mm = pe.matmul(o, G["u"][:, h, :], G["at_"][:, h, :], start=(c == 0), stop=True)
                mm.then_inc(S("o"), 1)
                if c < TT - 1:
                    for h in range(4):
                        mm = pe.matmul(bank[5][:, h * P:(h + 1) * P], G["kend"][:, h, :], G["u"][:, h, :], start=True, stop=True)
                    mm.then_inc(S("ds"), 1)
                if c < TT - 1:
                    scores(n + 1)
                modulation(1 if c < 2 else 2)
            attention_tail(32)
            weigh(7)
            assert units[pos[0]]["lin"]
            pe.wait_ge(S("o_ev"), TT)
            for i in range(8, 12):
                col_sum(i)

            pe.wait_ge(S("oa_lo"), 4)
            pe.wait_ge(S("ob_lo"), 4)
            units_to(T_OUT + KT - 1)
            norm_sum(1, T)
            pairs = 0
            for r, (t0, t1_) in enumerate(ffn_tiles):
                units_to(t1_ - 1, ("h_ready", KT) if r == 0 else None)
                units_to(t1_ + KT - 1, ("flo", pairs))
                pairs += len(ROUND[r])
            norm_sum(2, T)
            norm_sum(3, T)
            pe.wait_ge(S("ctx_in"), 16)
            for k in range(KT):
                if k >= 2:
                    pe.wait_ge(S("cx_ev"), k - 1)
                for a in range(2):
                    mm = pe.transpose(bank[4 + k % 2][:, a * P:(a + 1) * P], ctxtok[:, a, k * P:(k + 1) * P], ident[:])
                mm.then_inc(S("cx_T"), 1)
            norm_sum(4, CT)

            def turn_values(h):
                tv = T_HG + 5 * h + 3
                pe.wait_ge(S(evac_name(tv)), tv // NLIN + 1)
                if h:
                    pe.wait_ge(S("osq"), h)
                    pe.wait_ge(S("y_pre"), h)
                for a in range(TT):
                    mm = pe.transpose(bank[6][:, a * P:(a + 1) * P], vT[:, a * P:(a + 1) * P], ident[:])
                mm.then_inc(S("b6"), 1)
                yield
                pe.wait_ge(S("kq_rdy"), h + 1)
                pe.wait_ge(S("b6e"), 4 * h + 1)
                for a in range(4):
                    mm = pe.transpose(bank[6][:, a * P:(a + 1) * P], kcx[:, a // 2, (a % 2) * P:(a % 2 + 1) * P], ident[:])
                mm.then_inc(S("b6"), 1)
                yield
                pe.wait_ge(S("b6e"), 4 * h + 2)
                for a in range(2):
                    mm = pe.transpose(bank[6][:, a * P:(a + 1) * P], vcT[:, 0, a * P:(a + 1) * P], ident[:])
                mm.then_inc(S("b6"), 1)
                yield
                pe.wait_ge(S("b6e"), 4 * h + 3)
                for dr in range(2):
                    for a in range(2):
                        mm = pe.matmul(bank[6][:, dr * P:(dr + 1) * P], ctok[:, 0, (2 * dr + a) * P:(2 * dr + a + 1) * P],
                                       st2[:, CT + a * P:CT + (a + 1) * P], start=(a == 0), stop=(a == 1))
                mm.then_inc(S("b6"), 1)

            def level(h, li):
                prod = min(li, 9)
                pe.wait_ge(S("lv_rdy"), 10 * h + prod + 1)
                if 11 * h + li >= 2:
                    pe.wait_ge(S("lv_ev%d" % (li % 2)), (6 if li % 2 == 0 else 5) * h + li // 2)
                b = bank[4 + li % 2]
                kc, qc = KC[:, prod % 2, :], QC[:, prod % 2, :]
                if li <= 7:
                    for a in range(TT):
                        mm = pe.matmul(b[:, a * P:(a + 1) * P], kc[:, a * P:(a + 1) * P], qc[:, a * P:(a + 1) * P],
                                       start=True, stop=True)
                elif li == 8:
                    for a in range(TT):
                        o = a ^ 1
                        mm = pe.matmul(b[:, a * P:(a + 1) * P], kc[:, a * P:(a + 1) * P], qc[:, o * P:(o + 1) * P],
                                       start=True, stop=True)
                else:
                    for i in range(2):
                        a = 2 * (li - 9) + i
                        o = 256 * (1 - a // 2)
                        mm = pe.matmul(b[:, i * 256:(i + 1) * 256], kc[:, a * P:(a + 1) * P], qc[:, o:o + 256],
                                       start=True, stop=True)
                mm.then_inc(S("lv_mm"), 1)

            def output(h):
                pe.wait_ge(S("b6e"), 4 * h + 4)
                pe.wait_ge(S("lv_ev0"), 6 * h + 6)
                pe.wait_ge(S("lv_ev1"), 5 * h + 5)
                pe.wait_ge(S("qp_rdy"), h + 1)
                for a in range(TT):
                    pe.matmul(bank[6][:], vt[:, a * P:(a + 1) * P], MT[:, a, :], start=(a == 0), stop=False)
                for dr in range(2):
                    mm = pe.matmul(bank[6][:], st2[:, dr * P:(dr + 1) * P], QQ[:, dr, :], start=False, stop=(dr == 1))
                mm.then_inc(S("o_mm"), 1)

            def meansq(h):
                pe.wait_ge(S("osq"), h + 1)
                pe.matmul(bank[3][0:HG, :], onecol[:, 15 - h:31 - h], vcT[:, 1, :], start=(h == 0), stop=(h == HG - 1)
                          ).then_inc(S("ms_mm"), 1)

            def scan(g):
                if g >= 1:
                    meansq(g - 1)
                yield from turn_values(g)
                for li in range(11):
                    level(g, li)
                    yield
                output(g)
                yield

            for h in range(HG + 1):
                steps = scan(h - 1) if h else iter(())
                if h < HG:
                    t = T_HG + 5 * h
                    units_to(t, ("h_ready", 2 * KT) if h == 0 else None)
                    if h == 0:
                        pe.wait_ge(S("h_ready"), 4 * KT)
                    for i in range(1, 5):
                        next(steps, None)
                        units_to(t + i, None, steps)
                for _ in steps:
                    pass
            meansq(HG - 1)
            pe.wait_ge(S("rs16"), 1)
            for h in range(HG):
                if h >= 2:
                    pe.wait_ge(S("y_norm"), h - 1)
                pe.matmul(bank[4 + h % 2][:], bass.AP(tensor=ident[:].tensor, offset=h, ap=[[P, HG], [0, P]]),
                          rs[0:HG, :], start=True, stop=True).then_inc(S("rs_row"), 1)
            pe.wait_ge(S("y_lo"), HG)
            units_to(T_HO + KT - 1)
            norm_sum(5, T)

            for gi in range(GROUPS):
                t = ft_tiles[gi // 4] + 4 * (gi % 4)
                units_to(t + 1, ("h_ready", 4 * KT) if gi == 0 else None)
                units_to(t + 3)
                pe.wait_ge(S(evac_name(t + 1)), (t + 1) // NLIN + 1)
                pe.wait_ge(S("dft_in"), 32)
                if gi:
                    pe.wait_ge(S("ab_ev"), 2 * gi)
                for a in range(TT):
                    for c in range(2):
                        mm = pe.matmul(bank[4 + a // 2][:, (a % 2) * GDIM:(a % 2 + 1) * GDIM], uT[:, c, a * P:(a + 1) * P],
                                       dch[:, c, :], start=(c == 0), stop=(c == 1))
                mm.then_inc(S("ab_mm"), 1)
                pe.wait_ge(S("ab_ev"), 2 * gi + 2)
                for g in range(2):
                    if gi:
                        pe.wait_ge(S("y_ev"), 2 * (gi - 1) + g + 1)
                    b = bank[6 + g]
                    for a in range(TT):
                        pe.matmul(b[:, 0:257], AB[:, a, g * P:(g + 1) * P], dtok[:, a, 0:257], start=(a == 0), stop=(a == TT - 1))
                    for a in range(TT):
                        mm = pe.matmul(b[:, 257:512], AB[:, a, GDIM + g * P:GDIM + (g + 1) * P], dtok[:, a, 257:512],
                                       start=(a == 0), stop=(a == TT - 1))
                    mm.then_inc(S("y_mm"), 1)
                if gi % 4 == 3:
                    pe.wait_ge(S("yg_lo"), 2 * gi + 2)
                    units_to(t + 4 + KT - 1)
            assert pos[0] == len(units)
            norm_sum(6, T)
            pe.wait_ge(S("x_final"), KT)
            for a in range(TT):
                for half in range(2):
                    i = 2 * a + half
                    if i >= 2:
                        pe.wait_ge(S("out_ready"), i - 1)
                    for k in range(4):
                        mm = pe.transpose(bank[4 + i % 2][:, k * P:(k + 1) * P],
                                          xT[:, 4 * half + k, a * P:(a + 1) * P], ident[:])
                    mm.then_inc(S("out_ps"), 1)

        @block.scalar
        def _(act):
            do = Own(act, "act_chain")
            A = nc.scalar

            def high(l):
                if l >= n_lin:
                    return
                u = lin_units[l]
                act.wait_ge(S(f"stage_in{u['slot']}"), 16 * (u["load"] + 1))
                if l >= NSPLIT:
                    act.wait_ge(S("unit_done"), l - NSPLIT + 1)
                nk = u["rows"][1]
                do(A.activation(wh[:, l % NSPLIT, 0:nk, :], stage[:, u["slot"], 0:nk, :], ACT.Copy), "hi_ready")

            def finish_tile(t):
                for l in tiles[t]:
                    if l + NSPLIT < tiles[T_OUT][0] or l >= tiles[T_OUT][0]:
                        high(l + NSPLIT)
                act.wait_ge(S("unit_done"), tile_last(t) + 1)

            def evac(t, ins):
                do(ins, evac_name(t), t // NLIN + 1)

            def norm(n, width, src, ready):
                for k in range(KT):
                    if k >= 2 or n:
                        act.wait_ge(S("sq_used"), KT * n + k - 1)
                    act.wait_ge(S(ready[0]), ready[1] + (k + 1 if ready[2] else 0))
                    do(A.activation(sq[:, k % 2, 0:width], src[:, k, :], ACT.Square), "sq_ready")
                act.wait_ge(S("sq_used"), KT * n + KT)
                do(A.activation(rs[:, 0:width], bank[3][:, 0:width], ACT.Ln, scale=1.0 / D, bias=halfeps))
                do.settle()
                do(A.activation(rs[:, 0:width], rs[:, 0:width], ACT.Exp, scale=-0.5), "rs_ready")

            def split_high(m, dst, width):
                for k in range(KT):
                    act.wait_ge(S("hf_ready"), KT * m + k + 1)
                    do(A.activation(dst[:, k, :], hf[:, k % 2, 0:width], ACT.Copy), "hh_ready")

            def col_roots(i, eps_scale, between):
                for n in (i, i + 1):
                    act.wait_ge(S("l2_sum"), n + 1)
                    if n >= 2:
                        act.wait_ge(S("l2_done"), n - 1)
                    do(A.activation(hf[:, n % 2, :], bank[4 + n % 2][:], ACT.Ln, scale=eps_scale, bias=halfeps), "l2_ln")
                between()
                for n in (i, i + 1):
                    act.wait_ge(S("l2_ln"), n + 1)
                    do(A.activation(hf[:, n % 2, :], hf[:, n % 2, :], ACT.Exp, scale=-0.5), "l2_rs")

            def col_square(i, src):
                if i >= 2:
                    act.wait_ge(S("l2_sum"), i - 1)
                do(A.activation(sq[:, i % 2, :], src, ACT.Square), "l2_sq")

            act.wait_ge(S("rows_T"), 1)
            do(A.activation(V[:, 0:NROWS], bank[4][:, 0:NROWS], ACT.Copy), "V_ready")
            do.settle()
            act.wait_ge(S("const_set"), 2)
            norm(0, T, xT, ("xT_ev", 0, True))
            split_high(0, hh, T)
            for l in range(NSPLIT):
                high(l)
            act.wait_ge(S("lb_diff"), 2)
            do(A.activation(lb, lb, ACT.Exp))
            do(A.activation(oml, oml, ACT.Exp), "lb_exp")

            def silu_conv(t):
                act.wait_ge(S("conv_done"), t + 1)
                do(A.activation(qkv[:, t, :], hf[:, t % 2, :], ACT.Silu), "silu_done")
            do(A.activation(silc[:, 0:16:2], V[:, ROWS["c"][0]:ROWS["c"][0] + 8], ACT.Silu), "silc_ready")
            do(A.activation(silc[:, 1:16:2], V[:, ROWS["c_ctx"][0]:ROWS["c_ctx"][0] + 8], ACT.Silu), "silc_ready")
            for t in range(28):
                finish_tile(t)
                if t < 12:
                    if t == 0:
                        act.wait_ge(S("raw_zero"), 1)
                    if t >= 2:
                        act.wait_ge(S("conv_done"), t - 1)
                    evac(t, A.activation(raw[:, t % 2, 3:3 + T], bank[t % NLIN][:], ACT.Copy))
                elif t < 16:
                    evac(t, A.activation(zT[:, t - 12, :], bank[t % NLIN][:], ACT.Silu))
                else:
                    evac(t, A.activation(bqkv[:, t - 16, :], bank[t % NLIN][:], ACT.Copy))
                if 1 <= t <= 12:
                    silu_conv(t - 1)
            act.wait_ge(S("ba_ready"), 1)
            b3 = bank[3][:, 0:32].rearrange("p (a c) -> p a c", c=8)
            do(A.activation(beta.rearrange("p (a c) -> p a c", c=4), b3[:, :, 0:4], ACT.Sigmoid))
            do(A.activation(ab[:, 4:8], bank[3][:, 68:72], ACT.Copy))
            do(A.activation(ab[:, 0:4], bank[3][:, 64:68], ACT.Exp), "ba_act")
            act.wait_ge(S("sp_abs"), 1)
            do(A.activation(t2[:, 16:32], t2[:, 16:32], ACT.Exp, scale=-1.0))
            do.settle()
            do(A.activation(t2[:, 16:32], t2[:, 16:32], ACT.Ln, bias=1.0), "sp_ln")
            def square_pair(i, last):
                if i < last:
                    for n in (i, i + 1):
                        col_square(n, qkv[:, n, :] if n < 8 else oT[:, n - 8, :])
            square_pair(0, 8)
            for i in range(0, 8, 2):
                col_roots(i, 1.0, lambda: square_pair(i + 2, 8))

            for a in range(TT):
                act.wait_ge(S("vb_T"), a + 1)
                do(A.activation(bqkv[:, 8:12, a * P:(a + 1) * P], bank[1][:].rearrange("p (j c) -> p j c", c=P), ACT.Copy), "vb_ev")

            def weights(n):
                w = (n % 4 + 1) * P
                act.wait_ge(S("nmx_ready"), n + 1)
                do(A.activation(sm[:, n % 2, 0:w], sm[:, n % 2, 0:w], ACT.Exp, bias=nmx[:, n:n + 1]), "pexp")

            def place(n):
                h, i = n // 4, n % 4
                act.wait_ge(S("pT_done"), n + 1)
                if h >= 2:
                    act.wait_ge(S("pv_done"), h - 1)
                do(A.activation(pT[:, h % 2, 0:i + 1, i * P:(i + 1) * P],
                                bank[1][:, 0:(i + 1) * P].rearrange("p (j c) -> p j c", c=P), ACT.Copy), "pT_ev")

            def attention_tail(n):
                if n > 8 and n % 8 == 1:
                    pair_high(n // 8 - 1)
                if n:
                    place(n - 1)

            def pair_high(hp):
                act.wait_ge(S("pv_done"), 2 * hp + 2)
                do(A.activation(gh[:, 4 + hp, :], bank[2][:], ACT.Copy), "ob_hi")

            def heads4(b):
                return b[:].rearrange("p (h c) -> p h c", c=P)

            act.wait_ge(S("gc_ps"), 1)
            do(A.activation(gcc, bank[3][:, 80:96], ACT.Copy))
            do(A.activation(egc, bank[3][:, 80:96], ACT.Exp), "gcc_ready")
            for c in range(TT):
                tok = slice(c * P, (c + 1) * P)
                act.wait_ge(S("dif"), c + 1)
                do(A.activation(G["ee"][:], G["ee"][:], ACT.Exp))
                do(A.activation(G["eg"][:], heads4(bank[3]), ACT.Exp))
                do(A.activation(kec[:, 4 * c:4 * c + 4], kec[:, 4 * c:4 * c + 4], ACT.Exp), "eex")
                attention_tail(8 * c)
                weights(8 * c)
                act.wait_ge(S("x1T"), c + 1)
                do(A.activation(G["xx"][:], heads4(bank[4]), ACT.Copy), "x1e")
                for l in range(1, 7):
                    act.wait_ge(S("T"), 6 * c + l)
                    do(A.activation(G["tt"][:], heads4(bank[3]), ACT.Copy), "Te")
                    attention_tail(8 * c + l)
                    weights(8 * c + l)
                act.wait_ge(S("uw"), c + 1)
                do(A.activation(G["u"][:], heads4(bank[6]), ACT.Copy))
                do(A.activation(G["wkT"][:], heads4(bank[5]), ACT.Copy), "uwe")
                attention_tail(8 * c + 7)
                weights(8 * c + 7)
                act.wait_ge(S("o"), c + 1)
                do(A.activation(oT[:, :, tok], heads4(bank[4]), ACT.Copy), "o_ev")
            attention_tail(32)
            pair_high(3)
            for l in range(tiles[T_OUT][0], tiles[T_OUT][0] + NSPLIT):
                high(l)
            do.settle()
            square_pair(8, 12)
            for i in range(8, 12, 2):
                col_roots(i, 1.0 / P, lambda: square_pair(i + 2, 12))
            for h in range(4):
                act.wait_ge(S("oa"), h + 1)
                do(A.activation(gh[:, h, :], oT[:, h, :], ACT.Copy), "oa_hi")

            for n in range(KT):
                finish_tile(T_OUT + n)
            norm(1, T, xT, (evac_name(T_OUT + KT - 1), (T_OUT + KT - 1) // NLIN + 1, False))
            split_high(1, hh, T)
            p = 0
            for r, (t0, t1_) in enumerate(ffn_tiles):
                for j in range(len(ROUND[r])):
                    for half in range(2):
                        t = t0 + 2 * j + half
                        finish_tile(t)
                        if p == 0:
                            act.wait_ge(S("fraw_zero"), 1)
                        if p >= 2:
                            act.wait_ge(S("fconv"), 2 * p - 2)
                        evac(t, A.activation(fraw[:, 2 * (p % 2) + half, 2:2 + T], bank[t % NLIN][:], ACT.Copy))
                    act.wait_ge(S("fconv"), 2 * p + 1)
                    do(A.activation(fg[:, p % 2, :], facc[:, 2 * (p % 2), :], ACT.Silu), "fsilu")
                    act.wait_ge(S("fprod"), p + 1)
                    do(A.activation(gh[:, j, :], facc[:, 2 * (p % 2) + 1, :], ACT.Copy), "fhi")
                    p += 1
                for n in range(KT):
                    finish_tile(t1_ + n)
            last = T_HG - 1
            norm(2, T, xT, (evac_name(last), last // NLIN + 1, False))
            norm(3, T, xT, ("x1_norm", 0, True))
            split_high(2, hh, T)
            for k in range(KT):
                act.wait_ge(S("cx_T"), k + 1)
                do(A.activation(craw[:, k, :], bank[4 + k % 2][:, 0:CT], ACT.Copy), "cx_ev")
            norm(4, CT, craw, ("cx_ev", 0, True))
            split_high(3, ch, CT)

            def aux_early(g):
                act.wait_ge(S("b6"), 4 * g + 1)
                do(A.activation(vt[:], bank[6][:], ACT.Copy), "b6e")
                act.wait_ge(S("b6"), 4 * g + 2)
                do(A.activation(ctok[:, 0, :], bank[6][:], ACT.Copy), "b6e")
                act.wait_ge(S("b6"), 4 * g + 3)
                do(A.activation(st2[:, CT:2 * CT], bank[6][:, 0:CT], ACT.Copy), "b6e")

            def aux_states(g):
                act.wait_ge(S("b6"), 4 * g + 4)
                do(A.activation(st2[:, 0:CT], bank[6][:, 0:CT], ACT.Copy), "b6e")

            def place_level(g, li):
                act.wait_ge(S("lv_mm"), 11 * g + li + 1)
                b = bank[4 + li % 2]
                if li == 8:
                    src = view(b[:], [[2 * P, 2], [P, 2], [1, P]])
                    dst = view(MT[:, 0, 0:1], [[2 * T + 2 * P, 2], [T - P, 2], [1, P]], P)
                else:
                    a = 2 * (li - 9)
                    src = b[:].rearrange("p (i c) -> p i c", i=2)
                    dst = MT[:, a:a + 2, 256 * (10 - li):256 * (10 - li) + 256]
                do(A.activation(dst, src, ACT.Copy), "lv_ev%d" % (li % 2), (6 if li % 2 == 0 else 5) * g + li // 2 + 1)

            for h in range(HG + 1):
                t = T_HG + 5 * h
                if h < HG:
                    finish_tile(t)
                    if h:
                        act.wait_ge(S("sgt_q"), h)
                    do(A.activation(sgt[:, 0, :], bank[t % NLIN][:], ACT.Sigmoid), "sg_q")
                if h:
                    aux_early(h - 1)
                if h == HG:
                    aux_states(h - 1)
                if h < HG:
                    for dr in range(2):
                        finish_tile(t + 1 + dr)
                        if h:
                            act.wait_ge(S("sgf_used"), h)
                            act.wait_ge(S("kq_rdy"), h)
                        do(A.activation(sgc[:, dr, :], bank[7][:, dr * CT:(dr + 1) * CT], ACT.Sigmoid), "cevac")
                        evac(t + 1 + dr, A.activation(sgf[:, dr, :], bank[(t + 1 + dr) % NLIN][:], ACT.Sigmoid))
                        if h and dr == 0:
                            aux_states(h - 1)
                    finish_tile(t + 3)
                    if h:
                        act.wait_ge(S("b6"), 4 * h)
                    do(A.activation(vcT[:, 0, 0:CT], bank[7][:, 0:CT], ACT.Copy), "cevac")
                    do(A.activation(vT[:], bank[(t + 3) % NLIN][:], ACT.Copy), evac_name(t + 3), (t + 3) // NLIN + 1)
                if h:
                    place_level(h - 1, 8)
                if h:
                    place_level(h - 1, 9)
                    place_level(h - 1, 10)
                if h < HG:
                    finish_tile(t + 4)
                    if h:
                        act.wait_ge(S("sz_rdy"), h)
                    do(A.activation(sgt[:, 1, :], bank[(t + 4) % NLIN][:], ACT.Sigmoid), "sg_z")
                if h:
                    act.wait_ge(S("o_mm"), h)
                    if h >= 2:
                        act.wait_ge(S("ms_mm"), h - 1)
                    do(A.activation(vcT[:, 1, :], bank[6][:], ACT.Square), "osq")
            act.wait_ge(S("ms_mm"), HG)
            do(A.activation(rs[0:HG, :], bank[3][0:HG, :], ACT.Ln, scale=1.0 / P, bias=halfeps[0:HG, :]))
            do.settle()
            do(A.activation(rs[0:HG, :], rs[0:HG, :], ACT.Exp, scale=-0.5), "rs16")
            for h in range(HG):
                act.wait_ge(S("y_norm"), h + 1)
                src = yA[:, h, :] if h < 8 else yB[:, h - 8, :]
                dst = hh[:, h, :] if h < 8 else gh[:, h - 8, :]
                do(A.activation(dst, src, ACT.Copy), "y_hi")
            for n in range(KT):
                finish_tile(T_HO + n)
            norm(5, T, xT, (evac_name(T_HO + KT - 1), (T_HO + KT - 1) // NLIN + 1, False))
            split_high(4, hh, T)

            for gi in range(GROUPS):
                t = ft_tiles[gi // 4] + 4 * (gi % 4)
                for c in range(2):
                    finish_tile(t + c)
                    if gi:
                        act.wait_ge(S("ab_mm"), gi)
                    do(A.activation(uT[:, c, :], bank[(t + c) % NLIN][:], ACT.Copy), evac_name(t + c), (t + c) // NLIN + 1)
                for c in range(2):
                    finish_tile(t + 2 + c)
                    if gi:
                        act.wait_ge(S("zs_rdy"), 2 * gi)
                    do(A.activation(zsg[:, c, :], bank[(t + 2 + c) % NLIN][:], ACT.Sigmoid), "zsg")
                act.wait_ge(S("ab_mm"), gi + 1)
                if gi:
                    act.wait_ge(S("y_mm"), 2 * gi)
                else:
                    act.wait_ge(S("ab_zero"), 2)
                for i in range(2):
                    src, dst = bank[4 + i], AB[:, 2 * i, 0:1]
                    do(A.activation(view(dst, [[T, 2], [1, 129]]), view(src[:, 0:1], [[GDIM, 2], [1, 129]]), ACT.Copy))
                    do(A.activation(view(dst, [[T, 2], [1, 127]], 129), view(src[:, 0:1], [[GDIM, 2], [-1, 127]], 127), ACT.Copy))
                    do(A.activation(view(dst, [[T, 2], [1, 127]], GDIM + 1), view(src[:, 0:1], [[GDIM, 2], [1, 127]], 129), ACT.Copy),
                       "ab_act")
                for g in range(2):
                    act.wait_ge(S("y_mm"), 2 * gi + g + 1)
                    if gi:
                        act.wait_ge(S("yf_rdy"), 2 * gi + g - 1)
                    do(A.activation(qsn[:, g, 0:255], bank[6 + g][:, 257:512], ACT.Copy), "qsn")
                for g in range(2):
                    act.wait_ge(S("yg_rdy"), 2 * gi + g + 1)
                    if gi == 4:
                        pass
                    do(A.activation(gh[:, 2 * (gi % 4) + g, :], yg[:, g, :], ACT.Copy), "yg_hi")
                if gi % 4 == 3:
                    for n in range(KT):
                        finish_tile(t + 4 + n)
            last = len(tiles) - 1
            norm(6, T, xT, (evac_name(last), last // NLIN + 1, False))
            for i in range(2 * TT):
                act.wait_ge(S("out_ps"), i + 1)
                do(A.activation(otok[:, i // 2, (i % 2) * 512:(i % 2 + 1) * 512], bank[4 + i % 2][:], ACT.Copy), "out_ready")

        @block.vector
        def _(dve):
            do = Own(dve, "dve_chain")
            X = nc.vector

            def evac(t, ins):
                do(ins, evac_name(t), t // NLIN + 1)

            def finish_tile(t):
                dve.wait_ge(S("unit_done"), tile_last(t) + 1)

            def norm(n, m, width, src, coef, shift, dst_hi, dst_lo):
                dve.wait_ge(S("rs_ready"), n + 1)
                do.settle()

                def low(k):
                    dve.wait_ge(S("hh_ready"), KT * m + k + 1)
                    do(X.tensor_tensor(dst_lo[:, k, :], hf[:, k % 2, 0:width], dst_hi[:, k, :].bitcast(F32), ALU.subtract),
                       "h_ready")
                for k in range(KT):
                    if k >= 2:
                        do.settle()
                    if shift:
                        do(X.scalar_tensor_tensor(hf[:, k % 2, 0:width], src[:, k, :], coef(k), rs[:, 0:width], ALU.mult, ALU.mult))
                        do.settle()
                        do(X.tensor_scalar(hf[:, k % 2, 0:width], hf[:, k % 2, 0:width], shift(k), None, ALU.add), "hf_ready")
                    else:
                        do(X.scalar_tensor_tensor(hf[:, k % 2, 0:width], src[:, k, :], coef(k), rs[:, 0:width], ALU.mult, ALU.mult),
                           "hf_ready")
                    if k:
                        low(k - 1)
                low(KT - 1)

            def residual(t, n, gate=None):
                finish_tile(t)
                if gate is None:
                    evac(t, X.tensor_tensor(xT[:, n, :], xT[:, n, :], bank[t % NLIN][:], ALU.add))
                else:
                    evac(t, X.scalar_tensor_tensor(xT[:, n, :], bank[t % NLIN][:], gate(n), xT[:, n, :], ALU.mult, ALU.add))

            do(X.memset(ones[:], 1.0), "const_set")
            do(X.memset(halfeps, EPS), "const_set")
            for k in range(KT):
                dve.wait_ge(S("xT_ps"), k + 1)
                do(X.tensor_copy(xT[:, k, :], bank[k % 2][:]), "xT_ev")
            dve.wait_ge(S("V_ready"), 1)
            L0 = V[:, ROWS["lb0"][0]:ROWS["lb0"][0] + 32]
            L1 = V[:, ROWS["lb1"][0]:ROWS["lb1"][0] + 32]
            mxl = small[:, 192:224]
            do(X.tensor_tensor(mxl, L0, L1, ALU.max))
            do.settle()
            do(X.tensor_tensor(lb, L0, mxl, ALU.subtract), "lb_diff")
            do(X.tensor_tensor(oml, L1, mxl, ALU.subtract), "lb_diff")
            norm(0, 0, T, xT, lambda k: vcol("norm1", k), None, hh, hl)
            dve.wait_ge(S("lb_exp"), 1)
            do.settle()
            do(X.tensor_tensor(mxl, lb, oml, ALU.add))
            do.settle()
            do(X.reciprocal(mxl, mxl))
            do.settle()
            do(X.tensor_tensor(lb, lb, mxl, ALU.mult))
            do.settle()
            do(X.tensor_scalar(oml, lb, -1.0, 1.0, ALU.mult, ALU.add))

            do(X.memset(raw[:, :, 0:3], 0.0), "raw_zero")
            for t in range(12):
                dve.wait_ge(S(evac_name(t)), t // NLIN + 1)
                if t >= 2:
                    dve.wait_ge(S("silu_done"), t - 1)
                a, r = hf[:, t % 2, :], raw[:, t % 2, :]
                do(X.tensor_scalar(a, r[:, 0:T], vcol("conv", t), None, ALU.mult))
                for i in range(1, 4):
                    do.settle()
                    do(X.scalar_tensor_tensor(a, r[:, i:i + T], vcol("conv", 12 * i + t), a, ALU.mult, ALU.add),
                       "conv_done" if i == 3 else None)
            dve.wait_ge(S("ba_act"), 1)
            b3 = bank[3][:, 0:32].rearrange("p (a c) -> p a c", c=8)
            do(X.tensor_tensor(t2[:, 0:16].rearrange("p (a c) -> p a c", c=4), b3[:, :, 4:8],
                               view(ab, [[0, 4], [1, 4]], 4), ALU.add))
            do.settle()
            do(X.scalar_tensor_tensor(t2[:, 16:32], t2[:, 0:16], -1.0, t2[:, 0:16], ALU.mult, ALU.max), "sp_abs")
            dve.wait_ge(S("sp_ln"), 1)
            do.settle()
            do(X.scalar_tensor_tensor(t2[:, 16:32], t2[:, 0:16], 0.0, t2[:, 16:32], ALU.max, ALU.add))
            do.settle()
            do(X.scalar_tensor_tensor(ggc.rearrange("p (a c) -> p a c", c=4), t2[:, 16:32].rearrange("p (a c) -> p a c", c=4),
                                      -1.0, view(ab, [[0, 4], [1, 4]]), ALU.mult, ALU.mult), "g_ready")
            for i in range(8):
                dve.wait_ge(S("l2_rs"), i + 1)
                do(X.scalar_tensor_tensor(qkv[:, i, :], qkv[:, i, :], 128.0 ** -0.5 if i < 4 else 1.0, hf[:, i % 2, :],
                                          ALU.mult, ALU.mult), "l2_done")

            def front(n):
                w = (n % 4 + 1) * P
                dve.wait_ge(S("s_done"), n + 1)
                if n >= 2:
                    dve.wait_ge(S("p_ready"), n - 1)
                do(X.scalar_tensor_tensor(sm[:, n % 2, 0:w], bank[0][:, 0:w], 0.125, dneg[:, T - w:T],
                                          ALU.mult, ALU.add), "sm_ready")
                do.settle()
                do(X.tensor_reduce(mx[:, n:n + 1], sm[:, n % 2, 0:w], AX.X, ALU.max))
                do.settle()
                do(X.tensor_scalar(nmx[:, n:n + 1], mx[:, n:n + 1], -1.0, None, ALU.mult), "nmx_ready")

            def back(n):
                w = (n % 4 + 1) * P
                dve.wait_ge(S("pexp"), n + 1)
                if n >= 2:
                    dve.wait_ge(S("pT_done"), n - 1)
                do(X.tensor_tensor_reduce(pr[:, n % 2, 0:w], sm[:, n % 2, 0:w], dcnt[:, T - w:T], 1.0, 0.0, ALU.mult, ALU.add,
                                          den[:, n:n + 1]))
                do.settle()
                do(X.reciprocal(rden[:, n:n + 1], den[:, n:n + 1]))
                do.settle()
                do(X.tensor_scalar(pr[:, n % 2, 0:w], pr[:, n % 2, 0:w], rden[:, n:n + 1], None, ALU.mult), "p_ready")

            def pair_low(hp):
                dve.wait_ge(S("ob_hi"), hp + 1)
                do(X.tensor_tensor(gl[:, 4 + hp, :], bank[2][:], gh[:, 4 + hp, :].bitcast(F32), ALU.subtract), "ob_lo")

            def attention_tail(n):
                if n:
                    back(n - 1)
                if n > 8 and n % 8 == 2:
                    pair_low(n // 8 - 1)

            dve.wait_ge(S("gcc_ready"), 1)
            up = cst[:, 0:P]
            for c in range(TT):
                tok = slice(c * P, (c + 1) * P)
                if c:
                    dve.wait_ge(S("o_ev"), c)
                for h in range(4):
                    do(X.tensor_scalar(G["ug"][:, h, :], up, ggc[:, 4 * c + h:4 * c + h + 1], None, ALU.mult),
                       "ug" if h == 3 else None)
                dve.wait_ge(S("gr"), c + 1)
                for h in range(4):
                    do(X.tensor_scalar(G["ee"][:, h, :], bank[3][:, h * P:(h + 1) * P], gcc[:, 4 * c + h:4 * c + h + 1], 0.0,
                                       ALU.subtract, ALU.min))
                do(X.tensor_tensor(kec[:, 4 * c:4 * c + 4], view(bank[3][:, 0:1], [[P, 4]], P - 1), gcc[:, 4 * c:4 * c + 4],
                                   ALU.subtract), "dif")
                attention_tail(8 * c)
                front(8 * c)
                dve.wait_ge(S("eex"), c + 1)
                for h in range(4):
                    do(X.scalar_tensor_tensor(G["ee"][:, h, :], G["ee"][:, h, :], beta[:, 4 * c + h:4 * c + h + 1], up,
                                              ALU.mult, ALU.mult))
                do(X.tensor_tensor(kec[:, 4 * c:4 * c + 4], kec[:, 4 * c:4 * c + 4], beta[:, 4 * c:4 * c + 4], ALU.mult))
                do.settle()
                dve.wait_ge(S("kk"), c + 1)
                b4, b5 = (bank[i][:].rearrange("p (h c) -> p h c", c=P) for i in (4, 5))
                do(X.tensor_tensor(G["lt"][:], G["ee"][:], b4, ALU.mult))
                do(X.tensor_tensor(G["at_"][:], G["ee"][:], b5, ALU.mult))
                do.settle(1)
                do(X.tensor_tensor(G["m0"][:], G["lt"][:], view(gmask[:, 0, :], [[0, 4], [1, P]]), ALU.mult))
                do.settle()
                do(X.tensor_tensor(G["xt"][:], view(ident[:], [[0, 4], [1, P]]), G["m0"][:], ALU.subtract), "x1")
                dve.wait_ge(S("vk"), c + 1)
                for h in range(4):
                    i = 4 * c + h
                    do(X.tensor_scalar(G["gk"][:, h, :], bank[3][:, h * P:(h + 1) * P], egc[:, i:i + 1], None, ALU.mult))
                    do(X.tensor_scalar(G["kend"][:, h, :], bank[3][:, h * P:(h + 1) * P], kec[:, i:i + 1], None, ALU.mult))
                do(X.tensor_copy(G["vtok"][:], bank[6][:].rearrange("p (h c) -> p h c", c=P)), "gkv")
                do(X.tensor_tensor(G["m1"][:], G["lt"][:], view(gmask[:, 1, :], [[0, 4], [1, P]]), ALU.mult), "m_rdy")
                do(X.tensor_tensor(G["qdec"][:], qkv[:, 0:4, tok], G["eg"][:], ALU.mult))
                for l in range(1, 7):
                    attention_tail(8 * c + l)
                    front(8 * c + l)
                    if l < 6:
                        if l == 1:
                            dve.wait_ge(S("x1"), c + 1)
                        do(X.tensor_tensor(G["m%d" % ((l + 1) % 2)][:], G["lt"][:], view(gmask[:, l + 1, :], [[0, 4], [1, P]]),
                                           ALU.mult), "m_rdy")
                    dve.wait_ge(S("XX"), 6 * c + l)
                    if l < 6:
                        if l == 1:
                            dve.wait_ge(S("x1e"), c + 1)
                        do(X.tensor_tensor(G["xx"][:], G["xx"][:], b4, ALU.subtract))
                    do(X.tensor_tensor(G["xt"][:], G["xt"][:], b5, ALU.subtract), "x_upd")
                attention_tail(8 * c + 7)
                front(8 * c + 7)
                dve.wait_ge(S("uwe"), c + 1)
                if c:
                    dve.wait_ge(S("PS"), c)
                    do(X.tensor_tensor(G["u"][:], G["u"][:], bank[3][:].rearrange("p (h c) -> p h c", c=P), ALU.subtract), "u")
                else:
                    do(X.tensor_copy(small[:, 250:251], small[:, 0:1]), "u")
                if c < TT - 1:
                    dve.wait_ge(S("ds"), c + 1)
                    if c == 0:
                        do(X.tensor_copy(G["st"][:], b5), "st_upd")
                    else:
                        for h in range(4):
                            do(X.scalar_tensor_tensor(G["st"][:, h, :], G["st"][:, h, :], G["eg"][:, h, P - 1:P],
                                                      bank[5][:, h * P:(h + 1) * P], ALU.mult, ALU.add),
                               "st_upd" if h == 3 else None)
            attention_tail(32)
            pair_low(3)
            for i in range(8, 12):
                h = i - 8
                dve.wait_ge(S("l2_rs"), i + 1)
                do(X.scalar_tensor_tensor(oT[:, h, :], oT[:, h, :], vcol("gdn_norm"), hf[:, i % 2, :], ALU.mult, ALU.mult), "l2_done")
                do.settle()
                do(X.tensor_tensor(oT[:, h, :], oT[:, h, :], zT[:, h, :], ALU.mult), "oa")
            for h in range(4):
                dve.wait_ge(S("oa_hi"), h + 1)
                do(X.tensor_tensor(gl[:, h, :], oT[:, h, :], gh[:, h, :].bitcast(F32), ALU.subtract), "oa_lo")

            do(X.memset(fraw[:, :, 0:2], 0.0), "fraw_zero")
            for n in range(KT):
                residual(T_OUT + n, n)
            norm(1, 1, T, xT, lambda k: vcol("norm2", k), None, hh, hl)
            p = 0
            for r, (t0, t1_) in enumerate(ffn_tiles):
                for j in range(len(ROUND[r])):
                    for half in range(2):
                        t = t0 + 2 * j + half
                        jj = ROUND[r][j] + half * FT
                        dve.wait_ge(S(evac_name(t)), t // NLIN + 1)
                        i = 2 * (p % 2) + half
                        a, w = facc[:, i, :], fraw[:, i, :]
                        do(X.tensor_scalar(a, w[:, 0:T], vcol("ffn_conv", jj), None, ALU.mult))
                        for k in range(1, 3):
                            do.settle()
                            do(X.scalar_tensor_tensor(a, w[:, k:k + T], vcol("ffn_conv", 2 * FT * k + jj), a, ALU.mult, ALU.add),
                               "fconv" if k == 2 else None)
                    dve.wait_ge(S("fsilu"), p + 1)
                    do.settle()
                    do(X.tensor_tensor(a, a, fg[:, p % 2, :], ALU.mult), "fprod")
                    dve.wait_ge(S("fhi"), p + 1)
                    do(X.tensor_tensor(gl[:, j, :], a, gh[:, j, :].bitcast(F32), ALU.subtract), "flo")
                    p += 1
                for n in range(KT):
                    residual(t1_ + n, n)
            for s, n in enumerate([48, 16]):
                do(X.tensor_tensor(ada[:, s:2 * n:2], bank[7][:, s:2 * n:2], V[:, ROWS["ada_b"][0]:ROWS["ada_b"][0] + n], ALU.add))
            do.settle()
            for i, (l, s) in enumerate([(0, 0), (0, 1), (1, 0)]):
                g0 = ROWS["norm_g"][0] + 8 * l
                do(X.scalar_tensor_tensor(acoef[:, 8 * i:8 * i + 8], view(ada, [[2, 8]], (24 * l + 8) * 2 + s), 1.0, V[:, g0:g0 + 8],
                                          ALU.add, ALU.mult))

            def shift(l, s):
                return lambda k: ada[:, (24 * l + k) * 2 + s:(24 * l + k) * 2 + s + 1]

            def gate(l):
                return lambda k: ada[:, (24 * l + 16 + k) * 2:(24 * l + 16 + k) * 2 + 1]

            def coef(i):
                return lambda k: acoef[:, 8 * i + k:8 * i + k + 1]
            dve.wait_ge(S("rs_ready"), 3)
            for k in range(KT):
                do(X.scalar_tensor_tensor(xT[:, k, :], xT[:, k, :], vcol("final1", k), rs[:], ALU.mult, ALU.mult), "x1_norm")
            norm(3, 2, T, xT, coef(0), shift(0, 0), hh, hl)
            norm(4, 3, CT, craw, coef(1), shift(0, 1), ch, cl)

            do.settle()
            do(X.memset(qcx[:, 0, CT - 1:CT], 1.0))
            do(X.memset(qcx[:, 1, 0:1], 1.0))
            dve.wait_ge(S("hmask_in"), 16)

            def col(vec, dr, g):
                return vec[:, 16 * dr + g:16 * dr + g + 1]

            def context(g):
                dve.wait_ge(S("cevac"), 3 * g + 2)
                for dr in range(2):
                    do(X.tensor_scalar(sgc[:, dr, :], sgc[:, dr, :], col(oml, dr, g), col(lb, dr, g), ALU.mult, ALU.add))
                do.settle()
                if g:
                    dve.wait_ge(S("b6"), 4 * g - 2)
                do(X.tensor_scalar(kcx[:], sgc[:], -1.0, 1.0, ALU.mult, ALU.add))
                f0, f1, q0, q1 = sgc[:, 0, :], sgc[:, 1, :], qcx[:, 0, :], qcx[:, 1, :]
                r0 = view(f0[:, 0:1], [[-1, CT - 1]], CT - 1)
                do(X.tensor_tensor_scan(view(q0[:, 0:1], [[-1, CT - 1]], CT - 2), r0, r0, 1.0, ALU.mult, ALU.bypass))
                do(X.tensor_tensor_scan(q1[:, 1:CT], f1[:, 0:CT - 1], f1[:, 0:CT - 1], 1.0, ALU.mult, ALU.bypass))
                do.settle()
                do(X.tensor_tensor(kcx[:], kcx[:], qcx[:], ALU.mult), "kq_rdy")

            def start(g):
                dve.wait_ge(S(evac_name(T_HG + 5 * g + 2)), (T_HG + 5 * g + 2) // NLIN + 1)
                for dr in range(2):
                    do(X.tensor_scalar(PP[:, dr, :], sgf[:, dr, :], col(oml, dr, g), col(lb, dr, g), ALU.mult, ALU.add),
                       "sgf_used" if dr else None)
                if g:
                    dve.wait_ge(S("o_mm"), g)
                do(X.memset(QQ[:], 1.0))
                do.settle()
                do(X.tensor_scalar(KK[:], PP[:], -1.0, 1.0, ALU.mult, ALU.add))
                do.settle()

            def produce(g, pi, between=None):
                used = 11 * g + pi - 1 if pi >= 2 else (11 * g + (-1 if pi == 0 else 0) if g else 0)
                if used > 0:
                    dve.wait_ge(S("lv_mm"), used)
                kc, qc = KC[:, pi % 2, :], QC[:, pi % 2, :]
                q = qs[:, g % 2, :]
                if pi == 0:
                    do.settle()
                    do(X.tensor_tensor(kc, KK[:, 0, :], KK[:, 1, :], ALU.add))
                    do(X.tensor_copy(qc, q), "lv_rdy")
                    return
                n = LEVELS[pi - 1]
                nb = T // (2 * n)
                sel = [[2 * n, nb], [T + n, 2], [1, n]]
                flat = [[2 * n, nb], [n, 2], [1, n]]
                do.settle(1)
                do(X.tensor_tensor(view(kc[:, 0:1], flat), view(KK[:, 0, 0:1], sel), view(QQ[:, 0, 0:1], sel), ALU.mult))
                do.settle(1)
                do(X.tensor_tensor(view(qc[:, 0:1], flat), view(q[:, 0:1], flat),
                                   view(PP[:, 0, 0:1], [[2 * n, nb], [n - T, 2], [1, n]], T), ALU.mult), "lv_rdy")
                if pi < 9:
                    do.settle(1)
                    do(X.tensor_tensor(view(QQ[:, 0, 0:1], [[T + n, 2], [2 * n, nb], [1, n]]),
                                       view(QQ[:, 0, 0:1], [[T + n, 2], [2 * n, nb], [1, n]]),
                                       view(PP[:, 0, 0:1], [[T - 2 * n + 1, 2], [2 * n, nb], [0, n]], 2 * n - 1), ALU.mult))
                if between:
                    between()
                    do.settle(1)
                else:
                    do.settle()
                do(X.tensor_tensor(view(PP[:, 0, 0:1], [[T - n, 2], [2 * n, nb], [1, n]], n),
                                   view(PP[:, 0, 0:1], [[T - n, 2], [2 * n, nb], [1, n]], n),
                                   view(PP[:, 0, 0:1], [[T + 1, 2], [2 * n, nb], [0, n]], n - 1), ALU.mult))

            def take(g, li):
                dve.wait_ge(S("lv_mm"), 11 * g + li + 1)
                do(X.copy_predicated(view(MT[:, 0, 0:1], [[T + P, 4], [1, P]]), view(hmask[:, li, :], [[0, 4], [1, P]]),
                                     bank[4 + li % 2][:].rearrange("p (a c) -> p a c", c=P)),
                   "lv_ev%d" % (li % 2), (6 if li % 2 == 0 else 5) * g + li // 2 + 1)

            def silu(h, which, t, dst):
                i = t % NLIN
                dve.wait_ge(S("sg_q" if which == 0 else "sg_z"), h + 1)
                evac(t, X.tensor_tensor(dst, bank[i][:], sgt[:, which, :], ALU.mult))

            for h in range(HG + 1):
                t = T_HG + 5 * h
                g = h - 1
                if h:
                    context(g)
                    start(g)
                    produce(g, 0)
                    produce(g, 1)
                if h < HG:
                    silu(h, 0, t, qs[:, h % 2, :])
                    do(X.tensor_copy(small[:, 250:251], small[:, 0:1]), "sgt_q")
                if h:
                    for pi in range(2, 10):
                        produce(g, pi, (lambda li=pi - 2: take(g, li)))
                    do.settle()
                    for dr in range(2):
                        do(X.tensor_tensor(QQ[:, dr, :], qs[:, g % 2, :], PP[:, dr, :], ALU.mult), "qp_rdy" if dr else None)
                if h < HG:
                    silu(h, 1, t + 4, sz[:, h % 2, :])
                    do(X.tensor_copy(small[:, 251:252], small[:, 0:1]), "sz_rdy")
                if h:
                    dve.wait_ge(S("osq"), h)
                    y = yA[:, g, :] if g < 8 else yB[:, g - 8, :]
                    do(X.scalar_tensor_tensor(y, bank[6][:], vcol("hg_norm"), sz[:, g % 2, :], ALU.mult, ALU.mult), "y_pre")
            do.settle()
            for h in range(HG + 1):
                if h < HG:
                    y = yA[:, h, :] if h < 8 else yB[:, h - 8, :]
                    dve.wait_ge(S("rs_row"), h + 1)
                    do(X.tensor_tensor(y, y, bank[4 + h % 2][:], ALU.mult), "y_norm")
                if h:
                    g = h - 1
                    dve.wait_ge(S("y_hi"), h)
                    y = yA[:, g, :] if g < 8 else yB[:, g - 8, :]
                    hi_, lo_ = (hh[:, g, :], hl[:, g, :]) if g < 8 else (gh[:, g - 8, :], gl[:, g - 8, :])
                    do(X.tensor_tensor(lo_, y, hi_.bitcast(F32), ALU.subtract), "y_lo")
            for n in range(KT):
                residual(T_HO + n, n, gate(0))
            norm(5, 4, T, xT, coef(2), shift(1, 0), hh, hl)

            do(X.memset(AB[:, :, GDIM:GDIM + 1], 0.0), "ab_zero")
            do(X.memset(AB[:, :, GDIM + 128:GDIM + 129], 0.0), "ab_zero")
            for gi in range(GROUPS):
                t = ft_tiles[gi // 4] + 4 * (gi % 4)
                for c in range(2):
                    dve.wait_ge(S("zsg"), 2 * gi + c + 1)
                    evac(t + 2 + c, X.tensor_tensor(zs[:, c, :], bank[(t + 2 + c) % NLIN][:], zsg[:, c, :], ALU.mult))
                    do(X.tensor_copy(small[:, 250 + c:251 + c], small[:, 0:1]), "zs_rdy")
                for i in range(2):
                    dve.wait_ge(S("ab_mm"), gi + 1)
                    dve.wait_ge(S("ab_act"), 2 * gi + i + 1)
                    src, dst = bank[4 + i], AB[:, 2 * i, 0:1]
                    do(X.tensor_scalar(view(dst, [[T, 2], [1, 127]], GDIM + 129), view(src[:, 0:1], [[GDIM, 2], [-1, 127]], 255),
                                       -1.0, None, ALU.mult), "ab_ev")
                for g in range(2):
                    b, q, y = bank[6 + g], qsn[:, g, :], yf[:, g, :]
                    dve.wait_ge(S("qsn"), 2 * gi + g + 1)
                    do(X.tensor_tensor(y[:, 1:256], b[:, 1:256], q[:, 0:255], ALU.subtract))
                    do(X.tensor_tensor(y[:, 257:512], view(b[:, 0:1], [[-1, 255]], 255), view(q[:, 0:1], [[-1, 255]], 254), ALU.add),
                       "yf_rdy")
                    do(X.tensor_copy(y[:, 0:512:256], b[:, 0:512:256]), "y_ev")
                    do.settle()
                    if gi:
                        dve.wait_ge(S("yg_hi"), 2 * (gi - 1) + g + 1)
                    do(X.tensor_tensor(yg[:, g, :], y, zs[:, g, :], ALU.mult), "yg_rdy")
                for g in range(2):
                    k = 2 * (gi % 4) + g
                    dve.wait_ge(S("yg_hi"), 2 * gi + g + 1)
                    do(X.tensor_tensor(gl[:, k, :], yg[:, g, :], gh[:, k, :].bitcast(F32), ALU.subtract), "yg_lo")
                if gi % 4 == 3:
                    for n in range(KT):
                        residual(t + 4 + n, n, gate(1))
            dve.wait_ge(S("rs_ready"), 7)
            for k in range(KT):
                do(X.scalar_tensor_tensor(xT[:, k, :], xT[:, k, :], vcol("final_g", k), rs[:], ALU.mult, ALU.mult), "x_final")


ROWS_LOADED = 0
for _name, (_r, _n) in ROWS.items():
    ROWS_LOADED += 16 * ((_r + _n - 1) // P - _r // P + 1)

INPUTS = ["x", "norm1_w", "w_in", "conv_qkv_w", "a_log", "dt_bias", "gdn_norm_w", "w_out", "norm2_w", "w_up", "ffn_conv_w",
          "w_down", "final_norm_w", "c_2", "ctx_2", "c_ctx_2", "ada_w_2", "ada_b_2", "norm_g_2", "hg_w_in_2",
          "hg_lb_logits_2", "hg_norm_g_2", "hg_w_out_2", "ft_w_in_2", "ft_w_out_2", "final_g_2"]


def kernel(**inputs):
    import concourse.bacc as bacc
    from concourse.bass_utils import run_bass_kernel_spmd

    nc = bacc.Bacc("TRN2", target_bir_lowering=False, num_devices=1)
    arrays, aps = {}, {}
    for name in INPUTS:
        arrays[f"in_{name}"] = np.ascontiguousarray(inputs[name])
    for name, a in host_constants().items():
        arrays[f"const_{name}"] = a
    for name, a in arrays.items():
        aps[name.split("_", 1)[1]] = nc.dram_tensor(name, a.shape, mybir.dt.from_np(a.dtype), kind="ExternalInput").ap()
    out = nc.dram_tensor("out", (1, T, D), F32, kind="ExternalOutput").ap()
    build(nc, aps, out)
    r = run_bass_kernel_spmd(nc, [arrays], core_ids=[0])
    return r.results[0]["out"]
```

```python
from contextlib import ExitStack

import numpy as np

import concourse.bass as bass
from concourse import mybir

F32 = mybir.dt.float32
F32R = mybir.dt.float32r
U32 = mybir.dt.uint32
ALU = mybir.AluOpType
ACT = mybir.ActivationFunctionType
AX = mybir.AxisListType

P = 128
T = 512
TT = T // P
D = 1024
KT = D // P
GH_N, DH_N = 4, 8
GW, DW = 512, 512
O_Z, O_BA, O_B = 3 * GW, 4 * GW, 4 * GW + 2 * GH_N
FF = 2816
FT = FF // P
ROUND = [range(0, 8), range(8, 16), range(16, 22)]
HG = 16
E_IN = 2048
CT = 256
EPS = 1e-6
GROUPS, GDIM = 8, 256
NST, NSPLIT, NLIN = 4, 3, 3
LEVELS = [1, 2, 4, 8, 16, 32, 64, 128, 256]

ROWS = {}
_at = 0
for _name, _n in [("norm1", 8), ("norm2", 8), ("final1", 8), ("conv", 48), ("gdn_norm", 1),
                  ("hg_norm", 1), ("norm_g", 16), ("final_g", 8), ("lb0", 32), ("lb1", 32),
                  ("ada_b", 48), ("c", 8), ("c_ctx", 8), ("ffn_conv", 132)]:
    ROWS[_name] = (_at, _n)
    _at += _n
NROWS = _at
NV = 3 * P
assert NROWS <= NV


def modulated(i):
    return (0, 1) if i < 2 * KT else (0,)


def modulation_sums(i):
    return 2 * i if i < 2 * KT else i + 2 * KT


def host_constants():
    i = np.arange(P)
    ident = np.eye(P)
    upper = (i[:, None] <= i[None, :]) * 1.0
    lev = []
    for h in [1, 2, 4, 8, 16, 32, 64]:
        same = (i[:, None] // (2 * h)) == (i[None, :] // (2 * h))
        first, second = (i // h) % 2 == 0, (i // h) % 2 == 1
        lev.append((same & first[:, None] & second[None, :]) * 1.0)
    cnt = []
    for dist in [3, 2, 1, 0]:
        d = i[:, None] - i[None, :] + dist * P
        cnt.append(((d >= 0) & (d <= 128)) * 1.0 + ((d >= 0) & (d % 4 == 0)) + ((d >= 0) & (d % 16 == 0)))
    cnt = np.concatenate(cnt, 1)
    neg = np.where(cnt > 0, 0.0, -1e30)
    cf = np.concatenate([ident, upper] + lev + [cnt, neg], 1).astype(np.float32)
    m = [np.eye(P)]
    for h in [1, 2, 4, 8, 16, 32, 64]:
        same = (i[:, None] // (2 * h)) == (i[None, :] // (2 * h))
        m.append(same & ((i[:, None] // h) % 2 != (i[None, :] // h) % 2))
    hm = np.stack(m, 1).astype(np.uint32)
    c = np.arange(GDIM)
    g = np.arange(GDIM // 2 + 1)
    dch = np.concatenate([np.cos(2 * np.pi * np.outer(c, g) / GDIM),
                          np.sin(2 * np.pi * np.outer(c, g[1:-1]) / GDIM)], 1).astype(np.float32)
    t = np.arange(T)
    u = np.arange(T // 2 + 1)
    s = 1.0 / np.sqrt(T * GDIM)
    dtok = (s * np.concatenate([np.cos(2 * np.pi * (np.outer(t, u) % T) / T),
                                np.sin(2 * np.pi * (np.outer(t, u[1:-1]) % T) / T)], 1)).astype(np.float32)
    onecol = np.zeros((P, 31), np.float32)
    onecol[:, 15] = 1.0
    return {"cf": cf, "hm": hm, "dch": dch, "dtok": dtok, "onecol": onecol}


def make_units():
    units, tiles = [], []

    def add(w, rows, col, x, start=True, stop=True, ctx=False):
        if start:
            tiles.append([])
        tiles[-1].append(sum(u["lin"] for u in units))
        units.append(dict(w=w, rows=rows, col=col, x=x, start=start, stop=stop, lin=True,
                          tile=len(tiles) - 1, ctx=ctx))

    raws = [dict(w="ada_w", layer=l, rows=(0, 8), col=j * P, lin=False, raw=l * 24 + j)
            for l in range(2) for j in range(24)]
    late = raws[24:]

    for t in range(28):
        add("w_in", (0, 8), t * P if t < 16 else O_B + (t - 16) * P, "h")
    units.extend(raws[:24])
    for n in range(KT):
        add("w_out", (0, 8), n * P, "g")
    for r in ROUND:
        for j in r:
            for half in range(2):
                add("w_up", (0, 8), half * FF + j * P, "h")
            units.extend(late[:2 if j < 2 else 1])
            late = late[2 if j < 2 else 1:]
        for n in range(KT):
            add("w_down", (r[0], len(r)), n * P, "g")
    for hd in range(HG):
        for s in range(5):
            add("hg_w_in", (0, 8), s * E_IN + hd * P, "h", ctx=s in (1, 2, 3))
    for n in range(KT):
        add("hg_w_out", (0, 8), n * P, "h", stop=False)
        add("hg_w_out", (8, 8), n * P, "g", start=False)
    for half in range(2):
        for gi in range(4 * half, 4 * half + 4):
            for part in range(2):
                for c in range(2):
                    add("ft_w_in", (0, 8), part * E_IN + (2 * gi + c) * P, "h")
        for n in range(KT):
            add("ft_w_out", (8 * half, 8), n * P, "g")
    lin = 0
    seen = [0] * NST
    for n, u in enumerate(units):
        u["slot"], u["load"] = n % NST, n // NST
        if u["lin"]:
            u["lin_no"] = lin
            lin += 1
    return units, tiles


def view(ap, dims, off=0):
    return bass.AP(tensor=ap.tensor, offset=ap.offset + off, ap=[list(ap.ap[0])] + [list(x) for x in dims])


def build(nc, d, out, upto=99, debug=None):
    units, tiles = make_units()
    lin_units = [u for u in units if u["lin"]]
    n_lin = len(lin_units)
    ctx = ExitStack()
    with ctx:
        sems = {}

        def S(name):
            if name not in sems:
                sems[name] = ctx.enter_context(nc.semaphore("s_" + name))
            return sems[name]

        base = 16640
        assert nc.sbuf_base <= base

        def at(name, kib, shape, dt=F32):
            size = int(np.prod(shape[1:])) * 4
            assert base + kib * 1024 + size <= 229360, name
            return nc.alloc_sbuf_tensor_at(name, shape, dt, offset=int(base + kib * 1024))

        xT = at("xT", 0, [P, KT, T])
        stage = at("stage", 16, [P, NST, KT, P])
        wh = at("wh", 32, [P, NSPLIT, KT, P], F32R)
        wl = at("wl", 44, [P, NSPLIT, KT, P], F32R)
        hh = at("hh", 56, [P, KT, T], F32R)
        hl = at("hl", 72, [P, KT, T], F32R)
        gh = at("gh", 88, [P, KT, T], F32R)
        gl = at("gl", 104, [P, KT, T], F32R)
        V = at("V", 120, [P, NV])
        ident = at("ident", 121.5, [P, P])
        ones = at("ones", 122, [P, P])
        sq = at("sq", 122.5, [P, 2, T])
        hf = at("hf", 126.5, [P, 2, T])
        rs = at("rs", 130.5, [P, T])
        small = at("small", 132.5, [P, 256])
        A0 = 133.5
        zT = at("zT", A0, [P, 4, T])
        qkv = at("qkv", A0 + 8, [P, 12, T])
        xtok = at("xtok", A0 + 8, [P, TT, D])
        rowsT = at("rowsT", A0 + 24, [P, 3, P])
        bqkv = at("bqkv", A0 + 32, [P, 12, T])
        raw = at("raw", A0 + 56, [P, 2, T + 8])
        mprod = at("mprod", A0 + 56, [P, KT, P])
        mod = at("mod", A0 + 60.25, [P, 2, 2, P])
        cst = at("cst", A0 + 62.25, [P, 2 * P])
        gmask = at("gmask", A0 + 63.25, [P, 7, P])
        dcnt = at("dcnt", A0 + 66.75, [P, T])
        dneg = at("dneg", A0 + 68.75, [P, T])
        w8 = at("w8", A0 + 70.75, [P, KT, 8])
        w8h = at("w8h", A0 + 72.25, [P, KT, 8], F32R)
        w8l = at("w8l", A0 + 72.5, [P, KT, 8], F32R)
        gs = at("gs", A0 + 71, [P, 320])
        pT = at("pT", 32, [P, 2, TT, T])
        sm = at("sm", 48, [P, 2, T])
        pr = at("pr", 52, [P, 2, T])
        names = ["ee", "eg", "at_", "lt", "m0", "m1", "xx", "xt", "tt", "vtok", "gk", "kend", "u", "wkT", "qdec", "st"]
        G = {n: at("g_" + n, 56 + 2 * i, [P, 4, P]) for i, n in enumerate(names)}
        G["ug"] = G["tt"]
        oT = at("oT", 104, [P, 4, T])

        fraw = at("fraw", A0, [P, 4, T + 8])
        facc = at("facc", A0 + 9, [P, 4, T])
        fg = at("fg", A0 + 64, [P, 2, T])
        rs2 = at("rs2", A0 + 68, [P, T])
        yA = at("yA", 88, [P, 8, T])
        yB = at("yB", A0, [P, 8, T])
        hmask = at("hmask", A0 + 16, [P, 8, P], U32)
        ch = at("ch", A0 + 20, [P, KT, CT], F32R)
        cl = at("cl", A0 + 28, [P, KT, CT], F32R)
        W0 = A0 + 36
        PP = at("PP", W0, [P, 2, T])
        QQ = at("QQ", W0 + 4, [P, 2, T])
        KK = at("KK", W0 + 8, [P, 2, T])
        KC = at("KC", W0 + 12, [P, 2, T])
        QC = at("QC", W0 + 16, [P, 2, T])
        qs = at("qs", W0 + 20, [P, 2, T])
        sz = at("sz", W0 + 24, [P, 2, T])
        sgt = at("sgt", W0 + 28, [P, 2, T])
        sgf = at("sgf", W0 + 32, [P, 2, T])
        MT = at("MT", 104, [P, TT, T])
        vT = at("vT", 112, [P, T])
        vt = at("vt", 114, [P, T])
        sgc = at("sgc", 116, [P, 2, CT])
        kcx = at("kcx", 118, [P, 2, CT])
        qcx = at("qcx", W0 + 36, [P, 2, CT])
        vcT = sq
        ctok = hf
        st2 = rs
        craw = at("craw", W0, [P, KT, CT])
        ctxtok = at("ctxtok", W0 + 8, [P, 2, D])
        dtok = at("dtok", A0, [P, TT, T])
        dch = at("dch", A0 + 8, [P, 2, GDIM])
        uT = at("uT", A0 + 10, [P, 2, T])
        zs = at("zs", A0 + 14, [P, 2, T])
        zsg = at("zsg", A0 + 18, [P, 2, T])
        AB = at("AB", A0 + 22, [P, TT, T])
        qsn = at("qsn", A0 + 30, [P, 2, T])
        yf = at("yf", A0 + 34, [P, 2, T])
        yg = at("yg", A0 + 38, [P, 2, T])
        otok = at("otok", A0 + 44, [P, TT, D])

        bank = [ctx.enter_context(nc.psum_tensor(f"bank{i}", [P, 512], F32)) for i in range(8)]

        def vcol(name, i=0):
            c = ROWS[name][0] + i
            return V[:, c:c + 1]

        halfeps = small[:, 0:1]
        onecol = small[:, 1:32]
        ada = small[:, 32:128]
        lb, oml = small[:, 128:160], small[:, 160:192]
        acoef = small[:, 192:240]
        beta, ggc, gcc, egc, kec = (gs[:, 16 * i:16 * i + 16] for i in range(5))
        ab = gs[:, 80:96]
        t1, t2 = gs[:, 96:128], gs[:, 128:160]
        mx, nmx, den, rden = gs[:, 160:192], gs[:, 192:224], gs[:, 224:256], gs[:, 256:288]
        silc = gs[:, 288:304]

        block = ctx.enter_context(nc.Block())

        def tile_last(t):
            return tiles[t][-1]

        FIRST = {}
        for t_no in range(len(tiles)):
            u = lin_units[tiles[t_no][0]]
            FIRST.setdefault(u["w"], t_no)
        T_OUT, T_UP, T_HG, T_HO, T_FT = FIRST["w_out"], FIRST["w_up"], FIRST["hg_w_in"], FIRST["hg_w_out"], FIRST["ft_w_in"]
        ffn_tiles = []
        t_no = T_UP
        for r in ROUND:
            ffn_tiles.append((t_no, t_no + 2 * len(r)))
            t_no += 2 * len(r) + KT
        ft_tiles = [T_FT, T_FT + 16 + KT]

        def shift(l, s):
            return lambda k: ada[:, (24 * l + k) * 2 + s:(24 * l + k) * 2 + s + 1]

        def gate(l):
            return lambda k: ada[:, (24 * l + 16 + k) * 2:(24 * l + 16 + k) * 2 + 1]

        def coef(i):
            return lambda k: acoef[:, 8 * i + k:8 * i + k + 1]

        @block.sync
        def _(sp):
            sp.dma_start(xtok[:], d["x"][0].rearrange("(a p) c -> p a c", p=P)).then_inc(S("x_in"), 16)
            sp.dma_start(ident[:], d["cf"][:, 0:P]).then_inc(S("ident_in"), 16)

            def rows_in(name, src):
                r0, n = ROWS[name]
                done = 0
                while done < n:
                    a = r0 + done
                    k = min(n - done, P - a % P)
                    sp.dma_start(rowsT[a % P:a % P + k, a // P, :], src[done:done + k, :]).then_inc(S("rows_in"), 16)
                    rows_in.count += 16
                    done += k
            rows_in.count = 0
            rows_in("norm1", d["norm1_w"].rearrange("a (k p) -> (a k) p", p=P))
            rows_in("norm2", d["norm2_w"].rearrange("a (k p) -> (a k) p", p=P))
            rows_in("final1", d["final_norm_w"].rearrange("(k p) -> k p", p=P))
            rows_in("conv", d["conv_qkv_w"].rearrange("a i (k p) -> (a i k) p", p=P))
            rows_in("gdn_norm", d["gdn_norm_w"])
            rows_in("hg_norm", d["hg_norm_g_2"])
            rows_in("norm_g", d["norm_g_2"].rearrange("a (k p) -> (a k) p", p=P))
            rows_in("final_g", d["final_g_2"].rearrange("(k p) -> k p", p=P))
            lbl = d["hg_lb_logits_2"].rearrange("l s (k p) -> l (s k) p", p=P)
            rows_in("lb0", lbl[0])
            rows_in("lb1", lbl[1])
            rows_in("ada_b", d["ada_b_2"].rearrange("a (k p) -> (a k) p", p=P))
            rows_in("c", d["c_2"].rearrange("a (k p) -> (a k) p", p=P))
            rows_in("c_ctx", d["c_ctx_2"].rearrange("(k p) -> k p", p=P))
            rows_in("ffn_conv", d["ffn_conv_w"].rearrange("a i (k p) -> (a i k) p", p=P))
            assert rows_in.count == ROWS_LOADED
            weights = {"w_in": d["w_in"][0], "w_out": d["w_out"][0], "w_up": d["w_up"][0], "w_down": d["w_down"][0],
                       "hg_w_in": d["hg_w_in_2"][0], "hg_w_out": d["hg_w_out_2"][0],
                       "ft_w_in": d["ft_w_in_2"][0], "ft_w_out": d["ft_w_out_2"][0]}

            def load(u):
                w = d["ada_w_2"][u["layer"]] if u["w"] == "ada_w" else weights[u["w"]]
                k0, nk = u["rows"]
                sp.dma_start(stage[:, u["slot"], 0:nk, :],
                             w[k0 * P:(k0 + nk) * P, u["col"]:u["col"] + P].rearrange("(k p) c -> p k c", p=P)
                             ).then_inc(S(f"stage_in{u['slot']}"), 16)
            for u in units[:NST]:
                load(u)
            sp.dma_start(cst[:, 0:P], d["cf"][:, P:2 * P]).then_inc(S("cst_in"), 16)
            sp.dma_start(gmask[:], d["cf"][:, 2 * P:9 * P].rearrange("p (l c) -> p l c", c=P)).then_inc(S("cst_in"), 16)
            sp.dma_start(dcnt[:], d["cf"][:, 9 * P:13 * P]).then_inc(S("cst_in"), 16)
            sp.dma_start(dneg[:], d["cf"][:, 13 * P:17 * P]).then_inc(S("cst_in"), 16)
            sp.dma_start(onecol, d["onecol"]).then_inc(S("cst_in"), 16)
            sp.dma_start(t1[0:1, 0:4], d["a_log"]).then_inc(S("cst_in"), 16)
            sp.dma_start(t1[0:1, 4:8], d["dt_bias"]).then_inc(S("cst_in"), 16)
            sp.dma_start(w8[:], d["w_in"][0, :, O_BA:O_BA + 8].rearrange("(k p) c -> p k c", p=P)).then_inc(S("cst_in"), 16)
            for u in units[NST:]:
                sp.wait_ge(S(f"stage_free{u['slot']}"), u["load"])
                if u["lin"] and u["tile"] == T_UP and u["start"]:
                    sp.wait_ge(S("pv_done"), DH_N)
                    sp.dma_start(ctxtok[:], d["ctx_2"][0].rearrange("(a p) c -> p a c", p=P)).then_inc(S("ctx_in"), 16)
                if u["lin"] and u["tile"] == T_HG and u["start"]:
                    sp.wait_ge(S("flo"), FT)
                    sp.dma_start(hmask[:], d["hm"]).then_inc(S("hmask_in"), 16)
                if u["lin"] and u["tile"] == T_FT and u["start"]:
                    sp.wait_ge(S("y_lo"), HG)
                    sp.dma_start(dtok[:], d["dtok"].rearrange("(a p) c -> p a c", p=P)).then_inc(S("dft_in"), 16)
                    sp.dma_start(dch[:], d["dch"].rearrange("(a p) c -> p a c", p=P)).then_inc(S("dft_in"), 16)
                load(u)
            for half in range(2):
                sp.wait_ge(S("out_ready"), TT * (half + 1))
                cols = slice(half * 512, (half + 1) * 512)
                sp.dma_start(out[0].rearrange("(a p) c -> p a c", p=P)[:, :, cols], otok[:, :, cols]).then_inc(S("stored"), 16)
            sp.wait_ge(S("stored"), 32)

        class Own:

            def __init__(self, eng, chain):
                self.eng, self.chain, self.n, self.past = eng, chain, {}, []

            def __call__(self, ins, name=None, value=None):
                name = name or self.chain
                self.n[name] = value or self.n.get(name, 0) + 1
                ins.then_inc(S(name), 1)
                self.past = self.past[-3:] + [(name, self.n[name])]

            def settle(self, back=0):
                name, value = self.past[-1 - back]
                self.eng.wait_ge(S(name), value)

        @block.gpsimd
        def _(pool):
            do = Own(pool, "pool_chain")
            for u in units:
                nk = u["rows"][1]
                if not u["lin"]:
                    i, vecs = u["raw"], modulated(u["raw"])
                    if i == 0:
                        pool.wait_ge(S("silc_ready"), 2)
                        pool.wait_ge(S("conv_done"), 12)
                    pool.wait_ge(S(f"stage_in{u['slot']}"), 16 * (u["load"] + 1))
                    for v in vecs:
                        n = modulation_sums(i) + v
                        if n:
                            do.settle()
                        end = v == vecs[-1]
                        do(nc.gpsimd.tensor_tensor(mprod[:], stage[:, u["slot"], :, :], view(silc[:, v:v + 1], [[2, KT], [0, P]]),
                                                   ALU.mult),
                           f"stage_free{u['slot']}" if end else None, u["load"] + 1 if end else None)
                        do.settle()
                        do(nc.gpsimd.tensor_tensor(mprod[:, 0:4, :], mprod[:, 0:4, :], mprod[:, 4:8, :], ALU.add))
                        if n >= 2:
                            pool.wait_ge(S("mod_mm"), n - 1)
                        do.settle()
                        do(nc.gpsimd.tensor_tensor(mod[:, n % 2, :, :], mprod[:, 0:2, :], mprod[:, 2:4, :], ALU.add), "mod_ready")
                    continue
                l = u["lin_no"]
                pool.wait_ge(S("hi_ready"), l + 1)
                pool.tensor_tensor(wl[:, l % NSPLIT, 0:nk, :], stage[:, u["slot"], 0:nk, :],
                                   wh[:, l % NSPLIT, 0:nk, :].bitcast(F32), ALU.subtract
                                   ).then_inc(S(f"stage_free{u['slot']}"), 1)

        def evac_name(t):
            return f"evac{t % NLIN}"

        @block.tensor
        def _(pe):
            pos = [0]

            def unit(u, first_x=None, between=iter(()), ks=None):
                slot, nk = u["slot"], u["rows"][1]
                if not u["lin"]:
                    if u["raw"] == 24:
                        pe.wait_ge(S("ada0"), 1)
                    for v in modulated(u["raw"]):
                        n = modulation_sums(u["raw"]) + v
                        pe.wait_ge(S("mod_ready"), n + 1)
                        for k in range(2):
                            mm = pe.matmul(bank[7][:, 2 * u["raw"] + v:2 * u["raw"] + v + 1], mod[:, n % 2, k, :],
                                           ones[:, 0:1], start=(k == 0), stop=(k == 1))
                        mm.then_inc(S("mod_mm"), 1)
                    return
                l, t = u["lin_no"], u["tile"]
                xh, xl = (hh, hl) if u["x"] == "h" else (gh, gl)
                pe.wait_ge(S(f"stage_free{slot}"), u["load"] + 1)
                if u["start"] and t >= NLIN:
                    pe.wait_ge(S(evac_name(t)), t // NLIN)
                s = l % NSPLIT
                ks = ks or list(range(nk))
                for k in ks:
                    if callable(first_x):
                        first_x(u, k)
                    elif first_x:
                        pe.wait_ge(S(first_x[0]), first_x[1] + k + 1)
                    a, b = u["start"] and k == ks[0], u["stop"] and k == ks[-1]
                    pe.matmul(bank[t % NLIN][:], wh[:, s, k, :], xh[:, k, :], start=a, stop=False)
                    pe.matmul(bank[t % NLIN][:], wh[:, s, k, :], xl[:, k, :], start=False, stop=False)
                    mm = pe.matmul(bank[t % NLIN][:], wl[:, s, k, :], xh[:, k, :], start=False, stop=b)
                    if k % 4 == 1:
                        next(between, None)
                if u["ctx"]:
                    next(between, None)
                    ci = 3 * ((t - T_HG) // 5) + (t - T_HG) % 5 - 1
                    half = [0, CT, 0][ci % 3]
                    if ci == 0:
                        pe.wait_ge(S("ada1"), 1)
                    if ci:
                        pe.wait_ge(S("cevac"), ci)
                    for k in range(nk):
                        a, b = k == 0, k == nk - 1
                        o = bank[7][:, half:half + CT]
                        pe.matmul(o, wh[:, s, k, :], ch[:, k, :], start=a, stop=False)
                        pe.matmul(o, wh[:, s, k, :], cl[:, k, :], start=False, stop=False)
                        mm = pe.matmul(o, wl[:, s, k, :], ch[:, k, :], start=False, stop=b)
                mm.then_inc(S("unit_done"), 1)

            def units_to(tile, first_x=None, between=iter(())):
                while True:
                    u = units[pos[0]]
                    unit(u, first_x, between)
                    first_x = None if u["lin"] else first_x
                    pos[0] += 1
                    if u["lin"] and u["tile"] == tile and u["stop"]:
                        break

            def sum_mm(j, k, width=T, b=3):
                pe.wait_ge(S("sq_ready"), j + 1)
                pe.matmul(bank[b][:, 0:width], ones[:], sq[:, j % 2, 0:width], start=(k == 0), stop=(k == KT - 1)
                          ).then_inc(S("sq_used"), 1)

            def residual_units(t0, sums, first_x):
                for n in range(KT):
                    units_to(t0 + n, first_x if n == 0 else None)
                    if n:
                        sums(n - 1)
                sums(KT - 1)

            def col_sum(i):
                pe.wait_ge(S("l2_sq"), i + 1)
                if i >= 2:
                    pe.wait_ge(S("l2_ln"), i - 1)
                pe.matmul(bank[4 + i % 2][:], ones[:], sq[:, i % 2, :], start=True, stop=True
                          ).then_inc(S("l2_sum"), 1)

            pe.wait_ge(S("ident_in"), 16)
            pe.wait_ge(S("rows_in"), ROWS_LOADED)
            for a in range(3):
                n = min(P, NROWS - a * P)
                mm = pe.transpose(bank[4][:, a * P:a * P + n], rowsT[0:n, a, :], ident[0:n, 0:n])
            mm.then_inc(S("rows_T"), 1)
            pe.wait_ge(S("x_in"), 16)
            for k in range(KT):
                if k >= 2:
                    pe.wait_ge(S("xT_ev"), k - 1)
                for a in range(TT):
                    mm = pe.transpose(bank[k % 2][:, a * P:(a + 1) * P], xtok[:, a, k * P:(k + 1) * P], ident[:])
                mm.then_inc(S("xT_ps"), 1)
            pe.wait_ge(S("const_set"), 2)
            for k in range(KT):
                sum_mm(k, k)
            for t in range(28):
                units_to(t, ("h_ready", 0) if t == 0 else None)
                if t in range(16, 24, 2):
                    col_sum(t - 16)
                    col_sum(t - 15)
                if t == 22:
                    pe.wait_ge(S("w8_lo"), 1)
                    for k in range(KT):
                        for w, x_ in ((w8h, hh), (w8h, hl), (w8l, hh)):
                            mm = pe.matmul(bank[3][0:8, :], w[:, k, :], x_[:, k, :], start=(k == 0 and w is w8h and x_ is hh),
                                           stop=(k == KT - 1 and w is w8l))
                    mm.then_inc(S("ba_T"), 1)
                if t == 23:
                    pe.wait_ge(S("ba_ev"), 1)
                    for a in range(TT):
                        pe.transpose(bank[3][:, a * 8:a * 8 + 8], rs[0:8, a * P:(a + 1) * P], ident[0:8, 0:8])
                    pe.matmul(bank[3][:, 64:72], ones[0:1, :], t1[0:1, 0:8], start=True, stop=True).then_inc(S("ba_ready"), 1)
                if t == 26:
                    pe.wait_ge(S("g_ready"), 1)
                    pe.matmul(bank[3][:, 80:96], cst[:, 0:P], ggc, start=True, stop=True).then_inc(S("gc_ps"), 1)

            for a in range(TT):
                if a == 0:
                    for t in (25, 26, 27):
                        pe.wait_ge(S(evac_name(t)), t // NLIN + 1)
                elif a >= 2:
                    pe.wait_ge(S("vb_ev"), a - 1)
                for j in range(4):
                    mm = pe.transpose(bank[1 + a % 2][:, j * P:(j + 1) * P], bqkv[:, 8 + j, a * P:(a + 1) * P], ident[:])
                mm.then_inc(S("vb_T"), 1)

            def scores(n):
                h, i = n // 4, n % 4
                o = 64 * (h % 2)
                if n:
                    pe.wait_ge(S("sm_ready"), n)
                pe.matmul(bank[0][:, 0:(i + 1) * P], bqkv[o:o + 64, h // 2, i * P:(i + 1) * P],
                          bqkv[o:o + 64, 4 + h // 2, 0:(i + 1) * P], start=True, stop=True).then_inc(S("s_done"), 1)

            def turn(n):
                h, i = n // 4, n % 4
                pe.wait_ge(S("p_ready"), n + 1)
                if n:
                    pe.wait_ge(S("pT_ev"), n)
                else:
                    pe.wait_ge(S("vb_ev"), TT)
                for j in range(i + 1):
                    mm = pe.transpose(bank[1][:, j * P:(j + 1) * P], pr[:, n % 2, j * P:(j + 1) * P], ident[:])
                mm.then_inc(S("pT_done"), 1)

            def weigh(h):
                pe.wait_ge(S("pT_ev"), 4 * h + 4)
                if h % 2 == 0 and h >= 2:
                    pe.wait_ge(S("ob_lo"), h // 2)
                o = 64 * (h % 2)
                for j in range(TT):
                    mm = pe.matmul(bank[2][o:o + 64, j * P:T],
                                   bqkv[:, 8 + h // 2, j * P + 64 * (h % 2):j * P + 64 * (h % 2) + 64],
                                   pT[:, h % 2, j, j * P:T], start=(j == 0), stop=(j == TT - 1))
                mm.then_inc(S("pv_done"), 1)

            def modulation(step):
                while not units[pos[0]]["lin"] and modulation_sums(units[pos[0]]["raw"] + 1) <= 1.3 * (step + 1):
                    unit(units[pos[0]])
                    pos[0] += 1

            def attention_tail(n):
                if n >= 1:
                    if n % 4 == 1 and n > 1:
                        weigh(n // 4 - 1)
                    turn(n - 1)

            scores(0)
            for c in range(TT):
                tok = slice(c * P, (c + 1) * P)
                n = 8 * c
                pe.wait_ge(S("ug"), c + 1)
                for h in range(4):
                    mm = pe.matmul(bank[3][:, h * P:(h + 1) * P], ones[:], G["ug"][:, h, :], start=True, stop=True)
                mm.then_inc(S("gr"), 1)
                if c:
                    pe.wait_ge(S("o_ev"), c)
                    pe.wait_ge(S("st_upd"), c)
                else:
                    pe.wait_ge(S("l2_rs"), 8)
                    pe.wait_ge(S("l2_done"), 8)
                for h in range(4):
                    pe.matmul(bank[4][:, h * P:(h + 1) * P], qkv[:, 4 + h, tok], qkv[:, 4 + h, tok], start=True, stop=True)
                for h in range(4):
                    pe.matmul(bank[5][:, h * P:(h + 1) * P], qkv[:, 4 + h, tok], qkv[:, h, tok], start=True, stop=True)
                for h in range(4):
                    mm = pe.transpose(bank[6][:, h * P:(h + 1) * P], qkv[:, 8 + h, tok], ident[:])
                mm.then_inc(S("kk"), 1)
                attention_tail(n)
                pe.wait_ge(S("eex"), c + 1)
                for h in range(4):
                    mm = pe.transpose(bank[3][:, h * P:(h + 1) * P], qkv[:, 4 + h, tok], ident[:])
                mm.then_inc(S("vk"), 1)
                pe.wait_ge(S("x1"), c + 1)
                for h in range(4):
                    mm = pe.transpose(bank[4][:, h * P:(h + 1) * P], G["xt"][:, h, :], ident[:])
                mm.then_inc(S("x1T"), 1)
                scores(n + 1)
                modulation(n)
                for l in range(1, 7):
                    q = 6 * c + l
                    n = 8 * c + l
                    pe.wait_ge(S("m_rdy"), q)
                    if l == 1:
                        pe.wait_ge(S("x1e"), c + 1)
                        pe.wait_ge(S("gkv"), c + 1)
                    else:
                        pe.wait_ge(S("xx_upd"), 5 * c + l - 1)
                    for h in range(4):
                        mm = pe.matmul(bank[3][:, h * P:(h + 1) * P], G["m%d" % (l % 2)][:, h, :], G["xx"][:, h, :],
                                       start=True, stop=True)
                    mm.then_inc(S("T"), 1)
                    modulation(n)
                    attention_tail(n)
                    pe.wait_ge(S("Te"), q)
                    if l > 1:
                        pe.wait_ge(S("x_upd"), q - 1)
                    if l < 6:
                        for h in range(4):
                            mm = pe.matmul(bank[4][:, h * P:(h + 1) * P], G["xt"][:, h, :], G["tt"][:, h, :], start=True, stop=True)
                        mm.then_inc(S("XA"), 1)
                    for h in range(4):
                        mm = pe.matmul(bank[5][:, h * P:(h + 1) * P], G["tt"][:, h, :], G["xt"][:, h, :], start=True, stop=True)
                    mm.then_inc(S("XX"), 1)
                    scores(n + 1)
                n = 8 * c + 7
                pe.wait_ge(S("x_upd"), 6 * c + 6)
                for h in range(4):
                    pe.matmul(bank[6][:, h * P:(h + 1) * P], G["xt"][:, h, :], G["vtok"][:, h, :], start=True, stop=True)
                for h in range(4):
                    mm = pe.matmul(bank[5][:, h * P:(h + 1) * P], G["gk"][:, h, :], G["xt"][:, h, :], start=True, stop=True)
                mm.then_inc(S("uw"), 1)
                attention_tail(n)
                pe.wait_ge(S("uwe"), c + 1)
                if c:
                    for h in range(4):
                        mm = pe.matmul(bank[3][:, h * P:(h + 1) * P], G["wkT"][:, h, :], G["st"][:, h, :], start=True, stop=True)
                    mm.then_inc(S("PS"), 1)
                pe.wait_ge(S("u"), c + 1)
                for h in range(4):
                    o = bank[4][:, h * P:(h + 1) * P]
                    if c:
                        pe.matmul(o, G["st"][:, h, :], G["qdec"][:, h, :], start=True, stop=False)
                    mm = pe.matmul(o, G["u"][:, h, :], G["at_"][:, h, :], start=(c == 0), stop=True)
                mm.then_inc(S("o"), 1)
                if c < TT - 1:
                    for h in range(4):
                        mm = pe.matmul(bank[5][:, h * P:(h + 1) * P], G["kend"][:, h, :], G["u"][:, h, :], start=True, stop=True)
                    mm.then_inc(S("ds"), 1)
                if c < TT - 1:
                    scores(n + 1)
                modulation(n)
            attention_tail(32)
            weigh(7)
            assert units[pos[0]]["lin"]
            pe.wait_ge(S("o_ev"), TT)
            for i in range(8, 12):
                col_sum(i)

            def mixed(u, k):
                if k < 4:
                    pe.wait_ge(S("oa_lo"), k + 1)
            pe.wait_ge(S("ob_lo"), 4)
            assert units[pos[0]]["w"] == "w_out"
            unit(units[pos[0]], mixed, ks=[4, 5, 6, 7, 0, 1, 2, 3])
            pos[0] += 1
            for n in range(1, KT):
                units_to(T_OUT + n)
                sum_mm(KT + n - 1, n - 1)
            sum_mm(2 * KT - 1, KT - 1)
            pairs = 0
            for r, (t0, t1_) in enumerate(ffn_tiles):
                for j in range(len(ROUND[r])):
                    units_to(t0 + 2 * j + 1, ("h_ready", KT) if r == 0 and j == 0 else None)
                    if r == 1:
                        if j == 0:
                            pe.wait_ge(S("ctx_in"), 16)
                        if j >= 2:
                            pe.wait_ge(S("cx_ev"), j - 1)
                        for a in range(2):
                            mm = pe.transpose(bank[4 + j % 2][:, a * P:(a + 1) * P], ctxtok[:, a, j * P:(j + 1) * P], ident[:])
                        mm.then_inc(S("cx_T"), 1)
                        if j:
                            sum_mm(2 * KT + j - 1, j - 1, CT)
                if r < 2:
                    units_to(t1_, ("flo", pairs))
                    if r == 1:
                        sum_mm(3 * KT - 1, KT - 1, CT)
                    units_to(t1_ + KT - 1)
                else:
                    for n in range(KT):
                        units_to(t1_ + n, ("flo", pairs) if n == 0 else None)
                        for k in ([n - 1] if n else []) + ([n] if n == KT - 1 else []):
                            sum_mm(3 * KT + 2 * k, k)
                            sum_mm(3 * KT + 2 * k + 1, k, b=4)
                pairs += len(ROUND[r])

            def turn_values(h):
                tv = T_HG + 5 * h + 3
                pe.wait_ge(S(evac_name(tv)), tv // NLIN + 1)
                if h:
                    pe.wait_ge(S("osq"), h)
                    pe.wait_ge(S("y_pre"), h)
                for a in range(TT):
                    mm = pe.transpose(bank[6][:, a * P:(a + 1) * P], vT[:, a * P:(a + 1) * P], ident[:])
                mm.then_inc(S("b6"), 1)
                yield
                pe.wait_ge(S("kq_rdy"), h + 1)
                pe.wait_ge(S("b6e"), 4 * h + 1)
                for a in range(4):
                    mm = pe.transpose(bank[6][:, a * P:(a + 1) * P], kcx[:, a // 2, (a % 2) * P:(a % 2 + 1) * P], ident[:])
                mm.then_inc(S("b6"), 1)
                yield
                pe.wait_ge(S("b6e"), 4 * h + 2)
                for a in range(2):
                    mm = pe.transpose(bank[6][:, a * P:(a + 1) * P], vcT[:, 0, a * P:(a + 1) * P], ident[:])
                mm.then_inc(S("b6"), 1)
                yield
                pe.wait_ge(S("b6e"), 4 * h + 3)
                for dr in range(2):
                    for a in range(2):
                        mm = pe.matmul(bank[6][:, dr * P:(dr + 1) * P], ctok[:, 0, (2 * dr + a) * P:(2 * dr + a + 1) * P],
                                       st2[:, CT + a * P:CT + (a + 1) * P], start=(a == 0), stop=(a == 1))
                mm.then_inc(S("b6"), 1)

            def level(h, li):
                prod = min(li, 9)
                pe.wait_ge(S("lv_rdy"), 10 * h + prod + 1)
                if 11 * h + li >= 2:
                    pe.wait_ge(S("lv_ev%d" % (li % 2)), (6 if li % 2 == 0 else 5) * h + li // 2)
                b = bank[4 + li % 2]
                kc, qc = KC[:, prod % 2, :], QC[:, prod % 2, :]
                if li <= 7:
                    for a in range(TT):
                        mm = pe.matmul(b[:, a * P:(a + 1) * P], kc[:, a * P:(a + 1) * P], qc[:, a * P:(a + 1) * P],
                                       start=True, stop=True)
                elif li == 8:
                    for a in range(TT):
                        o = a ^ 1
                        mm = pe.matmul(b[:, a * P:(a + 1) * P], kc[:, a * P:(a + 1) * P], qc[:, o * P:(o + 1) * P],
                                       start=True, stop=True)
                else:
                    for i in range(2):
                        a = 2 * (li - 9) + i
                        o = 256 * (1 - a // 2)
                        mm = pe.matmul(b[:, i * 256:(i + 1) * 256], kc[:, a * P:(a + 1) * P], qc[:, o:o + 256],
                                       start=True, stop=True)
                mm.then_inc(S("lv_mm"), 1)

            def output(h):
                pe.wait_ge(S("b6e"), 4 * h + 4)
                pe.wait_ge(S("lv_ev0"), 6 * h + 6)
                pe.wait_ge(S("lv_ev1"), 5 * h + 5)
                pe.wait_ge(S("qp_rdy"), h + 1)
                for a in range(TT):
                    pe.matmul(bank[6][:], vt[:, a * P:(a + 1) * P], MT[:, a, :], start=(a == 0), stop=False)
                for dr in range(2):
                    mm = pe.matmul(bank[6][:], st2[:, dr * P:(dr + 1) * P], QQ[:, dr, :], start=False, stop=(dr == 1))
                mm.then_inc(S("o_mm"), 1)

            def meansq(h):
                pe.wait_ge(S("osq"), h + 1)
                pe.matmul(bank[3][0:HG, :], onecol[:, 15 - h:31 - h], vcT[:, 1, :], start=(h == 0), stop=(h == HG - 1)
                          ).then_inc(S("ms_mm"), 1)

            def scan(g):
                if g >= 1:
                    meansq(g - 1)
                yield from turn_values(g)
                for li in range(11):
                    level(g, li)
                    yield
                output(g)
                yield

            for h in range(HG + 1):
                steps = scan(h - 1) if h else iter(())
                if h < HG:
                    t = T_HG + 5 * h
                    units_to(t, ("h_ready", 3 * KT) if h == 0 else None)
                    for i in range(1, 5):
                        next(steps, None)
                        units_to(t + i, None, steps)
                for _ in steps:
                    pass
            meansq(HG - 1)
            pe.wait_ge(S("rs16"), 1)
            for h in range(HG):
                if h >= 2:
                    pe.wait_ge(S("y_norm"), h - 1)
                pe.matmul(bank[4 + h % 2][:], bass.AP(tensor=ident[:].tensor, offset=h, ap=[[P, HG], [0, P]]),
                          rs[0:HG, :], start=True, stop=True).then_inc(S("rs_row"), 1)
            def heads_in(u, k):
                pe.wait_ge(S("y_lo"), k + 1 + (8 if u["x"] == "g" else 0))
            for n in range(KT):
                t = T_HO + n
                for _ in range(2):
                    unit(units[pos[0]], heads_in if n == 0 else None)
                    pos[0] += 1
                if n:
                    sum_mm(5 * KT + n - 1, n - 1)
            sum_mm(6 * KT - 1, KT - 1)

            for gi in range(GROUPS):
                t = ft_tiles[gi // 4] + 4 * (gi % 4)
                units_to(t + 1, ("h_ready", 4 * KT) if gi == 0 else None)
                units_to(t + 2)
                pe.wait_ge(S(evac_name(t + 1)), (t + 1) // NLIN + 1)
                pe.wait_ge(S("dft_in"), 32)
                if gi:
                    pe.wait_ge(S("ab_ev"), 2 * gi)
                for a in range(TT):
                    for c in range(2):
                        mm = pe.matmul(bank[4 + a // 2][:, (a % 2) * GDIM:(a % 2 + 1) * GDIM], uT[:, c, a * P:(a + 1) * P],
                                       dch[:, c, :], start=(c == 0), stop=(c == 1))
                mm.then_inc(S("ab_mm"), 1)
                units_to(t + 3)
                pe.wait_ge(S("ab_ev"), 2 * gi + 2)
                for g in range(2):
                    if gi:
                        pe.wait_ge(S("y_ev"), 2 * (gi - 1) + g + 1)
                    b = bank[6 + g]
                    for a in range(TT):
                        pe.matmul(b[:, 0:257], AB[:, a, g * P:(g + 1) * P], dtok[:, a, 0:257], start=(a == 0), stop=(a == TT - 1))
                    for a in range(TT):
                        mm = pe.matmul(b[:, 257:512], AB[:, a, GDIM + g * P:GDIM + (g + 1) * P], dtok[:, a, 257:512],
                                       start=(a == 0), stop=(a == TT - 1))
                    mm.then_inc(S("y_mm"), 1)
                if gi % 4 == 3:
                    def mixed_in(u, k):
                        if k >= 6:
                            pe.wait_ge(S("yg_lo"), 2 * gi + k - 5)
                    if gi < 4:
                        units_to(t + 4, mixed_in)
                        units_to(t + 4 + KT - 1)
                    else:
                        residual_units(t + 4, lambda k: sum_mm(6 * KT + k, k), mixed_in)
            assert pos[0] == len(units)
            for half in range(2):
                pe.wait_ge(S("x_final"), 4 * half + 4)
                for a in range(TT):
                    i = TT * half + a
                    if i >= 2:
                        pe.wait_ge(S("out_ready"), i - 1)
                    for k in range(4):
                        mm = pe.transpose(bank[4 + i % 2][:, k * P:(k + 1) * P],
                                          xT[:, 4 * half + k, a * P:(a + 1) * P], ident[:])
                    mm.then_inc(S("out_ps"), 1)

        @block.scalar
        def _(act):
            do = Own(act, "act_chain")
            A = nc.scalar

            def high(l):
                if l >= n_lin:
                    return
                u = lin_units[l]
                act.wait_ge(S(f"stage_in{u['slot']}"), 16 * (u["load"] + 1))
                if l >= NSPLIT:
                    act.wait_ge(S("unit_done"), l - NSPLIT + 1)
                nk = u["rows"][1]
                do(A.activation(wh[:, l % NSPLIT, 0:nk, :], stage[:, u["slot"], 0:nk, :], ACT.Copy), "hi_ready")

            def finish_tile(t):
                for l in tiles[t]:
                    if l + NSPLIT < tiles[T_OUT][0] or l >= tiles[T_OUT][0]:
                        high(l + NSPLIT)
                act.wait_ge(S("unit_done"), tile_last(t) + 1)

            def evac(t, ins):
                do(ins, evac_name(t), t // NLIN + 1)

            def square(j, src, name, value, width=T, scale=1.0):
                if j >= 2:
                    act.wait_ge(S("sq_used"), j - 1)
                act.wait_ge(S(name), value)
                do(A.activation(sq[:, j % 2, 0:width], src, ACT.Square, scale=scale), "sq_ready")

            def root(dst, src, width=T, ready="sq_used", value=None):
                do(A.activation(small[:, 252:253], halfeps, ACT.Ln))
                act.wait_ge(S(ready), value)
                do(A.activation(dst[:, 0:width], src[:, 0:width], ACT.Ln, scale=1.0 / D, bias=halfeps))
                do.settle()
                do(A.activation(dst[:, 0:width], dst[:, 0:width], ACT.Exp, scale=-0.5), "rs_ready")

            def split_high(m, dst, width=T, shift=None, k=None):
                for k in range(KT) if k is None else [k]:
                    act.wait_ge(S("hf_ready"), KT * m + k + 1)
                    if shift:
                        do(A.activation(dst[:, k, :], hf[:, k % 2, 0:width], ACT.Identity, bias=shift(k)), "hh_ready")
                    else:
                        do(A.activation(dst[:, k, :], hf[:, k % 2, 0:width], ACT.Copy), "hh_ready")

            def residual_tiles(t0, j0):
                for n in range(KT):
                    finish_tile(t0 + n)
                    square(j0 + n, xT[:, n, :], evac_name(t0 + n), (t0 + n) // NLIN + 1)

            def col_roots(i, eps_scale, between):
                for n in (i, i + 1):
                    act.wait_ge(S("l2_sum"), n + 1)
                    if n >= 2:
                        act.wait_ge(S("l2_done"), n - 1)
                    do(A.activation(hf[:, n % 2, :], bank[4 + n % 2][:], ACT.Ln, scale=eps_scale, bias=halfeps), "l2_ln")
                between()
                for n in (i, i + 1):
                    act.wait_ge(S("l2_ln"), n + 1)
                    do(A.activation(hf[:, n % 2, :], hf[:, n % 2, :], ACT.Exp, scale=-0.5), "l2_rs")

            def col_square(i, src):
                if i >= 2:
                    act.wait_ge(S("l2_sum"), i - 1)
                do(A.activation(sq[:, i % 2, :], src, ACT.Square), "l2_sq")

            act.wait_ge(S("rows_T"), 1)
            do(A.activation(V[:, 0:NROWS], bank[4][:, 0:NROWS], ACT.Copy), "V_ready")
            do.settle()
            act.wait_ge(S("const_set"), 2)
            for k in range(KT):
                square(k, xT[:, k, :], "xT_ev", k + 1)
            for l in range(NSPLIT):
                high(l)
            root(rs, bank[3], value=KT)
            split_high(0, hh)
            act.wait_ge(S("lb_diff"), 2)
            do(A.activation(lb, lb, ACT.Exp))
            do(A.activation(oml, oml, ACT.Exp), "lb_exp")

            def silu_conv(t):
                act.wait_ge(S("conv_done"), t + 1)
                do(A.activation(qkv[:, t, :], hf[:, t % 2, :], ACT.Silu), "silu_done")
            do(A.activation(silc[:, 0:16:2], V[:, ROWS["c"][0]:ROWS["c"][0] + 8], ACT.Silu), "silc_ready")
            do(A.activation(silc[:, 1:16:2], V[:, ROWS["c_ctx"][0]:ROWS["c_ctx"][0] + 8], ACT.Silu), "silc_ready")
            def square_pair(i, last):
                if i < last:
                    for n in (i, i + 1):
                        col_square(n, qkv[:, n, :] if n < 8 else oT[:, n - 8, :])
            for t in range(28):
                finish_tile(t)
                if t < 12:
                    if t == 0:
                        act.wait_ge(S("raw_zero"), 1)
                    if t >= 2:
                        act.wait_ge(S("conv_done"), t - 1)
                    evac(t, A.activation(raw[:, t % 2, 3:3 + T], bank[t % NLIN][:], ACT.Copy))
                elif t < 16:
                    evac(t, A.activation(zT[:, t - 12, :], bank[t % NLIN][:], ACT.Silu))
                else:
                    evac(t, A.activation(bqkv[:, t - 16, :], bank[t % NLIN][:], ACT.Copy))
                if 1 <= t <= 12:
                    silu_conv(t - 1)
                if t == 15:
                    act.wait_ge(S("silu_done"), 12)
                    square_pair(0, 8)
                if t in range(16, 24, 2):
                    col_roots(t - 16, 1.0, lambda: square_pair(t - 14, 8))
                if t == 14:
                    act.wait_ge(S("cst_in"), 8 * 16)
                    do(A.activation(w8h[:], w8[:], ACT.Copy), "w8_hi")
                if t == 23:
                    act.wait_ge(S("ba_T"), 1)
                    do(A.activation(rs[0:8, :], bank[3][0:8, :], ACT.Copy), "ba_ev")
                if t == 24:
                    act.wait_ge(S("ba_ready"), 1)
                    b3 = bank[3][:, 0:32].rearrange("p (a c) -> p a c", c=8)
                    do(A.activation(beta.rearrange("p (a c) -> p a c", c=4), b3[:, :, 0:4], ACT.Sigmoid))
                    do(A.activation(ab[:, 4:8], bank[3][:, 68:72], ACT.Copy))
                    do(A.activation(ab[:, 0:4], bank[3][:, 64:68], ACT.Exp), "ba_act")
                if t == 25:
                    act.wait_ge(S("sp_abs"), 1)
                    do(A.activation(t2[:, 16:32], t2[:, 16:32], ACT.Exp, scale=-1.0))
                    do.settle()
                    do(A.activation(t2[:, 16:32], t2[:, 16:32], ACT.Ln, bias=1.0), "sp_ln")
                if t == 27:
                    act.wait_ge(S("gc_ps"), 1)
                    do(A.activation(gcc, bank[3][:, 80:96], ACT.Copy))
                    do(A.activation(egc, bank[3][:, 80:96], ACT.Exp), "gcc_ready")
            for a in range(TT):
                act.wait_ge(S("vb_T"), a + 1)
                do(A.activation(bqkv[:, 8:12, a * P:(a + 1) * P], bank[1 + a % 2][:].rearrange("p (j c) -> p j c", c=P), ACT.Copy), "vb_ev")

            def weights(n):
                w = (n % 4 + 1) * P
                act.wait_ge(S("nmx_ready"), n + 1)
                do(A.activation(sm[:, n % 2, 0:w], sm[:, n % 2, 0:w], ACT.Exp, bias=nmx[:, n:n + 1]), "pexp")

            def place(n):
                h, i = n // 4, n % 4
                act.wait_ge(S("pT_done"), n + 1)
                if h >= 2:
                    act.wait_ge(S("pv_done"), h - 1)
                do(A.activation(pT[:, h % 2, 0:i + 1, i * P:(i + 1) * P],
                                bank[1][:, 0:(i + 1) * P].rearrange("p (j c) -> p j c", c=P), ACT.Copy), "pT_ev")

            def attention_tail(n):
                if n > 8 and n % 8 == 1:
                    pair_high(n // 8 - 1)
                if n:
                    place(n - 1)

            def pair_high(hp):
                act.wait_ge(S("pv_done"), 2 * hp + 2)
                do(A.activation(gh[:, 4 + hp, :], bank[2][:], ACT.Copy), "ob_hi")

            def heads4(b):
                return b[:].rearrange("p (h c) -> p h c", c=P)

            for c in range(TT):
                tok = slice(c * P, (c + 1) * P)
                act.wait_ge(S("dif"), c + 1)
                do(A.activation(G["ee"][:], G["ee"][:], ACT.Exp))
                do(A.activation(G["eg"][:], heads4(bank[3]), ACT.Exp))
                do(A.activation(kec[:, 4 * c:4 * c + 4], kec[:, 4 * c:4 * c + 4], ACT.Exp), "eex")
                attention_tail(8 * c)
                weights(8 * c)
                act.wait_ge(S("x1T"), c + 1)
                do(A.activation(G["xx"][:], heads4(bank[4]), ACT.Copy), "x1e")
                for l in range(1, 7):
                    act.wait_ge(S("T"), 6 * c + l)
                    do(A.activation(G["tt"][:], heads4(bank[3]), ACT.Copy), "Te")
                    attention_tail(8 * c + l)
                    weights(8 * c + l)
                act.wait_ge(S("uw"), c + 1)
                do(A.activation(G["u"][:], heads4(bank[6]), ACT.Copy))
                do(A.activation(G["wkT"][:], heads4(bank[5]), ACT.Copy), "uwe")
                attention_tail(8 * c + 7)
                weights(8 * c + 7)
                act.wait_ge(S("o"), c + 1)
                do(A.activation(oT[:, :, tok], heads4(bank[4]), ACT.Copy), "o_ev")
            attention_tail(32)
            pair_high(3)
            for l in range(tiles[T_OUT][0], tiles[T_OUT][0] + NSPLIT):
                high(l)
            do.settle()
            square_pair(8, 12)
            for i in range(8, 12, 2):
                col_roots(i, 1.0 / P, lambda: square_pair(i + 2, 12))
            for h in range(4):
                act.wait_ge(S("oa"), h + 1)
                do(A.activation(gh[:, h, :], oT[:, h, :], ACT.Copy), "oa_hi")

            residual_tiles(T_OUT, KT)
            root(rs, bank[3], value=2 * KT)
            split_high(1, hh)
            p = 0
            for r, (t0, t1_) in enumerate(ffn_tiles):
                for j in range(len(ROUND[r])):
                    for half in range(2):
                        t = t0 + 2 * j + half
                        finish_tile(t)
                        if p == 0:
                            act.wait_ge(S("fraw_zero"), 1)
                        if p >= 2:
                            act.wait_ge(S("fconv"), 2 * p - 2)
                        evac(t, A.activation(fraw[:, 2 * (p % 2) + half, 2:2 + T], bank[t % NLIN][:], ACT.Copy))
                    act.wait_ge(S("fconv"), 2 * p + 1)
                    do(A.activation(fg[:, p % 2, :], facc[:, 2 * (p % 2), :], ACT.Silu), "fsilu")
                    act.wait_ge(S("fprod"), p + 1)
                    do(A.activation(gh[:, j, :], facc[:, 2 * (p % 2) + 1, :], ACT.Copy), "fhi")
                    p += 1
                    if r == 1:
                        act.wait_ge(S("cx_T"), j + 1)
                        do(A.activation(craw[:, j, :], bank[4 + j % 2][:, 0:CT], ACT.Copy), "cx_ev")
                        square(2 * KT + j, craw[:, j, :], "cx_ev", j + 1, CT)
                for n in range(KT):
                    finish_tile(t1_ + n)
                    if r == 1 and n == 0:
                        root(rs, bank[3], CT, value=3 * KT)
                    if r == 1:
                        split_high(2, ch, CT, shift(0, 1), n)
                    if r == 2:
                        done = (evac_name(t1_ + n), (t1_ + n) // NLIN + 1)
                        square(3 * KT + 2 * n, xT[:, n, :], *done)
                        square(3 * KT + 2 * n + 1, xT[:, n, :], *done, scale=vcol("final1", n))
            root(rs, bank[3], value=5 * KT)
            root(rs2, rs2, ready="x1_square", value=1)
            split_high(3, hh, T, shift(0, 0))

            def aux_early(g):
                act.wait_ge(S("b6"), 4 * g + 1)
                do(A.activation(vt[:], bank[6][:], ACT.Copy), "b6e")
                act.wait_ge(S("b6"), 4 * g + 2)
                do(A.activation(ctok[:, 0, :], bank[6][:], ACT.Copy), "b6e")
                act.wait_ge(S("b6"), 4 * g + 3)
                do(A.activation(st2[:, CT:2 * CT], bank[6][:, 0:CT], ACT.Copy), "b6e")

            def aux_states(g):
                act.wait_ge(S("b6"), 4 * g + 4)
                do(A.activation(st2[:, 0:CT], bank[6][:, 0:CT], ACT.Copy), "b6e")

            def place_level(g, li):
                act.wait_ge(S("lv_mm"), 11 * g + li + 1)
                b = bank[4 + li % 2]
                if li == 8:
                    src = view(b[:], [[2 * P, 2], [P, 2], [1, P]])
                    dst = view(MT[:, 0, 0:1], [[2 * T + 2 * P, 2], [T - P, 2], [1, P]], P)
                else:
                    a = 2 * (li - 9)
                    src = b[:].rearrange("p (i c) -> p i c", i=2)
                    dst = MT[:, a:a + 2, 256 * (10 - li):256 * (10 - li) + 256]
                do(A.activation(dst, src, ACT.Copy), "lv_ev%d" % (li % 2), (6 if li % 2 == 0 else 5) * g + li // 2 + 1)

            for h in range(HG + 1):
                t = T_HG + 5 * h
                if h < HG:
                    finish_tile(t)
                    if h:
                        act.wait_ge(S("sgt_q"), h)
                    do(A.activation(sgt[:, 0, :], bank[t % NLIN][:], ACT.Sigmoid), "sg_q")
                if h:
                    aux_early(h - 1)
                if h == HG:
                    aux_states(h - 1)
                if h < HG:
                    for dr in range(2):
                        finish_tile(t + 1 + dr)
                        if h:
                            act.wait_ge(S("sgf_used"), h)
                            act.wait_ge(S("kq_rdy"), h)
                        do(A.activation(sgc[:, dr, :], bank[7][:, dr * CT:(dr + 1) * CT], ACT.Sigmoid), "cevac")
                        evac(t + 1 + dr, A.activation(sgf[:, dr, :], bank[(t + 1 + dr) % NLIN][:], ACT.Sigmoid))
                        if h and dr == 0:
                            aux_states(h - 1)
                    finish_tile(t + 3)
                    if h:
                        act.wait_ge(S("b6"), 4 * h)
                    do(A.activation(vcT[:, 0, 0:CT], bank[7][:, 0:CT], ACT.Copy), "cevac")
                    do(A.activation(vT[:], bank[(t + 3) % NLIN][:], ACT.Copy), evac_name(t + 3), (t + 3) // NLIN + 1)
                if h:
                    place_level(h - 1, 8)
                if h:
                    place_level(h - 1, 9)
                    place_level(h - 1, 10)
                if h < HG:
                    finish_tile(t + 4)
                    if h:
                        act.wait_ge(S("sz_rdy"), h)
                    do(A.activation(sgt[:, 1, :], bank[(t + 4) % NLIN][:], ACT.Sigmoid), "sg_z")
                if h:
                    act.wait_ge(S("o_mm"), h)
                    if h >= 2:
                        act.wait_ge(S("ms_mm"), h - 1)
                    do(A.activation(vcT[:, 1, :], bank[6][:], ACT.Square), "osq")
            act.wait_ge(S("ms_mm"), HG)
            do(A.activation(rs[0:HG, :], bank[3][0:HG, :], ACT.Ln, scale=1.0 / P, bias=halfeps[0:HG, :]))
            do.settle()
            do(A.activation(rs[0:HG, :], rs[0:HG, :], ACT.Exp, scale=-0.5), "rs16")
            for h in range(HG):
                act.wait_ge(S("y_norm"), h + 1)
                src = yA[:, h, :] if h < 8 else yB[:, h - 8, :]
                dst = hh[:, h, :] if h < 8 else gh[:, h - 8, :]
                do(A.activation(dst, src, ACT.Copy), "y_hi")
            residual_tiles(T_HO, 5 * KT)
            root(rs, bank[3], value=6 * KT)
            split_high(4, hh, T, shift(1, 0))

            for gi in range(GROUPS):
                t = ft_tiles[gi // 4] + 4 * (gi % 4)
                for c in range(2):
                    finish_tile(t + c)
                    if gi:
                        act.wait_ge(S("ab_mm"), gi)
                    do(A.activation(uT[:, c, :], bank[(t + c) % NLIN][:], ACT.Copy), evac_name(t + c), (t + c) // NLIN + 1)
                def z_gate(c):
                    finish_tile(t + 2 + c)
                    if gi:
                        act.wait_ge(S("zs_rdy"), 2 * gi)
                    do(A.activation(zsg[:, c, :], bank[(t + 2 + c) % NLIN][:], ACT.Sigmoid), "zsg")
                z_gate(0)
                act.wait_ge(S("ab_mm"), gi + 1)
                if gi:
                    act.wait_ge(S("y_mm"), 2 * gi)
                else:
                    act.wait_ge(S("ab_zero"), 2)
                for i in range(2):
                    src, dst = bank[4 + i], AB[:, 2 * i, 0:1]
                    do(A.activation(view(dst, [[T, 2], [1, 129]]), view(src[:, 0:1], [[GDIM, 2], [1, 129]]), ACT.Copy))
                    do(A.activation(view(dst, [[T, 2], [1, 127]], 129), view(src[:, 0:1], [[GDIM, 2], [-1, 127]], 127), ACT.Copy))
                    do(A.activation(view(dst, [[T, 2], [1, 127]], GDIM + 1), view(src[:, 0:1], [[GDIM, 2], [1, 127]], 129), ACT.Copy),
                       "ab_act")
                z_gate(1)
                for g in range(2):
                    act.wait_ge(S("y_mm"), 2 * gi + g + 1)
                    if gi:
                        act.wait_ge(S("yf_rdy"), 2 * gi + g - 1)
                    do(A.activation(qsn[:, g, 0:255], bank[6 + g][:, 257:512], ACT.Copy), "qsn")
                for g in range(2):
                    act.wait_ge(S("yg_rdy"), 2 * gi + g + 1)
                    do(A.activation(gh[:, 2 * (gi % 4) + g, :], yg[:, g, :], ACT.Copy), "yg_hi")
                if gi == 3:
                    for n in range(KT):
                        finish_tile(t + 4 + n)
            residual_tiles(len(tiles) - KT, 6 * KT)
            root(rs, bank[3], value=7 * KT)
            for i in range(2 * TT):
                act.wait_ge(S("out_ps"), i + 1)
                do(A.activation(otok[:, i % TT, (i // TT) * 512:(i // TT + 1) * 512], bank[4 + i % 2][:], ACT.Copy), "out_ready")

        @block.vector
        def _(dve):
            do = Own(dve, "dve_chain")
            X = nc.vector

            def evac(t, ins):
                do(ins, evac_name(t), t // NLIN + 1)

            def finish_tile(t):
                dve.wait_ge(S("unit_done"), tile_last(t) + 1)

            def scaled(k, width, src, coef, r):
                do(X.scalar_tensor_tensor(hf[:, k % 2, 0:width], src[:, k, :], coef(k), r[:, 0:width], ALU.mult, ALU.mult),
                   "hf_ready")

            def low(k, m, width, shift, dst_hi, dst_lo):
                dve.wait_ge(S("hh_ready"), KT * m + k + 1)
                if shift:
                    ins = X.scalar_tensor_tensor(dst_lo[:, k, :], hf[:, k % 2, 0:width], shift(k), dst_hi[:, k, :].bitcast(F32),
                                                 ALU.add, ALU.subtract)
                else:
                    ins = X.tensor_tensor(dst_lo[:, k, :], hf[:, k % 2, 0:width], dst_hi[:, k, :].bitcast(F32), ALU.subtract)
                do(ins, "h_ready")

            def norm(n, m, width, src, coef, shift, dst_hi, dst_lo):
                dve.wait_ge(S("rs_ready"), n + 1)
                for k in range(KT):
                    do.settle()
                    scaled(k, width, src, coef, rs)
                    if k:
                        low(k - 1, m, width, shift, dst_hi, dst_lo)
                low(KT - 1, m, width, shift, dst_hi, dst_lo)

            def residual(t, n, gate=None):
                finish_tile(t)
                if gate is None:
                    evac(t, X.tensor_tensor(xT[:, n, :], xT[:, n, :], bank[t % NLIN][:], ALU.add))
                else:
                    evac(t, X.scalar_tensor_tensor(xT[:, n, :], bank[t % NLIN][:], gate(n), xT[:, n, :], ALU.mult, ALU.add))

            do(X.memset(ones[:], 1.0), "const_set")
            do(X.memset(halfeps, EPS), "const_set")
            for k in range(KT):
                dve.wait_ge(S("xT_ps"), k + 1)
                do(X.tensor_copy(xT[:, k, :], bank[k % 2][:]), "xT_ev")
            dve.wait_ge(S("V_ready"), 1)
            L0 = V[:, ROWS["lb0"][0]:ROWS["lb0"][0] + 32]
            L1 = V[:, ROWS["lb1"][0]:ROWS["lb1"][0] + 32]
            mxl = small[:, 192:224]
            do(X.tensor_tensor(mxl, L0, L1, ALU.max))
            do.settle()
            do(X.tensor_tensor(lb, L0, mxl, ALU.subtract), "lb_diff")
            do(X.tensor_tensor(oml, L1, mxl, ALU.subtract), "lb_diff")
            norm(0, 0, T, xT, lambda k: vcol("norm1", k), None, hh, hl)
            dve.wait_ge(S("lb_exp"), 1)
            do.settle()
            do(X.tensor_tensor(mxl, lb, oml, ALU.add))
            do.settle()
            do(X.reciprocal(mxl, mxl))
            do.settle()
            do(X.tensor_tensor(lb, lb, mxl, ALU.mult))
            do.settle()
            do(X.tensor_scalar(oml, lb, -1.0, 1.0, ALU.mult, ALU.add))

            do(X.memset(raw[:, :, 0:3], 0.0), "raw_zero")
            for t in range(12):
                dve.wait_ge(S(evac_name(t)), t // NLIN + 1)
                if t >= 2:
                    dve.wait_ge(S("silu_done"), t - 1)
                a, r = hf[:, t % 2, :], raw[:, t % 2, :]
                do(X.tensor_scalar(a, r[:, 0:T], vcol("conv", t), None, ALU.mult))
                for i in range(1, 4):
                    do.settle()
                    do(X.scalar_tensor_tensor(a, r[:, i:i + T], vcol("conv", 12 * i + t), a, ALU.mult, ALU.add),
                       "conv_done" if i == 3 else None)
            dve.wait_ge(S("w8_hi"), 1)
            do(X.tensor_tensor(w8l[:], w8[:], w8h[:].bitcast(F32), ALU.subtract), "w8_lo")
            for i in range(8):
                dve.wait_ge(S("l2_rs"), i + 1)
                do(X.scalar_tensor_tensor(qkv[:, i, :], qkv[:, i, :], 128.0 ** -0.5 if i < 4 else 1.0, hf[:, i % 2, :],
                                          ALU.mult, ALU.mult), "l2_done")
            dve.wait_ge(S("ba_act"), 1)
            b3 = bank[3][:, 0:32].rearrange("p (a c) -> p a c", c=8)
            do(X.tensor_tensor(t2[:, 0:16].rearrange("p (a c) -> p a c", c=4), b3[:, :, 4:8],
                               view(ab, [[0, 4], [1, 4]], 4), ALU.add))
            do.settle()
            do(X.scalar_tensor_tensor(t2[:, 16:32], t2[:, 0:16], -1.0, t2[:, 0:16], ALU.mult, ALU.max), "sp_abs")
            dve.wait_ge(S("sp_ln"), 1)
            do.settle()
            do(X.scalar_tensor_tensor(t2[:, 16:32], t2[:, 0:16], 0.0, t2[:, 16:32], ALU.max, ALU.add))
            do.settle()
            do(X.scalar_tensor_tensor(ggc.rearrange("p (a c) -> p a c", c=4), t2[:, 16:32].rearrange("p (a c) -> p a c", c=4),
                                      -1.0, view(ab, [[0, 4], [1, 4]]), ALU.mult, ALU.mult), "g_ready")

            def front(n):
                w = (n % 4 + 1) * P
                dve.wait_ge(S("s_done"), n + 1)
                if n >= 2:
                    dve.wait_ge(S("p_ready"), n - 1)
                do(X.scalar_tensor_tensor(sm[:, n % 2, 0:w], bank[0][:, 0:w], 0.125, dneg[:, T - w:T],
                                          ALU.mult, ALU.add), "sm_ready")
                do.settle()
                do(X.tensor_reduce(mx[:, n:n + 1], sm[:, n % 2, 0:w], AX.X, ALU.max))
                do.settle()
                do(X.tensor_scalar(nmx[:, n:n + 1], mx[:, n:n + 1], -1.0, None, ALU.mult), "nmx_ready")

            def back(n):
                w = (n % 4 + 1) * P
                dve.wait_ge(S("pexp"), n + 1)
                if n >= 2:
                    dve.wait_ge(S("pT_done"), n - 1)
                do(X.tensor_tensor_reduce(pr[:, n % 2, 0:w], sm[:, n % 2, 0:w], dcnt[:, T - w:T], 1.0, 0.0, ALU.mult, ALU.add,
                                          den[:, n:n + 1]))
                do.settle()
                do(X.reciprocal(rden[:, n:n + 1], den[:, n:n + 1]))
                do.settle()
                do(X.tensor_scalar(pr[:, n % 2, 0:w], pr[:, n % 2, 0:w], rden[:, n:n + 1], None, ALU.mult), "p_ready")

            def pair_low(hp):
                dve.wait_ge(S("ob_hi"), hp + 1)
                do(X.tensor_tensor(gl[:, 4 + hp, :], bank[2][:], gh[:, 4 + hp, :].bitcast(F32), ALU.subtract), "ob_lo")

            def attention_tail(n):
                if n:
                    back(n - 1)
                if n > 8 and n % 8 == 2:
                    pair_low(n // 8 - 1)

            dve.wait_ge(S("gcc_ready"), 1)
            up = cst[:, 0:P]
            for c in range(TT):
                tok = slice(c * P, (c + 1) * P)
                if c:
                    dve.wait_ge(S("o_ev"), c)
                for h in range(4):
                    do(X.tensor_scalar(G["ug"][:, h, :], up, ggc[:, 4 * c + h:4 * c + h + 1], None, ALU.mult),
                       "ug" if h == 3 else None)
                dve.wait_ge(S("gr"), c + 1)
                for h in range(4):
                    do(X.tensor_scalar(G["ee"][:, h, :], bank[3][:, h * P:(h + 1) * P], gcc[:, 4 * c + h:4 * c + h + 1], 0.0,
                                       ALU.subtract, ALU.min))
                do(X.tensor_tensor(kec[:, 4 * c:4 * c + 4], view(bank[3][:, 0:1], [[P, 4]], P - 1), gcc[:, 4 * c:4 * c + 4],
                                   ALU.subtract), "dif")
                attention_tail(8 * c)
                front(8 * c)
                dve.wait_ge(S("eex"), c + 1)
                for h in range(4):
                    do(X.scalar_tensor_tensor(G["ee"][:, h, :], G["ee"][:, h, :], beta[:, 4 * c + h:4 * c + h + 1], up,
                                              ALU.mult, ALU.mult))
                do(X.tensor_tensor(kec[:, 4 * c:4 * c + 4], kec[:, 4 * c:4 * c + 4], beta[:, 4 * c:4 * c + 4], ALU.mult))
                do.settle()
                dve.wait_ge(S("kk"), c + 1)
                b4, b5 = (bank[i][:].rearrange("p (h c) -> p h c", c=P) for i in (4, 5))
                do(X.tensor_tensor(G["lt"][:], G["ee"][:], b4, ALU.mult))
                do(X.tensor_tensor(G["at_"][:], G["ee"][:], b5, ALU.mult))
                do.settle(1)
                do(X.tensor_tensor(G["m0"][:], G["lt"][:], view(gmask[:, 0, :], [[0, 4], [1, P]]), ALU.mult))
                do.settle()
                do(X.tensor_tensor(G["xt"][:], view(ident[:], [[0, 4], [1, P]]), G["m0"][:], ALU.subtract), "x1")
                dve.wait_ge(S("vk"), c + 1)
                for h in range(4):
                    i = 4 * c + h
                    do(X.tensor_scalar(G["gk"][:, h, :], bank[3][:, h * P:(h + 1) * P], egc[:, i:i + 1], None, ALU.mult))
                    do(X.tensor_scalar(G["kend"][:, h, :], bank[3][:, h * P:(h + 1) * P], kec[:, i:i + 1], None, ALU.mult))
                do(X.tensor_copy(G["vtok"][:], bank[6][:].rearrange("p (h c) -> p h c", c=P)), "gkv")
                do(X.tensor_tensor(G["m1"][:], G["lt"][:], view(gmask[:, 1, :], [[0, 4], [1, P]]), ALU.mult), "m_rdy")
                do(X.tensor_tensor(G["qdec"][:], qkv[:, 0:4, tok], G["eg"][:], ALU.mult))
                for l in range(1, 7):
                    attention_tail(8 * c + l)
                    front(8 * c + l)
                    if l < 6:
                        if l == 1:
                            dve.wait_ge(S("x1"), c + 1)
                        do(X.tensor_tensor(G["m%d" % ((l + 1) % 2)][:], G["lt"][:], view(gmask[:, l + 1, :], [[0, 4], [1, P]]),
                                           ALU.mult), "m_rdy")
                    if l < 6:
                        if l == 1:
                            dve.wait_ge(S("x1e"), c + 1)
                        dve.wait_ge(S("XA"), 5 * c + l)
                        do(X.tensor_tensor(G["xx"][:], G["xx"][:], b4, ALU.subtract), "xx_upd")
                    dve.wait_ge(S("XX"), 6 * c + l)
                    do(X.tensor_tensor(G["xt"][:], G["xt"][:], b5, ALU.subtract), "x_upd")
                attention_tail(8 * c + 7)
                front(8 * c + 7)
                dve.wait_ge(S("uwe"), c + 1)
                if c:
                    dve.wait_ge(S("PS"), c)
                    do(X.tensor_tensor(G["u"][:], G["u"][:], bank[3][:].rearrange("p (h c) -> p h c", c=P), ALU.subtract), "u")
                else:
                    do(X.tensor_copy(small[:, 250:251], small[:, 0:1]), "u")
                if c < TT - 1:
                    dve.wait_ge(S("ds"), c + 1)
                    if c == 0:
                        do(X.tensor_copy(G["st"][:], b5), "st_upd")
                    else:
                        for h in range(4):
                            do(X.scalar_tensor_tensor(G["st"][:, h, :], G["st"][:, h, :], G["eg"][:, h, P - 1:P],
                                                      bank[5][:, h * P:(h + 1) * P], ALU.mult, ALU.add),
                               "st_upd" if h == 3 else None)
            attention_tail(32)
            pair_low(3)
            for i in range(8, 12):
                h = i - 8
                dve.wait_ge(S("l2_rs"), i + 1)
                do(X.scalar_tensor_tensor(oT[:, h, :], oT[:, h, :], vcol("gdn_norm"), hf[:, i % 2, :], ALU.mult, ALU.mult), "l2_done")
                do.settle()
                do(X.tensor_tensor(oT[:, h, :], oT[:, h, :], zT[:, h, :], ALU.mult), "oa")
            for h in range(4):
                dve.wait_ge(S("oa_hi"), h + 1)
                do(X.tensor_tensor(gl[:, h, :], oT[:, h, :], gh[:, h, :].bitcast(F32), ALU.subtract), "oa_lo")

            bias = ROWS["ada_b"][0]
            dve.wait_ge(S("mod_mm"), modulation_sums(24))
            do(X.tensor_tensor(ada[:, 0:48:2], bank[7][:, 0:48:2], V[:, bias:bias + 24], ALU.add))
            do(X.tensor_tensor(ada[:, 1:32:2], bank[7][:, 1:32:2], V[:, bias:bias + 16], ALU.add), "ada0")
            do.settle()

            def coefficients(i, l, s):
                g0 = ROWS["norm_g"][0] + 8 * l
                do(X.scalar_tensor_tensor(acoef[:, 8 * i:8 * i + 8], view(ada, [[2, 8]], (24 * l + 8) * 2 + s), 1.0, V[:, g0:g0 + 8],
                                          ALU.add, ALU.mult))
            coefficients(0, 0, 0)
            coefficients(1, 0, 1)

            do(X.memset(fraw[:, :, 0:2], 0.0), "fraw_zero")
            for n in range(KT):
                residual(T_OUT + n, n)
            norm(1, 1, T, xT, lambda k: vcol("norm2", k), None, hh, hl)
            p = 0
            for r, (t0, t1_) in enumerate(ffn_tiles):
                for j in range(len(ROUND[r])):
                    for half in range(2):
                        t = t0 + 2 * j + half
                        jj = ROUND[r][j] + half * FT
                        dve.wait_ge(S(evac_name(t)), t // NLIN + 1)
                        i = 2 * (p % 2) + half
                        a, w = facc[:, i, :], fraw[:, i, :]
                        do(X.tensor_scalar(a, w[:, 0:T], vcol("ffn_conv", jj), None, ALU.mult))
                        for k in range(1, 3):
                            do.settle()
                            do(X.scalar_tensor_tensor(a, w[:, k:k + T], vcol("ffn_conv", 2 * FT * k + jj), a, ALU.mult, ALU.add),
                               "fconv" if k == 2 else None)
                    dve.wait_ge(S("fsilu"), p + 1)
                    do.settle()
                    do(X.tensor_tensor(a, a, fg[:, p % 2, :], ALU.mult), "fprod")
                    dve.wait_ge(S("fhi"), p + 1)
                    do(X.tensor_tensor(gl[:, j, :], a, gh[:, j, :].bitcast(F32), ALU.subtract), "flo")
                    p += 1
                for n in range(KT):
                    residual(t1_ + n, n)
                    if r == 1 and n == 0:
                        dve.wait_ge(S("rs_ready"), 3)
                    if r == 1:
                        do.settle()
                        scaled(n, CT, craw, coef(1), rs)
                        if n:
                            low(n - 1, 2, CT, shift(0, 1), ch, cl)
                if r == 1:
                    low(KT - 1, 2, CT, shift(0, 1), ch, cl)
            dve.wait_ge(S("rs_ready"), 4)
            do.settle()
            do(X.tensor_tensor(rs2[:], bank[4][:], rs[:], ALU.mult))
            do.settle()
            do(X.tensor_tensor(rs2[:], rs2[:], rs[:], ALU.mult), "x1_square")

            def x1_norm(k):
                do(X.scalar_tensor_tensor(xT[:, k, :], xT[:, k, :], vcol("final1", k), rs[:], ALU.mult, ALU.mult))
            for k in range(4):
                x1_norm(k)
            dve.wait_ge(S("rs_ready"), 5)
            for k in range(KT):
                do.settle()
                scaled(k, T, xT, coef(0), rs2)
                if k < 4:
                    x1_norm(k + 4)
                if k:
                    low(k - 1, 3, T, shift(0, 0), hh, hl)
            low(KT - 1, 3, T, shift(0, 0), hh, hl)
            dve.wait_ge(S("mod_mm"), modulation_sums(48))
            do(X.tensor_tensor(ada[:, 48:96:2], bank[7][:, 48:96:2], V[:, bias + 24:bias + 48], ALU.add), "ada1")
            do.settle()
            coefficients(2, 1, 0)

            do.settle()
            do(X.memset(qcx[:, 0, CT - 1:CT], 1.0))
            do(X.memset(qcx[:, 1, 0:1], 1.0))
            dve.wait_ge(S("hmask_in"), 16)

            def col(vec, dr, g):
                return vec[:, 16 * dr + g:16 * dr + g + 1]

            def context(g):
                dve.wait_ge(S("cevac"), 3 * g + 2)
                for dr in range(2):
                    do(X.tensor_scalar(sgc[:, dr, :], sgc[:, dr, :], col(oml, dr, g), col(lb, dr, g), ALU.mult, ALU.add))
                do.settle()
                if g:
                    dve.wait_ge(S("b6"), 4 * g - 2)
                do(X.tensor_scalar(kcx[:], sgc[:], -1.0, 1.0, ALU.mult, ALU.add))
                f0, f1, q0, q1 = sgc[:, 0, :], sgc[:, 1, :], qcx[:, 0, :], qcx[:, 1, :]
                r0 = view(f0[:, 0:1], [[-1, CT - 1]], CT - 1)
                do(X.tensor_tensor_scan(view(q0[:, 0:1], [[-1, CT - 1]], CT - 2), r0, r0, 1.0, ALU.mult, ALU.bypass))
                do(X.tensor_tensor_scan(q1[:, 1:CT], f1[:, 0:CT - 1], f1[:, 0:CT - 1], 1.0, ALU.mult, ALU.bypass))
                do.settle()
                do(X.tensor_tensor(kcx[:], kcx[:], qcx[:], ALU.mult), "kq_rdy")

            def start(g):
                dve.wait_ge(S(evac_name(T_HG + 5 * g + 2)), (T_HG + 5 * g + 2) // NLIN + 1)
                for dr in range(2):
                    do(X.tensor_scalar(PP[:, dr, :], sgf[:, dr, :], col(oml, dr, g), col(lb, dr, g), ALU.mult, ALU.add),
                       "sgf_used" if dr else None)
                if g:
                    dve.wait_ge(S("o_mm"), g)
                do(X.memset(QQ[:], 1.0))
                do.settle()
                do(X.tensor_scalar(KK[:], PP[:], -1.0, 1.0, ALU.mult, ALU.add))
                do.settle()

            def produce(g, pi, between=None):
                used = 11 * g + pi - 1 if pi >= 2 else (11 * g + (-1 if pi == 0 else 0) if g else 0)
                if used > 0:
                    dve.wait_ge(S("lv_mm"), used)
                kc, qc = KC[:, pi % 2, :], QC[:, pi % 2, :]
                q = qs[:, g % 2, :]
                if pi == 0:
                    do.settle()
                    do(X.tensor_tensor(kc, KK[:, 0, :], KK[:, 1, :], ALU.add))
                    do(X.tensor_copy(qc, q), "lv_rdy")
                    return
                n = LEVELS[pi - 1]
                nb = T // (2 * n)
                sel = [[2 * n, nb], [T + n, 2], [1, n]]
                flat = [[2 * n, nb], [n, 2], [1, n]]
                do.settle(1)
                do(X.tensor_tensor(view(kc[:, 0:1], flat), view(KK[:, 0, 0:1], sel), view(QQ[:, 0, 0:1], sel), ALU.mult))
                do.settle(1)
                do(X.tensor_tensor(view(qc[:, 0:1], flat), view(q[:, 0:1], flat),
                                   view(PP[:, 0, 0:1], [[2 * n, nb], [n - T, 2], [1, n]], T), ALU.mult), "lv_rdy")
                if pi < 9:
                    do.settle(1)
                    do(X.tensor_tensor(view(QQ[:, 0, 0:1], [[T + n, 2], [2 * n, nb], [1, n]]),
                                       view(QQ[:, 0, 0:1], [[T + n, 2], [2 * n, nb], [1, n]]),
                                       view(PP[:, 0, 0:1], [[T - 2 * n + 1, 2], [2 * n, nb], [0, n]], 2 * n - 1), ALU.mult))
                if between:
                    between()
                    do.settle(1)
                else:
                    do.settle()
                do(X.tensor_tensor(view(PP[:, 0, 0:1], [[T - n, 2], [2 * n, nb], [1, n]], n),
                                   view(PP[:, 0, 0:1], [[T - n, 2], [2 * n, nb], [1, n]], n),
                                   view(PP[:, 0, 0:1], [[T + 1, 2], [2 * n, nb], [0, n]], n - 1), ALU.mult))

            def take(g, li):
                dve.wait_ge(S("lv_mm"), 11 * g + li + 1)
                do(X.copy_predicated(view(MT[:, 0, 0:1], [[T + P, 4], [1, P]]), view(hmask[:, li, :], [[0, 4], [1, P]]),
                                     bank[4 + li % 2][:].rearrange("p (a c) -> p a c", c=P)),
                   "lv_ev%d" % (li % 2), (6 if li % 2 == 0 else 5) * g + li // 2 + 1)

            def silu(h, which, t, dst):
                i = t % NLIN
                dve.wait_ge(S("sg_q" if which == 0 else "sg_z"), h + 1)
                evac(t, X.tensor_tensor(dst, bank[i][:], sgt[:, which, :], ALU.mult))

            for h in range(HG + 1):
                t = T_HG + 5 * h
                g = h - 1
                if h:
                    context(g)
                    start(g)
                    produce(g, 0)
                    produce(g, 1)
                if h < HG:
                    silu(h, 0, t, qs[:, h % 2, :])
                    do(X.tensor_copy(small[:, 250:251], small[:, 0:1]), "sgt_q")
                if h:
                    for pi in range(2, 10):
                        produce(g, pi, (lambda li=pi - 2: take(g, li)))
                    do.settle()
                    for dr in range(2):
                        do(X.tensor_tensor(QQ[:, dr, :], qs[:, g % 2, :], PP[:, dr, :], ALU.mult), "qp_rdy" if dr else None)
                if h < HG:
                    silu(h, 1, t + 4, sz[:, h % 2, :])
                    do(X.tensor_copy(small[:, 251:252], small[:, 0:1]), "sz_rdy")
                if h:
                    dve.wait_ge(S("osq"), h)
                    y = yA[:, g, :] if g < 8 else yB[:, g - 8, :]
                    do(X.scalar_tensor_tensor(y, bank[6][:], vcol("hg_norm"), sz[:, g % 2, :], ALU.mult, ALU.mult), "y_pre")
            do.settle()
            for h in range(HG + 1):
                if h < HG:
                    y = yA[:, h, :] if h < 8 else yB[:, h - 8, :]
                    dve.wait_ge(S("rs_row"), h + 1)
                    do(X.tensor_tensor(y, y, bank[4 + h % 2][:], ALU.mult), "y_norm")
                if h:
                    g = h - 1
                    dve.wait_ge(S("y_hi"), h)
                    y = yA[:, g, :] if g < 8 else yB[:, g - 8, :]
                    hi_, lo_ = (hh[:, g, :], hl[:, g, :]) if g < 8 else (gh[:, g - 8, :], gl[:, g - 8, :])
                    do(X.tensor_tensor(lo_, y, hi_.bitcast(F32), ALU.subtract), "y_lo")
            for n in range(KT):
                residual(T_HO + n, n, gate(0))
            norm(5, 4, T, xT, coef(2), shift(1, 0), hh, hl)

            do(X.memset(AB[:, :, GDIM:GDIM + 1], 0.0), "ab_zero")
            do(X.memset(AB[:, :, GDIM + 128:GDIM + 129], 0.0), "ab_zero")
            for gi in range(GROUPS):
                t = ft_tiles[gi // 4] + 4 * (gi % 4)
                def z_silu(c):
                    dve.wait_ge(S("zsg"), 2 * gi + c + 1)
                    evac(t + 2 + c, X.tensor_tensor(zs[:, c, :], bank[(t + 2 + c) % NLIN][:], zsg[:, c, :], ALU.mult))
                    do(X.tensor_copy(small[:, 250 + c:251 + c], small[:, 0:1]), "zs_rdy")
                z_silu(0)
                for i in range(2):
                    dve.wait_ge(S("ab_mm"), gi + 1)
                    dve.wait_ge(S("ab_act"), 2 * gi + i + 1)
                    src, dst = bank[4 + i], AB[:, 2 * i, 0:1]
                    do(X.tensor_scalar(view(dst, [[T, 2], [1, 127]], GDIM + 129), view(src[:, 0:1], [[GDIM, 2], [-1, 127]], 255),
                                       -1.0, None, ALU.mult), "ab_ev")
                z_silu(1)
                for g in range(2):
                    b, q, y = bank[6 + g], qsn[:, g, :], yf[:, g, :]
                    dve.wait_ge(S("qsn"), 2 * gi + g + 1)
                    do(X.tensor_tensor(y[:, 1:256], b[:, 1:256], q[:, 0:255], ALU.subtract))
                    do(X.tensor_tensor(y[:, 257:512], view(b[:, 0:1], [[-1, 255]], 255), view(q[:, 0:1], [[-1, 255]], 254), ALU.add),
                       "yf_rdy")
                    do(X.tensor_copy(y[:, 0:512:256], b[:, 0:512:256]), "y_ev")
                    do.settle()
                    if gi:
                        dve.wait_ge(S("yg_hi"), 2 * (gi - 1) + g + 1)
                    do(X.tensor_tensor(yg[:, g, :], y, zs[:, g, :], ALU.mult), "yg_rdy")
                for g in range(2):
                    k = 2 * (gi % 4) + g
                    dve.wait_ge(S("yg_hi"), 2 * gi + g + 1)
                    do(X.tensor_tensor(gl[:, k, :], yg[:, g, :], gh[:, k, :].bitcast(F32), ALU.subtract), "yg_lo")
                if gi % 4 == 3:
                    for n in range(KT):
                        residual(t + 4 + n, n, gate(1))
            dve.wait_ge(S("rs_ready"), 7)
            for k in range(KT):
                do(X.scalar_tensor_tensor(xT[:, k, :], xT[:, k, :], vcol("final_g", k), rs[:], ALU.mult, ALU.mult), "x_final")


ROWS_LOADED = 0
for _name, (_r, _n) in ROWS.items():
    ROWS_LOADED += 16 * ((_r + _n - 1) // P - _r // P + 1)

INPUTS = ["x", "norm1_w", "w_in", "conv_qkv_w", "a_log", "dt_bias", "gdn_norm_w", "w_out", "norm2_w", "w_up", "ffn_conv_w",
          "w_down", "final_norm_w", "c_2", "ctx_2", "c_ctx_2", "ada_w_2", "ada_b_2", "norm_g_2", "hg_w_in_2",
          "hg_lb_logits_2", "hg_norm_g_2", "hg_w_out_2", "ft_w_in_2", "ft_w_out_2", "final_g_2"]


def kernel(**inputs):
    import concourse.bacc as bacc
    from concourse.bass_utils import run_bass_kernel_spmd

    nc = bacc.Bacc("TRN2", target_bir_lowering=False, num_devices=1)
    arrays, aps = {}, {}
    for name in INPUTS:
        arrays[f"in_{name}"] = np.ascontiguousarray(inputs[name])
    for name, a in host_constants().items():
        arrays[f"const_{name}"] = a
    for name, a in arrays.items():
        aps[name.split("_", 1)[1]] = nc.dram_tensor(name, a.shape, mybir.dt.from_np(a.dtype), kind="ExternalInput").ap()
    out = nc.dram_tensor("out", (1, T, D), F32, kind="ExternalOutput").ap()
    build(nc, aps, out)
    r = run_bass_kernel_spmd(nc, [arrays], core_ids=[0])
    return r.results[0]["out"]
```
